# Optimizing a Trainium2 kernel written in Bass

```python
import math
import jax, jax.numpy as jnp
from jax import lax
import numpy as np

D_MODEL = 1024
BATCH = 1
SEQ = 512
DEPTH = 1

NORM_EPS = 1e-6
N_MOD = 6

RW_HEADS = 8
RW_HEAD_DIM = 64
RW_WIDTH = RW_HEADS * RW_HEAD_DIM
RW_DECAY_LORA = 64
RW_AAA_LORA = 64
RW_GATE_LORA = 128
RW_GN_EPS = 64e-5
RW_COLS = 3 * RW_WIDTH + RW_DECAY_LORA + RW_AAA_LORA + RW_GATE_LORA

NSA_HEADS = 8
NSA_KV_GROUPS = 2
NSA_HPG = NSA_HEADS // NSA_KV_GROUPS
NSA_HEAD_DIM = 64
NSA_WIDTH = NSA_HEADS * NSA_HEAD_DIM
NSA_KV_WIDTH = NSA_KV_GROUPS * NSA_HEAD_DIM
NSA_N_BRANCH = 3
NSA_COLS = NSA_WIDTH + 6 * NSA_KV_WIDTH + NSA_N_BRANCH * NSA_HEADS
CMP_LEN = 32
CMP_STRIDE = 16
CMP_RATIO = CMP_LEN // CMP_STRIDE
CMP_HIDDEN = 256
SEL_BLK = 64
SEL_RATIO = SEL_BLK // CMP_STRIDE
SEL_TOPN = 16
WINDOW = 512
Q_BLK = 128
ROPE_THETA = 10000.0
MASK_NEG = -1e30
SEL_FORCE = 1e9

N_BRANCHES = 2
MERGE_COLS = N_BRANCHES * D_MODEL
IN_COLS = RW_COLS + NSA_COLS + MERGE_COLS

N_EXPERT_GROUPS = 4
EXPERTS_PER_GROUP = 8
N_EXPERTS = N_EXPERT_GROUPS * EXPERTS_PER_GROUP
EXPERT_TOPK = 2
EXPERT_HIDDEN = 512
MOE_BLK = 128

kernel_name = 'hybrid_rwkv7_nsa_hmoe_block'

def rmsnorm(x, g):
    xf = x.astype(jnp.float32)
    y = xf * lax.rsqrt(jnp.mean(xf * xf, axis=-1, keepdims=True) + NORM_EPS)
    return (y * g.astype(jnp.float32)).astype(x.dtype)

def rope(x, pos):
    half = x.shape[-1] // 2
    inv = jnp.exp(-math.log(ROPE_THETA) * jnp.arange(half, dtype=jnp.float32) / half)
    ang = pos.astype(jnp.float32)[:, None] * inv[None, :]
    cos = jnp.cos(ang)[None, :, None, :]
    sin = jnp.sin(ang)[None, :, None, :]
    xf = x.astype(jnp.float32)
    x1, x2 = xf[..., :half], xf[..., half:]
    return jnp.concatenate([x1 * cos - x2 * sin, x2 * cos + x1 * sin], axis=-1).astype(x.dtype)

def masked_softmax(s, mask):
    s = jnp.where(mask, s.astype(jnp.float32), MASK_NEG)
    return jax.nn.softmax(s, axis=-1) * mask

def token_shift(z):
    return jnp.pad(z, ((0, 0), (1, 0), (0, 0)))[:, :-1]

def rwkv7_time_mix(zr, mu, w0, w2, a0, a2, g2, k_k, k_a, r_k, ln_w, ln_b):
    B, T, _ = zr.shape
    f32 = jnp.float32
    zr = zr + (token_shift(zr) - zr) * mu
    r, k, v, wl, al, gl = jnp.split(zr, [RW_WIDTH, 2 * RW_WIDTH, 3 * RW_WIDTH,
                                         3 * RW_WIDTH + RW_DECAY_LORA,
                                         3 * RW_WIDTH + RW_DECAY_LORA + RW_AAA_LORA], axis=-1)
    w_log = -jax.nn.softplus(-(w0 + jnp.tanh(wl) @ w2)) - 0.5
    decay = jnp.exp(-jnp.exp(w_log.astype(f32)))
    a = jax.nn.sigmoid(a0 + al @ a2)
    g = jax.nn.sigmoid(gl) @ g2
    heads = lambda t: t.reshape(B, T, RW_HEADS, RW_HEAD_DIM).astype(f32)
    kk = heads(k * k_k)
    kk = kk / jnp.maximum(jnp.sqrt(jnp.sum(kk * kk, axis=-1, keepdims=True)), 1e-12)
    k = k * (1 + (a - 1) * k_a)
    rh, kh, vh, ah, dh = heads(r), heads(k), heads(v), heads(a), heads(decay)
    xs = tuple(jnp.moveaxis(t, 1, 0) for t in (rh, dh, kh, vh, -kk, kk * ah))

    def step(S, inp):
        r_t, w_t, k_t, v_t, a_t, b_t = inp
        sa = jnp.einsum('bhvk,bhk->bhv', S, a_t)
        S = S * w_t[:, :, None, :] + sa[..., None] * b_t[:, :, None, :] + v_t[..., None] * k_t[:, :, None, :]
        return S, jnp.einsum('bhvk,bhk->bhv', S, r_t)

    S0 = jnp.zeros((B, RW_HEADS, RW_HEAD_DIM, RW_HEAD_DIM), f32)
    _, ys = lax.scan(step, S0, xs)
    y = jnp.moveaxis(ys, 0, 1)
    mean = jnp.mean(y, axis=-1, keepdims=True)
    var = jnp.mean(jnp.square(y - mean), axis=-1, keepdims=True)
    y = ((y - mean) * lax.rsqrt(var + RW_GN_EPS)).reshape(B, T, RW_WIDTH) * ln_w + ln_b
    bonus = jnp.sum(rh * kh * r_k, axis=-1, keepdims=True) * vh
    y = y + bonus.reshape(B, T, RW_WIDTH)
    return (y * g).astype(zr.dtype)

def nsa_mix(zn, pos, pe_k, w1_k, w2_k, pe_v, w1_v, w2_v):
    B, T, _ = zn.shape
    G, HPG, DK = NSA_KV_GROUPS, NSA_HPG, NSA_HEAD_DIM
    q, kc, vc, ks, vs, kw, vw, gl = jnp.split(
        zn, [NSA_WIDTH + i * NSA_KV_WIDTH for i in range(7)], axis=-1)
    kv = lambda t: t.reshape(B, T, G, DK)
    q = rope(q.reshape(B, T, NSA_HEADS, DK), pos)
    kc, vc, vs, vw = kv(kc), kv(vc), kv(vs), kv(vw)
    ks = rope(kv(ks), pos)
    kw = rope(kv(kw), pos)
    gates = jax.nn.sigmoid(gl.astype(jnp.float32)).reshape(B, T, NSA_HEADS, NSA_N_BRANCH)

    n_cmp = (T - CMP_LEN) // CMP_STRIDE + 1
    cmp_idx = jnp.arange(n_cmp)[:, None] * CMP_STRIDE + jnp.arange(CMP_LEN)[None, :]
    cmp_end = jnp.arange(n_cmp) * CMP_STRIDE + CMP_LEN - 1

    def compress(t, pe, w1, w2):
        blocks = t[:, cmp_idx] + pe[None, None, :, None, :]
        hid = jax.nn.gelu(jnp.einsum('bnlgd,ldf->bngf', blocks, w1.reshape(CMP_LEN, DK, CMP_HIDDEN)))
        return jnp.einsum('bngf,fd->bngd', hid, w2)

    kc_c = rope(compress(kc, pe_k, w1_k, w2_k), cmp_end)
    vc_c = compress(vc, pe_v, w1_v, w2_v)

    n_sel = T // SEL_BLK
    top_n = min(SEL_TOPN, n_sel)
    remap_idx = jnp.arange(n_sel)[:, None] * SEL_RATIO + jnp.arange(SEL_RATIO + CMP_RATIO - 1)[None, :]
    remap_w = jnp.asarray(np.convolve(np.ones(SEL_RATIO), np.ones(CMP_RATIO)), jnp.float32)
    right_pad = max(0, n_sel * SEL_RATIO - n_cmp)
    jsel = jnp.arange(n_sel)
    ks_blk = ks.reshape(B, n_sel, SEL_BLK, G, DK).transpose(0, 3, 1, 2, 4)
    vs_blk = vs.reshape(B, n_sel, SEL_BLK, G, DK).transpose(0, 3, 1, 2, 4)
    bi = jnp.arange(B)[:, None, None, None]
    gi = jnp.arange(G)[None, :, None, None]
    kw_pad = jnp.pad(kw, ((0, 0), (WINDOW, 0), (0, 0), (0, 0)))
    vw_pad = jnp.pad(vw, ((0, 0), (WINDOW, 0), (0, 0), (0, 0)))
    scale = NSA_HEAD_DIM ** -0.5

    def block(qb):
        q0 = qb * Q_BLK
        qpos = q0 + jnp.arange(Q_BLK)
        qg = lax.dynamic_slice_in_dim(q, q0, Q_BLK, axis=1).reshape(B, Q_BLK, G, HPG, DK)
        s_c = jnp.einsum('bqghd,bngd->bghqn', qg, kc_c) * scale
        p_c = masked_softmax(s_c, cmp_end[None, :] <= qpos[:, None])
        o_c = jnp.einsum('bghqn,bngd->bqghd', p_c, vc_c)
        p_pad = jnp.pad(p_c.sum(axis=2), ((0, 0), (0, 0), (0, 0), (CMP_RATIO - 1, right_pad)))
        p_slc = jnp.einsum('bgqjs,s->bgqj', p_pad[..., remap_idx], remap_w)
        qblk = qpos // SEL_BLK
        forced = (jsel[None, :] == 0) | (jsel[None, :] == qblk[:, None]) | (jsel[None, :] == qblk[:, None] - 1)
        future = jsel[None, :] > qblk[:, None]
        score = jnp.where(forced, SEL_FORCE, jnp.where(future, -SEL_FORCE, p_slc))
        _, sel = lax.top_k(score, top_n)
        k_sel = ks_blk[bi, gi, sel]
        v_sel = vs_blk[bi, gi, sel]
        s_s = jnp.einsum('bqghd,bgqnld->bghqnl', qg, k_sel) * scale
        tok = sel[..., None] * SEL_BLK + jnp.arange(SEL_BLK)
        mask_s = (tok <= qpos[None, None, :, None, None]).reshape(B, G, 1, Q_BLK, -1)
        p_s = masked_softmax(s_s.reshape(B, G, HPG, Q_BLK, -1), mask_s).reshape(s_s.shape)
        o_s = jnp.einsum('bghqnl,bgqnld->bqghd', p_s, v_sel)
        kwin = lax.dynamic_slice_in_dim(kw_pad, q0, Q_BLK + WINDOW, axis=1)
        vwin = lax.dynamic_slice_in_dim(vw_pad, q0, Q_BLK + WINDOW, axis=1)
        kpos = q0 - WINDOW + jnp.arange(Q_BLK + WINDOW)
        mask_w = (kpos[None, :] <= qpos[:, None]) & (kpos[None, :] > qpos[:, None] - WINDOW) & (kpos[None, :] >= 0)
        s_w = jnp.einsum('bqghd,bkgd->bghqk', qg, kwin) * scale
        p_w = masked_softmax(s_w, mask_w)
        o_w = jnp.einsum('bghqk,bkgd->bqghd', p_w, vwin)
        gb = lax.dynamic_slice_in_dim(gates, q0, Q_BLK, axis=1).reshape(B, Q_BLK, G, HPG, NSA_N_BRANCH)
        o = gb[..., 0:1] * o_c + gb[..., 1:2] * o_s + gb[..., 2:3] * o_w
        return o.reshape(B, Q_BLK, NSA_WIDTH)

    outs = lax.map(block, jnp.arange(T // Q_BLK))
    return outs.transpose(1, 0, 2, 3).reshape(B, T, NSA_WIDTH).astype(zn.dtype)

def hier_moe(u, w_rg, b_rg, w_re, b_re, w_gate, w_up, w_down):
    B, T, D = u.shape
    N = B * T
    f32 = jnp.float32
    xf = u.reshape(N, D)
    grp_p = jax.nn.softmax((xf @ w_rg).astype(f32) + b_rg, axis=-1)
    grp_w, grp = lax.top_k(grp_p, 1)
    exp_logits = ((xf @ w_re).astype(f32) + b_re).reshape(N, N_EXPERT_GROUPS, EXPERTS_PER_GROUP)
    in_grp = jnp.take_along_axis(exp_logits, grp[:, :, None], axis=1)[:, 0]
    top_v, top_i = lax.top_k(in_grp, EXPERT_TOPK)
    comb = grp_w * jax.nn.softmax(top_v, axis=-1)
    expert_id = grp * EXPERTS_PER_GROUP + top_i
    A = N * EXPERT_TOPK
    eid = expert_id.reshape(A)
    tid = jnp.repeat(jnp.arange(N, dtype=jnp.int32), EXPERT_TOPK)
    wts = comb.reshape(A)
    order = jnp.argsort(eid)
    se = eid[order]
    counts = jnp.bincount(eid, length=N_EXPERTS)
    starts = jnp.cumsum(counts) - counts
    pcounts = (counts + MOE_BLK - 1) // MOE_BLK * MOE_BLK
    pends = jnp.cumsum(pcounts)
    pstarts = pends - pcounts
    dest = pstarts[se] + jnp.arange(A) - starts[se]
    P = -(-A // MOE_BLK) * MOE_BLK + N_EXPERTS * MOE_BLK
    n_blk = P // MOE_BLK
    buf_tok = jnp.full((P,), N, jnp.int32).at[dest].set(tid[order])
    buf_w = jnp.zeros((P,), f32).at[dest].set(wts[order])
    blk_exp = jnp.minimum(jnp.searchsorted(pends, jnp.arange(n_blk) * MOE_BLK, side='right'), N_EXPERTS - 1)
    x_pad = jnp.concatenate([xf, jnp.zeros((1, D), xf.dtype)], axis=0)
    xb = x_pad[buf_tok].reshape(n_blk, MOE_BLK, D)

    def expert_block(args):
        xblk, e = args
        hid = jax.nn.silu(xblk @ w_gate[e]) * (xblk @ w_up[e])
        return hid @ w_down[e]

    yb = lax.map(expert_block, (xb, blk_exp)).reshape(P, D)
    y = jax.ops.segment_sum(yb * buf_w[:, None], buf_tok, num_segments=N + 1)[:N]
    return y.reshape(B, T, D).astype(u.dtype)

def setup_inputs(seed: int = 0):
    key = jax.random.key(seed)
    k = jax.random.split(key, 35)
    f32 = jnp.float32
    L, D = DEPTH, D_MODEL
    nrm = lambda i, shape, s: jax.random.normal(k[i], shape, f32) * s
    uni = lambda i, shape, lo, hi: jax.random.uniform(k[i], shape, f32, lo, hi)
    return {
        'x': nrm(0, (BATCH, SEQ, D), 1.0),
        'c': nrm(1, (BATCH, D), 1.0),
        'w_ada': nrm(2, (L, D, N_MOD * D), D ** -0.5),
        'b_ada': nrm(3, (L, N_MOD * D), 0.01),
        'norm_mix_g': 1.0 + nrm(4, (L, D), 0.02),
        'w_in': nrm(5, (L, D, IN_COLS), D ** -0.5),
        'rwkv_mu': uni(6, (L, RW_COLS), 0.0, 1.0),
        'rwkv_w0': uni(7, (L, RW_WIDTH), -5.0, -1.0),
        'rwkv_w2': nrm(8, (L, RW_DECAY_LORA, RW_WIDTH), 0.1 * RW_DECAY_LORA ** -0.5),
        'rwkv_a0': nrm(9, (L, RW_WIDTH), 0.5),
        'rwkv_a2': nrm(10, (L, RW_AAA_LORA, RW_WIDTH), 0.5 * RW_AAA_LORA ** -0.5),
        'rwkv_g2': nrm(11, (L, RW_GATE_LORA, RW_WIDTH), RW_GATE_LORA ** -0.5),
        'rwkv_kk': 0.85 + nrm(12, (L, RW_WIDTH), 0.05),
        'rwkv_ka': 1.0 + nrm(13, (L, RW_WIDTH), 0.05),
        'rwkv_rk': nrm(14, (L, RW_HEADS, RW_HEAD_DIM), 0.1),
        'rwkv_ln_w': 1.0 + nrm(15, (L, RW_WIDTH), 0.02),
        'rwkv_ln_b': nrm(16, (L, RW_WIDTH), 0.01),
        'cmp_pe_k': nrm(17, (L, CMP_LEN, NSA_HEAD_DIM), 0.1),
        'cmp_w1_k': nrm(18, (L, CMP_LEN * NSA_HEAD_DIM, CMP_HIDDEN), (CMP_LEN * NSA_HEAD_DIM) ** -0.5),
        'cmp_w2_k': nrm(19, (L, CMP_HIDDEN, NSA_HEAD_DIM), CMP_HIDDEN ** -0.5),
        'cmp_pe_v': nrm(20, (L, CMP_LEN, NSA_HEAD_DIM), 0.1),
        'cmp_w1_v': nrm(21, (L, CMP_LEN * NSA_HEAD_DIM, CMP_HIDDEN), (CMP_LEN * NSA_HEAD_DIM) ** -0.5),
        'cmp_w2_v': nrm(22, (L, CMP_HIDDEN, NSA_HEAD_DIM), CMP_HIDDEN ** -0.5),
        'p_rwkv': nrm(23, (L, RW_WIDTH, D), RW_WIDTH ** -0.5),
        'p_nsa': nrm(24, (L, NSA_WIDTH, D), NSA_WIDTH ** -0.5),
        'w_out': nrm(25, (L, D, D), D ** -0.5),
        'norm_ffn_g': 1.0 + nrm(26, (L, D), 0.02),
        'w_router_grp': nrm(27, (L, D, N_EXPERT_GROUPS), D ** -0.5),
        'b_router_grp': nrm(28, (L, N_EXPERT_GROUPS), 0.01),
        'w_router_exp': nrm(29, (L, D, N_EXPERTS), D ** -0.5),
        'b_router_exp': nrm(30, (L, N_EXPERTS), 0.01),
        'moe_w_gate': nrm(31, (L, N_EXPERTS, D, EXPERT_HIDDEN), D ** -0.5),
        'moe_w_up': nrm(32, (L, N_EXPERTS, D, EXPERT_HIDDEN), D ** -0.5),
        'moe_w_down': nrm(33, (L, N_EXPERTS, EXPERT_HIDDEN, D), EXPERT_HIDDEN ** -0.5),
        'norm_final_g': 1.0 + nrm(34, (D,), 0.02),
    }

def reference(x, c, w_ada, b_ada, norm_mix_g, w_in, rwkv_mu, rwkv_w0, rwkv_w2, rwkv_a0, rwkv_a2,
              rwkv_g2, rwkv_kk, rwkv_ka, rwkv_rk, rwkv_ln_w, rwkv_ln_b, cmp_pe_k, cmp_w1_k, cmp_w2_k,
              cmp_pe_v, cmp_w1_v, cmp_w2_v, p_rwkv, p_nsa, w_out, norm_ffn_g, w_router_grp,
              b_router_grp, w_router_exp, b_router_exp, moe_w_gate, moe_w_up, moe_w_down, norm_final_g):
    B, T, D = x.shape
    pos = jnp.arange(T)
    cs = jax.nn.silu(c)
    h = x
    for l in range(DEPTH):
        mod = cs @ w_ada[l] + b_ada[l]
        sh1, sc1, gt1, sh2, sc2, gt2 = jnp.split(mod[:, None, :], N_MOD, axis=-1)
        u = rmsnorm(h, norm_mix_g[l]) * (1 + sc1) + sh1
        z = u @ w_in[l]
        zr, zn, zg = jnp.split(z, [RW_COLS, RW_COLS + NSA_COLS], axis=-1)
        y_r = rwkv7_time_mix(zr, rwkv_mu[l], rwkv_w0[l], rwkv_w2[l], rwkv_a0[l], rwkv_a2[l], rwkv_g2[l],
                             rwkv_kk[l], rwkv_ka[l], rwkv_rk[l], rwkv_ln_w[l], rwkv_ln_b[l])
        y_n = nsa_mix(zn, pos, cmp_pe_k[l], cmp_w1_k[l], cmp_w2_k[l], cmp_pe_v[l], cmp_w1_v[l], cmp_w2_v[l])
        gates = jax.nn.sigmoid(zg).reshape(B, T, N_BRANCHES, D)
        merged = gates[:, :, 0] * (y_r @ p_rwkv[l]) + gates[:, :, 1] * (y_n @ p_nsa[l])
        h = h + gt1 * (merged @ w_out[l])
        u2 = rmsnorm(h, norm_ffn_g[l]) * (1 + sc2) + sh2
        h = h + gt2 * hier_moe(u2, w_router_grp[l], b_router_grp[l], w_router_exp[l], b_router_exp[l],
                               moe_w_gate[l], moe_w_up[l], moe_w_down[l])
    return rmsnorm(h, norm_final_g)


_drawn_inputs = setup_inputs


def setup_inputs(seed=0):
    import zlib

    import numpy as np

    out = dict(_drawn_inputs(seed))
    spreads = {}
    factors = {'norm_mix_g': 3.263,
     'rwkv_w2': 13.745,
     'rwkv_ln_w': 36.04,
     'rwkv_ln_b': 40.976,
     'cmp_pe_k': 8.0,
     'cmp_pe_v': 13.3,
     'b_router_grp': 64.0,
     'b_router_exp': 35.528,
     'norm_final_g': 7.924,
     'rwkv_kk': 3.722,
     'norm_ffn_g': 5.262}
    for name, (base, spread) in spreads.items():
        noise = np.random.default_rng([zlib.crc32(name.encode()), seed]).standard_normal(out[name].shape)
        drawn = base * np.exp(spread * noise) if base else spread * noise
        out[name] = __import__('jax').numpy.asarray(drawn.astype(out[name].dtype))
    for name, factor in factors.items():
        out[name] = (out[name] * factor).astype(out[name].dtype)
    return out
```

```python
from contextlib import ExitStack

import numpy as np

import concourse.bass as bass
from concourse import mybir

P = 128
D = 1024
T = 512
NT = T // P
KD = D // P
RW = 512
HEADS = 8
HD = 64
CT = RW // P
RW_COLS = 3 * RW + 64 + 64 + 128
ZT_TILES = RW_COLS // P
NSA0 = RW_COLS
GATE0 = NSA0 + 512 + 6 * 128 + 24
IN_COLS = GATE0 + 2 * D
NCMP = 31
E = 32
EG = 8
NG = 4
EH = 512
OVER = 7
NBLK = E + OVER
R = 6
SLOT = 4096
NEG = -1e30

F32 = mybir.dt.float32
BF16 = mybir.dt.bfloat16
I32 = mybir.dt.int32
U32 = mybir.dt.uint32
ALU = mybir.AluOpType
ACT = mybir.ActivationFunctionType
AX = mybir.AxisListType.X


def constants():
    f = np.float32
    i = np.arange(P)
    parts = {}
    parts["ident"] = np.eye(P)
    strict = (i[:, None] < i[None, :])
    parts["strict"] = strict
    parts["incl"] = (i[:, None] <= i[None, :])
    for n in range(7):
        m = 1 << n
        same = (i[:, None] // (2 * m)) == (i[None, :] // (2 * m))
        parts[f"lvl{n}"] = same & (i[:, None] % (2 * m) < m) & (i[None, :] % (2 * m) >= m)
    parts["headsum"] = (i[:, None] // HD == i[None, :] // HD)
    parts["headsel"] = (i[:, None] // HD == np.arange(2)[None, :])
    parts["causal"] = np.where(i[None, :] <= i[:, None], 0.0, NEG)
    parts["ones"] = np.ones((P, P))
    half = HD // 2
    inv = np.exp(f(-np.log(10000.0)) * np.arange(half, dtype=f) / f(half)).astype(f)
    ang = (np.arange(T, dtype=f)[:, None] * inv[None, :]).astype(f)
    cos, sin = np.cos(ang).astype(f), np.sin(ang).astype(f)
    tile = lambda a: a.reshape(NT, P, -1).transpose(1, 0, 2).reshape(P, -1)
    parts["cos"], parts["sin"] = tile(cos), tile(sin)
    end = np.arange(NCMP) * 16 + 31
    cc, cs = np.zeros((P, half), f), np.zeros((P, half), f)
    cc[:NCMP], cs[:NCMP] = cos[end], sin[end]
    parts["ccos"], parts["csin"] = cc, cs
    seen = end[None, :] <= np.arange(T)[:, None]
    parts["cmask"] = tile(np.where(seen, 0.0, NEG))
    parts["cseen"] = tile(seen.astype(f))
    parts["expert"] = np.broadcast_to(np.arange(E), (P, E))
    parts["expert_down"] = np.broadcast_to(E - np.arange(E), (P, E))
    parts["group_down"] = np.broadcast_to(NG - np.arange(NG), (P, NG))
    parts["group_down_of"] = np.broadcast_to(NG - np.arange(E) // EG, (P, E))
    parts["token"] = i[:, None] + P * np.arange(NT)[None, :]
    late = lambda k: k.startswith("lvl") or k in ("headsum", "headsel")
    at, cols, n, common = {}, [], 0, 0
    for k in sorted(parts, key=late):
        at[k] = (n, n + parts[k].shape[1])
        n += parts[k].shape[1]
        common = common if late(k) else n
        cols.append(parts[k].astype(f))
    return np.concatenate(cols, 1), at, common


def stream_units(A):
    ada = A["w_ada"][0].rearrange("(p k) n -> p k n", k=KD)
    win = A["w_in"][0].rearrange("(p k) n -> p k n", k=KD)
    units = []

    def ada_unit(u):
        units.append((f"ada{u}", [(0, P, (KD, 512), ada[:, :, 512 * u:512 * u + 512])]))

    def win_unit(name, c0, n):
        units.append((name, [(0, P, (KD, n), win[:, :, c0:c0 + n])]))

    for u in range(4):
        ada_unit(u)
    win_unit("zr0", 0, 512)
    win_unit("zr1", 512, 512)
    ada_unit(4)
    win_unit("zr2", 1024, 512)
    ada_unit(5)
    win_unit("zr3", 1536, 256)
    ada_unit(6)
    win_unit("q", NSA0, 512)
    ada_unit(7)
    win_unit("kcvc", NSA0 + 512, 256)
    ada_unit(8)
    win_unit("kv", NSA0 + 768, 512)
    for u in (9, 10, 11):
        ada_unit(u)
    for name in ("k", "v"):
        units.append((f"w1{name}", [(0, P, (16, 256), A[f"cmp_w1_{name}"][0].rearrange("(l q) f -> q l f", q=P))]))
    for name in ("p_rwkv", "p_nsa"):
        units.append((name, [(0, P, (4, D), A[name][0].rearrange("(p j) n -> p j n", j=4))]))
    for j in range(2):
        for b in range(2):
            win_unit(f"zg{b}{j}", GATE0 + D * b + 512 * j, 512)
    wo = A["w_out"][0].rearrange("(p k) n -> p k n", k=KD)
    for h in range(2):
        units.append((f"wo{h}", [(0, P, (4, D), wo[:, 4 * h:4 * h + 4, :])]))
    return units


def build(nc, A, out):
    consts_np, at, NC = constants()
    units = stream_units(A)
    index = {name: n for n, (name, _) in enumerate(units)}
    NU = len(units)
    total, arrived = [0] * R, []
    for n, (_, parts) in enumerate(units):
        total[n % R] += 16 * len(parts)
        arrived.append(total[n % R])

    with ExitStack() as top:
        stage_sems = []

        def sem(name):
            stage_sems.append(nc.alloc_semaphore(name))
            return stage_sems[-1]

        def end_stage():
            nc.clear_and_free_semaphores(stage_sems)
            nc.all_engine_barrier()
            stage_sems.clear()

        def alloc(ctx, name, shape, dt=F32):
            return ctx.enter_context(nc.sbuf_tensor(name, shape, dt))

        def sb(name, shape, dt=F32):
            return alloc(top, name, shape, dt)

        ring = sb("ring", [P, R, SLOT])
        cst = sb("cst", [P, NC])
        ones_bf = sb("ones_bf", [P, P], BF16)
        strict_bf = sb("strict_bf", [P, P], BF16)
        mod = sb("mod", [P, 6, D])
        ps = top.enter_context(nc.psum_tensor("ps", [P, 8, 512], F32))
        uT_dram = nc.dram_tensor("uT_dram", [P, KD, T], F32).ap()
        yn_dram = nc.dram_tensor("yn_dram", [P, NT, RW], F32).ap()
        u2_dram = nc.dram_tensor("u2_dram", [T, D], F32).ap()
        slots_dram = nc.dram_tensor("slots_dram", [P * NBLK, 1], I32).ap()
        y_dram = nc.dram_tensor("y_dram", [NBLK * P, D], F32).ap()

        def C(name):
            a, b = at[name]
            return cst[:, a:b]

        unit_in = [nc.alloc_semaphore(f"unit_in{s}") for s in range(R)]
        unit_free = [nc.alloc_semaphore(f"unit_free{s}") for s in range(R)]
        s_const = sem("s_const")
        s_spill = sem("s_spill")

        def slot(name, k, n):
            return ring[:, index[name] % R, 0:k * n].rearrange("p (k n) -> p k n", k=k)

        def need(eng, name):
            n = index[name]
            eng.wait_ge(unit_in[n % R], arrived[n])

        def give_back(ins, name):
            ins.then_inc(unit_free[index[name] % R], 1)

        def load_units(eng, first, last):
            for n in range(first, last):
                if n >= R:
                    eng.wait_ge(unit_free[n % R], n // R)
                for p0, np_, (k, w), src in units[n][1]:
                    eng.dma_start(ring[p0:p0 + np_, n % R, 0:k * w].rearrange("p (k n) -> p k n", k=k), src)\
                       .then_inc(unit_in[n % R], 16)

        def warm(pe, n=8):
            for _ in range(n):
                pe.matmul(ps[:, 7, :], C("ident"), cst[:, 0:T], start=True, stop=True)

        class Chain:

            def __init__(self, eng, s):
                self.eng, self.s, self.n = eng, s, 0

            def __call__(self, ins):
                self.n += 1
                ins.then_inc(self.s, 1)
                self.eng.wait_ge(self.s, self.n)

        def norm_mod(ctx, tag, src, u, uT, g_row, shift, scale, keep_rows):
            s_sq, s_sc, s_rt, s_u, s_uT, s_ev, s_row = (sem(f"{tag}_{x}") for x in
                                                      ("sq", "sc", "rt", "u", "uT", "ev", "row"))
            gs = g_row
            junk = ps[:, 6:8, :].rearrange("p b n -> p (b n)")
            ss = alloc(ctx, f"{tag}_ss", [P, NT])
            ms = alloc(ctx, f"{tag}_ms", [P, NT])
            rt = alloc(ctx, f"{tag}_rt", [P, NT])
            rs = alloc(ctx, f"{tag}_rs", [P, NT])

            def scalar(eng):
                for i in range(NT):
                    ins = eng.activation(junk, src[:, i, :], ACT.Square, accum_out=ss[:, i:i + 1])
                    ins.then_inc(s_sq, 1)
                    eng.wait_ge(s_sq, i + 1)
                eng.wait_ge(s_sc, 1)
                eng.activation(rt[:, :], ms[:, :], ACT.Sqrt).then_inc(s_rt, 1)

            def scalar_evacuate(eng):
                for i in range(NT):
                    for b in range(2):
                        eng.wait_ge(s_uT, 2 * i + b + 1)
                        eng.activation(uT[:, 4 * b:4 * b + 4, P * i:P * i + P],
                                       ps[:, (2 * i + b) % 4, :].rearrange("p (k t) -> p k t", k=4),
                                       ACT.Copy).then_inc(s_ev, 1)

            def vector_mean(eng):
                eng.wait_ge(s_sq, NT)
                eng.tensor_scalar(ms[:, :], ss[:, :], 1.0 / D, 1e-6, ALU.mult, ALU.add).then_inc(s_sc, 1)

            def vector(eng, link):
                link(eng.scalar_tensor_tensor(gs[:, :], mod[:, scale, :], 1.0, gs[:, :], ALU.add, ALU.mult))
                eng.wait_ge(s_rt, 1)
                link(eng.reciprocal(rs[:, :], rt[:, :]))
                for i in range(NT):
                    if i >= 2:
                        eng.wait_ge(s_uT, 2 * (i - 1))
                        if keep_rows:
                            eng.wait_ge(s_row, 16 * (i - 1))
                    link(eng.scalar_tensor_tensor(u[:, i % 2, :], src[:, i, :], rs[:, i:i + 1], gs[:, :],
                                                  ALU.mult, ALU.mult))
                    eng.tensor_tensor(u[:, i % 2, :], u[:, i % 2, :], mod[:, shift, :], ALU.add).then_inc(s_u, 1)

            def tensor(eng):
                for i in range(NT):
                    eng.wait_ge(s_u, i + 1)
                    uv = u[:, i % 2, :].rearrange("t (p k) -> t k p", k=KD)
                    for b in range(2):
                        n = 2 * i + b
                        if n >= 4:
                            eng.wait_ge(s_ev, n - 3)
                        for k in range(4):
                            ins = eng.transpose(ps[:, n % 4, P * k:P * k + P], uv[:, 4 * b + k, :], C("ident"))
                        ins.then_inc(s_uT, 1)

            def store(eng):
                for i in range(NT):
                    eng.wait_ge(s_u, i + 1)
                    eng.dma_start(u2_dram[P * i:P * i + P, :], u[:, i % 2, :]).then_inc(s_row, 16)
                    eng.wait_ge(s_row, 16 * (i + 1))

            return scalar, scalar_evacuate, vector_mean, vector, tensor, store, s_ev

        mixers = top.enter_context(ExitStack())
        attn = top.enter_context(ExitStack())
        zrT = alloc(mixers, "zrT", [P, ZT_TILES, T])
        par = alloc(mixers, "par", [P, 34])
        x = zrT[:, 0:8, :].rearrange("p (i a) n -> p i (a n)", a=2)
        kcvc = alloc(attn, "kcvc", [P, 2, T])
        q = alloc(attn, "q", [P, NT, 512])
        kv = alloc(attn, "kv", [P, NT, 512])
        glog = alloc(attn, "glog", [P, NT, 24])
        stage1 = top.enter_context(ExitStack())
        crow = alloc(stage1, "crow", [P, KD])
        csil = alloc(stage1, "csil", [P, KD])
        csig = alloc(stage1, "csig", [P, KD])
        bada = alloc(stage1, "bada", [12, 512])
        uT = alloc(stage1, "uT", [P, KD, T])
        acc = alloc(stage1, "acc", [P, 2, 512])
        parr = alloc(stage1, "parr", [34, P])
        wgl = alloc(stage1, "wgl", [P, KD, 24])
        misc = alloc(stage1, "misc", [P, 3 * T + 2])
        grow = misc[:, 0:D]
        u1 = zrT[:, 8:12, :].rearrange("p (b a) n -> p b (a n)", b=2)
        zb = misc[:, 0:2 * T + 2].rearrange("p (b t) -> p b t", b=2)
        zd = misc[:, 2 * T + 2:3 * T + 2]
        s_c, s_h, s_small = sem("s_c"), sem("s_h"), sem("s_small")
        s_csig, s_dve, s_bf, s_par, s_parT = sem("s_csig"), sem("s_dve"), sem("s_bf"), sem("s_par"), sem("s_parT")
        s_acc, s_modp, s_mod, s_zp, s_ze, s_zbz, s_shift = (sem(x) for x in
            ("s_acc", "s_modp", "s_mod", "s_zp", "s_ze", "s_zbz", "s_shift"))
        n_act, n_evac, n_mean, n_dve, n_pe, _, n1_ev = norm_mod(stage1, "n1", x, u1, uT, grow, 0, 1, False)

        ztiles = [("T", f"zr{t // 4}", t, P * (t % 4)) for t in range(ZT_TILES)]
        ztiles += [("q", "q", i, 0) for i in range(NT)]
        ztiles += [("T", "kcvc", ZT_TILES + t, P * t) for t in range(2)]
        ztiles += [("kv", "kv", i, 0) for i in range(NT)]
        ztiles += [("gl", None, i, 0) for i in range(NT)]
        last_of = {u: n for n, (_, u, _, _) in enumerate(ztiles) if u}
        stage1_units = index["ada11"] + 1

        with nc.Block() as block:
            @block.sync
            def _(sp):
                sp.dma_start(crow[:, :], A["c"][0].rearrange("(p k) -> p k", k=KD)).then_inc(s_c, 16)
                sp.dma_start(bada[:, :], A["b_ada"].rearrange("a (u n) -> (a u) n", n=512)).then_inc(s_c, 16)
                sp.dma_start(cst[:, :], A["consts"][:, 0:NC]).then_inc(s_const, 16)
                load_units(sp, 0, 2)
                sp.dma_start(x, A["x"][0].rearrange("(i p) d -> p i d", p=P)).then_inc(s_h, 16)
                load_units(sp, 2, 10)
                sp.wait_ge(n1_ev, 2 * NT)
                sp.dma_start(uT_dram, uT[:, :, :]).then_inc(s_spill, 16)
                load_units(sp, 10, stage1_units)
                sp.wait_ge(s_spill, 16)

            @block.gpsimd
            def _(pool):
                pool.dma_start(grow[:, :], A["norm_mix_g"][0].partition_broadcast(P)).then_inc(s_small, 16)
                pool.dma_start(wgl[:, :, :], A["w_in"][0].rearrange("(p k) n -> p k n", k=KD)
                               [:, :, NSA0 + 1280:NSA0 + 1304]).then_inc(s_small, 16)
                row = 0
                for name in ("rwkv_mu", "rwkv_w0", "rwkv_a0", "rwkv_kk", "rwkv_ka"):
                    v = A[name].rearrange("a (t p) -> (a t) p", p=P)
                    pool.dma_start(parr[row:row + v.shape[0], :], v).then_inc(s_par, 16)
                    row += v.shape[0]
                pool.dma_start(parr[row:row + CT, :], A["rwkv_rk"][0].rearrange("(t h) d -> t (h d)", h=2))\
                    .then_inc(s_par, 16)
                pool.wait_ge(n1_ev, 2 * NT)
                pool.memset(zb[:, :, 0:1], 0.0).then_inc(s_zbz, 1)
                pool.wait_ge(s_small, 32)
                pool.wait_ge(s_par, 96)

            @block.scalar
            def _(act):
                act.wait_ge(s_c, 32)
                act.activation(csig[:, :], crow[:, :], ACT.Sigmoid).then_inc(s_csig, 1)
                act.wait_ge(s_h, 16)
                n_act(act)
                act.wait_ge(s_const, 16)
                for u in range(4):
                    act.wait_ge(s_modp, u + 1)
                    act.activation(mod[:, u // 2, 512 * (u % 2):512 * (u % 2) + 512], ps[:, 4 + u % 2, :],
                                   ACT.Copy).then_inc(s_mod, 1)
                act.wait_ge(s_parT, 1)
                act.activation(par[:, :], ps[:, 6, 0:34], ACT.Copy).then_inc(s_mod, 1)
                n_evac(act)
                nshift = 0
                for n, (kind, _, i, _) in enumerate(ztiles):
                    act.wait_ge(s_zp, n + 1)
                    src = ps[:, n % 4, :]
                    if kind == "T" and i < ZT_TILES:
                        if nshift >= 2:
                            act.wait_ge(s_shift, nshift - 1)
                        if nshift == 0:
                            act.wait_ge(s_zbz, 1)
                        dst = zb[:, nshift % 2, 1:T + 1]
                        nshift += 1
                    elif kind == "T":
                        dst = kcvc[:, i - ZT_TILES, :]
                    elif kind == "gl":
                        dst, src = glog[:, i, :], ps[:, n % 4, 0:24]
                    else:
                        dst = (q if kind == "q" else kv)[:, i, :]
                    act.activation(dst, src, ACT.Copy).then_inc(s_ze, 1)

            @block.vector
            def _(dve):
                link = Chain(dve, s_dve)
                dve.wait_ge(s_csig, 1)
                link(dve.tensor_tensor(csil[:, :], crow[:, :], csig[:, :], ALU.mult))

                def ada(u):
                    need(dve, f"ada{u}")
                    w = slot(f"ada{u}", KD, 512)
                    a = acc[:, u % 2, :]
                    if u >= 2:
                        dve.wait_ge(s_modp, u - 1)
                    link(dve.tensor_scalar(a, w[:, 0, :], csil[:, 0:1], None, ALU.mult))
                    for k in range(1, KD):
                        link(dve.scalar_tensor_tensor(a, w[:, k, :], csil[:, k:k + 1], a, ALU.mult, ALU.add))
                    dve.sem_inc(unit_free[index[f"ada{u}"] % R], 1)
                    dve.sem_inc(s_acc, 1)

                for u in range(4):
                    ada(u)
                dve.wait_ge(s_const, 16)
                dve.tensor_copy(ones_bf[:, :], C("ones")).then_inc(s_bf, 1)
                dve.tensor_copy(strict_bf[:, :], C("strict")).then_inc(s_bf, 1)
                dve.wait_ge(s_small, 32)
                n_mean(dve)
                dve.wait_ge(s_mod, 5)
                n_dve(dve, link)
                nshift, u = 0, 4
                for n, (kind, name, i, _) in enumerate(ztiles):
                    if kind == "T" and i < ZT_TILES:
                        dve.wait_ge(s_ze, n + 1)
                        z = zb[:, nshift % 2, :]
                        link(dve.tensor_tensor(zd, z[:, 0:T], z[:, 1:T + 1], ALU.subtract))
                        dve.scalar_tensor_tensor(zrT[:, i, :], zd, par[:, i:i + 1], z[:, 1:T + 1],
                                                 ALU.mult, ALU.add).then_inc(s_shift, 1)
                        nshift += 1
                        dve.wait_ge(s_shift, nshift)
                    while u < 12 and index[f"ada{u}"] < (index[name] if name else NU) + R - 2:
                        ada(u)
                        dve.wait_ge(s_modp, u + 1)
                        dve.tensor_copy(mod[:, u // 2, 512 * (u % 2):512 * (u % 2) + 512],
                                        ps[:, 4 + u % 2, :]).then_inc(s_mod, 1)
                        u += 1

            @block.tensor
            def _(pe):
                pe.wait_ge(s_const, 16)
                pe.wait_ge(s_c, 32)

                def spread(u):
                    pe.wait_ge(s_acc, u + 1)
                    if 2 <= u < 4:
                        pe.wait_ge(s_mod, u - 1)
                    elif u == 4:
                        pe.wait_ge(s_mod, 5)
                    elif u > 4:
                        pe.wait_ge(s_mod, u)
                    pe.matmul(ps[:, 4 + u % 2, :], C("ones"), acc[:, u % 2, :], start=True, stop=False)
                    pe.matmul(ps[:, 4 + u % 2, :], C("ident")[0:12, u:u + 1].to_broadcast([12, P]), bada[:, :],
                              start=False, stop=True).then_inc(s_modp, 1)

                for u in range(4):
                    spread(u)
                pe.wait_ge(s_par, 96)
                pe.transpose(ps[:, 6, 0:34], parr[:, :], C("ident")[0:34, 0:34]).then_inc(s_parT, 1)
                n_pe(pe)
                pe.wait_ge(n1_ev, 2 * NT)
                pe.wait_ge(s_small, 32)
                u = 4
                for n, (kind, name, i, c0) in enumerate(ztiles):
                    if name:
                        need(pe, name)
                    if n >= 4:
                        pe.wait_ge(s_ze, n - 3)
                    for k in range(KD):
                        if kind == "T":
                            w = 256 if name in ("zr3", "kcvc") else 512
                            ins = pe.matmul(ps[:, n % 4, :], slot(name, KD, w)[:, k, c0:c0 + P], uT[:, k, :],
                                            start=(k == 0), stop=(k == KD - 1))
                        elif kind == "gl":
                            ins = pe.matmul(ps[:, n % 4, 0:24], uT[:, k, P * i:P * i + P], wgl[:, k, :],
                                            start=(k == 0), stop=(k == KD - 1))
                        else:
                            w = slot(name, KD, 512)[:, k, :]
                            if kind == "q":
                                w = w.rearrange("p (g j d) -> p j g d", g=2, j=4)
                            ins = pe.matmul(ps[:, n % 4, :], uT[:, k, P * i:P * i + P], w, start=(k == 0), stop=(k == KD - 1))
                    ins.then_inc(s_zp, 1)
                    if name and last_of[name] == n:
                        pe.wait_ge(s_zp, n + 1)
                        pe.sem_inc(unit_free[index[name] % R], 1)
                    while u < 12 and index[f"ada{u}"] < (index[name] if name else NU) + R - 2:
                        spread(u)
                        u += 1
        stage1.close()

        stage2 = top.enter_context(ExitStack())
        yn = q
        qT = alloc(stage2, "qT", [P, CT, T])
        kT = alloc(stage2, "kT", [P, 2, T])
        buf = alloc(stage2, "buf", [P, 6 * 512])
        rope_k = alloc(stage2, "rope_k", [P, 2, 128])
        kc2 = qT.rearrange("p (n g) t -> p n g t", n=2)
        pe_rows = alloc(stage2, "pe_rows", [16, 2, P])
        peT = alloc(stage2, "peT", [P, 2, 16])
        w2 = alloc(stage2, "w2", [P, 2, 2, HD])
        hid = kcvc[:, 1, 0:496].rearrange("p (m n) -> p m n", m=4)
        kcmp = alloc(stage2, "kcmp", [NCMP, 2, 128])
        kcr = alloc(stage2, "kcr", [NCMP, 3, 128])
        kcT = alloc(stage2, "kcT", [P, NCMP])
        gate = alloc(stage2, "gate", [P, NT, 24])
        top8 = alloc(stage2, "top8", [P, 3, NT, HEADS])
        rsum = alloc(stage2, "rsum", [P, 3, NT, HEADS])
        coef = alloc(stage2, "coef", [P, 3, NT, HEADS])
        causal_bf = alloc(stage2, "causal_bf", [P, P], BF16)
        ident_bf = alloc(stage2, "ident_bf", [P, P], BF16)
        cmask_bf = alloc(stage2, "cmask_bf", [P, NT, NCMP], BF16)
        ot = kcvc[:, 0, :]
        prob = [buf[:, 512 * n:512 * n + 512] for n in range(3)]
        probT = [buf[:, 512 * n:512 * n + 512] for n in range(3, 6)]
        blk = [buf[:, 1024 * n:1024 * n + 32 * NCMP].rearrange("p (l g n) -> p l g n", l=16, g=2) for n in (1, 2)]
        pc = buf[:, 1024:1024 + 8 * NT * NCMP].rearrange("p (i h n) -> p i h n", i=NT, h=8)
        pcT = [buf[0:NCMP, 0:1024], buf[0:NCMP, 2048:3072]]
        (a_ld, a_kc, a_bf, a_peT, a_pe, a_blk, a_rq, a_qT, a_q, a_rk, a_kT, a_k, a_hid, a_g1, a_tanh, a_g2, a_cmp, a_cev,
         a_crope, a_cT, a_cTe, a_gate, a_sc, a_sub, a_cexp, a_pm, a_ptr, a_pte, a_oc, a_y, a_dve, a_pool) = (
            sem(f"a_{n}") for n in ("ld kc bf peT pe blk rq qT q rk kT k hid g1 tanh g2 cmp cev crope cT cTe gate sc sub "
                                    "cexp pm ptr pte oc y dve pool").split())
        a_S, a_mx, a_ex, a_TR, a_evD, a_evA, a_PV, a_out = (sem(f"a_{n}") for n in
                                                           ("S", "mx", "ex", "TR", "evD", "evA", "PV", "out"))
        items = [(i, b, hh) for i in reversed(range(NT)) for b in (1, 2) for hh in range(HEADS)]
        NI = len(items)

        with nc.Block() as block:
            @block.sync
            def _(sp):
                for parity in range(2):
                    for g in range(2):
                        sp.dma_start(kc2[HD * parity:HD * parity + HD, :, g, 0:T - parity],
                                     kcvc[HD * g:HD * g + HD, :, parity:T]).then_inc(a_kc, 16)
                for n, name in enumerate(("k", "v")):
                    sp.dma_start(pe_rows[:, n, :], A[f"cmp_pe_{name}"][0].rearrange("(l q) d -> l (q d)", q=2))\
                        .then_inc(a_ld, 16)
                    sp.dma_start(w2[:, n, :, :], A[f"cmp_w2_{name}"][0].rearrange("(t f) d -> f t d", t=2))\
                        .then_inc(a_ld, 16)
                load_units(sp, stage1_units, index["p_rwkv"] + R)
                sp.wait_ge(a_y, 1 + NT * 3)
                sp.dma_start(yn_dram, yn[:, :, :]).then_inc(a_out, 16)
                sp.wait_ge(a_out, 16)

            @block.gpsimd
            def _(pool):
                link = Chain(pool, a_pool)
                pool.wait_ge(a_pe, 1)
                pool.wait_ge(a_kc, 64)
                for n in range(2):
                    for half in range(2):
                        for g in range(2):
                            src = kc2[:, n, g, :].rearrange("p (m r x) -> p r m x", r=8, x=2)
                            link(pool.tensor_tensor(blk[n][:, 8 * half:8 * half + 8, g, :],
                                                    src[:, :, half:half + NCMP, 0],
                                                    peT[:, n, 8 * half:8 * half + 8].unsqueeze(2)
                                                    .to_broadcast([P, 8, NCMP]), ALU.add))
                    pool.sem_inc(a_blk, 1)
                for i in range(NT):
                    for b in range(2):
                        k = kv[:, i, 256 * b:256 * b + 128].rearrange("p (h d) -> p h d", d=32)
                        kh = kv[:, i, 256 * b:256 * b + 128].rearrange("p (g c d) -> p g c d", c=2, d=32)
                        t, s_ = (rope_k[:, x, :].rearrange("p (h d) -> p h d", d=32) for x in range(2))
                        th, sh = (rope_k[:, x, :].rearrange("p (g c d) -> p g c d", c=2, d=32) for x in range(2))
                        cos = C("cos")[:, 32 * i:32 * i + 32].unsqueeze(1).to_broadcast([P, 4, 32])
                        sin = C("sin")[:, 32 * i:32 * i + 32].unsqueeze(1).to_broadcast([P, 4, 32])
                        link(pool.tensor_tensor(t, k, cos, ALU.mult))
                        link(pool.tensor_tensor(s_, k, sin, ALU.mult))
                        link(pool.tensor_tensor(kh[:, :, 0, :], th[:, :, 0, :], sh[:, :, 1, :], ALU.subtract))
                        link(pool.tensor_tensor(kh[:, :, 1, :], th[:, :, 1, :], sh[:, :, 0, :], ALU.add))
                    pool.sem_inc(a_rk, 1)

            @block.vector
            def _(dve):
                link = Chain(dve, a_dve)
                dve.tensor_copy(causal_bf[:, :], C("causal")).then_inc(a_bf, 1)
                dve.tensor_copy(ident_bf[:, :], C("ident")).then_inc(a_bf, 1)
                dve.tensor_copy(cmask_bf[:, :, :], C("cmask").rearrange("p (i n) -> p i n", i=NT)).then_inc(a_bf, 1)
                dve.wait_ge(a_peT, 1)
                dve.tensor_copy(peT[:, :, :], ps[:, 7, 0:32].rearrange("p (n l) -> p n l", n=2)).then_inc(a_pe, 1)
                for i in range(NT):
                    x_ = q[:, i, :].rearrange("p (h d) -> p h d", d=32)
                    xh = q[:, i, :].rearrange("p (g c d) -> p g c d", c=2, d=32)
                    t, s_ = (prob[n].rearrange("p (h d) -> p h d", d=32) for n in range(2))
                    th, sh = (prob[n].rearrange("p (g c d) -> p g c d", c=2, d=32) for n in range(2))
                    cos = C("cos")[:, 32 * i:32 * i + 32].unsqueeze(1).to_broadcast([P, 16, 32])
                    sin = C("sin")[:, 32 * i:32 * i + 32].unsqueeze(1).to_broadcast([P, 16, 32])
                    link(dve.tensor_tensor(t, x_, cos, ALU.mult))
                    link(dve.tensor_tensor(s_, x_, sin, ALU.mult))
                    link(dve.tensor_tensor(xh[:, :, 0, :], th[:, :, 0, :], sh[:, :, 1, :], ALU.subtract))
                    dve.tensor_tensor(xh[:, :, 1, :], th[:, :, 1, :], sh[:, :, 0, :], ALU.add).then_inc(a_rq, 1)
                    dve.wait_ge(a_rq, i + 1)
                dve.wait_ge(a_blk, 2)
                for n in range(2):
                    xg, g1, g2, g3 = (hid[:, m, :] for m in range(4))
                    if n:
                        dve.wait_ge(a_cmp, 1)
                    dve.wait_ge(a_hid, n + 1)
                    link(dve.tensor_copy(xg, ps[:, (5, 0)[n], 0:4 * NCMP]))
                    link(dve.tensor_tensor(g1, xg, xg, ALU.mult))
                    link(dve.tensor_scalar(g1, g1, 0.044715, 1.0, ALU.mult, ALU.add))
                    dve.tensor_tensor(g1, g1, xg, ALU.mult).then_inc(a_g1, 1)
                    dve.wait_ge(a_tanh, n + 1)
                    link(dve.scalar_tensor_tensor(g3, g2, 1.0, xg, ALU.add, ALU.mult))
                    dve.tensor_scalar(g3, g3, 0.5, None, ALU.mult).then_inc(a_g2, 1)
                    dve.wait_ge(a_g2, n + 1)
                dve.wait_ge(a_cmp, 2)
                link(dve.tensor_copy(kcmp[:, :, :], ps[0:NCMP, 7, 256:512].rearrange("p (n d) -> p n d", n=2)))
                kk_, kh = (kcmp[:, 0, :].rearrange("p (h d) -> p h d", d=32),
                           kcr[:, 2, :].rearrange("p (g c d) -> p g c d", c=2, d=32))
                t, s_ = (kcr[:, n, :].rearrange("p (h d) -> p h d", d=32) for n in range(2))
                th, sh = (kcr[:, n, :].rearrange("p (g c d) -> p g c d", c=2, d=32) for n in range(2))
                link(dve.tensor_tensor(t, kk_, C("ccos")[0:NCMP, :].unsqueeze(1).to_broadcast([NCMP, 4, 32]), ALU.mult))
                link(dve.tensor_tensor(s_, kk_, C("csin")[0:NCMP, :].unsqueeze(1).to_broadcast([NCMP, 4, 32]), ALU.mult))
                link(dve.tensor_tensor(kh[:, :, 0, :], th[:, :, 0, :], sh[:, :, 1, :], ALU.subtract))
                dve.tensor_tensor(kh[:, :, 1, :], th[:, :, 1, :], sh[:, :, 0, :], ALU.add).then_inc(a_crope, 1)
                dve.wait_ge(a_cT, 1)
                dve.tensor_copy(kcT[:, :], ps[:, 7, 0:NCMP]).then_inc(a_cTe, 1)

                for i in range(NT):
                    dve.wait_ge(a_sc, i + 1)
                    S = ps[:, 2 * (i % 2):2 * (i % 2) + 2, 0:4 * NCMP].rearrange("p g (j n) -> p g j n", j=4)
                    mx = top8[:, 0, i, :].rearrange("p (g j) -> p g j", g=2)
                    link(dve.tensor_reduce(mx, S, AX, ALU.max))
                    dve.tensor_tensor(pc[:, i, :, :].rearrange("p (g j) n -> p g j n", g=2), S,
                                      mx.unsqueeze(3).to_broadcast([P, 2, 4, NCMP]), ALU.subtract).then_inc(a_sub, 1)
                    dve.wait_ge(a_cexp, i + 1)
                    link(dve.tensor_reduce(rsum[:, 0, i, :], pc[:, i, :, :], AX, ALU.add))
                    seen = C("cseen")[:, NCMP * i:NCMP * i + NCMP].unsqueeze(1).to_broadcast([P, HEADS, NCMP])
                    dve.tensor_tensor(pc[:, i, :, :], pc[:, i, :, :], seen, ALU.mult).then_inc(a_pm, 1)
                dve.wait_ge(a_gate, 1)

                def coefs(b, i):
                    link(dve.reciprocal(coef[:, b, i, :], rsum[:, b, i, :]))
                    g = gate[:, i, :].rearrange("p (h b) -> p b h", b=3)[:, b, :]
                    link(dve.tensor_tensor(coef[:, b, i, :], coef[:, b, i, :], g, ALU.mult))
                    return coef[:, b, i, :].unsqueeze(2).to_broadcast([P, HEADS, HD])

                def heads(ap):
                    return ap.rearrange("p (h d) -> p h d", h=HEADS)

                dve.sem_inc(a_y, 1)
                for i in range(NT):
                    c = coefs(0, i)
                    dve.wait_ge(a_oc, i + 1)
                    dve.tensor_tensor(heads(yn[:, i, :]), heads(ps[:, 5 + i % 2, :]), c, ALU.mult).then_inc(a_y, 1)
                    dve.wait_ge(a_y, i + 2)

                def combine(grp):
                    i, b = NT - 1 - grp // 2, 1 + grp % 2
                    dve.wait_ge(a_ex, 8 * (grp + 1))
                    c = coefs(b, i)
                    dve.wait_ge(a_PV, 8 * (grp + 1))
                    link(dve.tensor_tensor(heads(ot), heads(ps[:, 5 + grp % 2, :]), c, ALU.mult))
                    dve.tensor_tensor(yn[:, i, :], yn[:, i, :], ot, ALU.add).then_inc(a_y, 1)
                    dve.wait_ge(a_y, 1 + NT + grp + 1)

                for t in range(NI + 4):
                    if t < NI:
                        i, b, hh = items[t]
                        dve.wait_ge(a_S, t + 1)
                        dve.tensor_reduce(top8[:, b, i, hh:hh + 1], ps[:, t % 3, 0:P * (i + 1)], AX, ALU.max,
                                          negate=True).then_inc(a_mx, 1)
                    e = t - 2
                    if 0 <= e < NI and e % 2 == 0:
                        n = P * (items[e][0] + 1)
                        dve.wait_ge(a_TR, e + 1)
                        dve.tensor_copy(probT[e % 3][:, 0:n], ps[:, 3 + e % 2, 0:n]).then_inc(a_evD, 1)
                    if t >= 11 and (t - 11) % 8 == 0 and (t - 11) // 8 < NI // 8:
                        combine((t - 11) // 8)

            @block.scalar
            def _(act):
                act.activation(gate[:, :, :], glog[:, :, :], ACT.Sigmoid).then_inc(a_gate, 1)
                act.wait_ge(a_blk, 2)
                for i in range(NT):
                    act.wait_ge(a_qT, i + 1)
                    act.activation(qT[:, :, P * i:P * i + P], ps[:, i % 2, :].rearrange("p (j t) -> p j t", j=CT),
                                   ACT.Copy, scale=HD ** -0.5).then_inc(a_q, 1)
                for i in range(NT):
                    act.wait_ge(a_kT, i + 1)
                    act.activation(kT[:, :, P * i:P * i + P],
                                   ps[:, 2 + i % 2, 0:256].rearrange("p (b t) -> p b t", b=2), ACT.Copy)\
                        .then_inc(a_k, 1)
                for n in range(2):
                    act.wait_ge(a_g1, n + 1)
                    act.activation(hid[:, 2, :], hid[:, 1, :], ACT.Tanh, scale=float(np.sqrt(2 / np.pi)))\
                        .then_inc(a_tanh, 1)
                for i in range(NT):
                    act.wait_ge(a_sub, i + 1)
                    act.activation(pc[:, i, :, :], pc[:, i, :, :], ACT.Exp).then_inc(a_cexp, 1)
                for i in range(NT):
                    act.wait_ge(a_ptr, i + 1)
                    if i >= 2:
                        act.wait_ge(a_oc, i - 1)
                    act.activation(pcT[i % 2], ps[0:NCMP, 1:3, :].rearrange("p b n -> p (b n)")
                                   if i % 2 else ps[0:NCMP, 3:5, :].rearrange("p b n -> p (b n)"), ACT.Copy)\
                        .then_inc(a_pte, 1)
                act.wait_ge(a_oc, NT)
                for t in range(NI + 4):
                    if t < NI:
                        i, b, hh = items[t]
                        act.wait_ge(a_mx, t + 1)
                        if t >= 3:
                            act.wait_ge(a_TR, t - 2)
                        n = P * (i + 1)
                        act.activation(prob[t % 3][:, 0:n], ps[:, t % 3, 0:n], ACT.Exp,
                                       bias=top8[:, b, i, hh:hh + 1], accum_out=rsum[:, b, i, hh:hh + 1])\
                            .then_inc(a_ex, 1)
                    e = t - 2
                    if 0 <= e < NI and e % 2 == 1:
                        n = P * (items[e][0] + 1)
                        act.wait_ge(a_TR, e + 1)
                        act.activation(probT[e % 3][:, 0:n], ps[:, 3 + e % 2, 0:n], ACT.Copy).then_inc(a_evA, 1)

            @block.tensor
            def _(pe):
                ident = C("ident")
                pe.wait_ge(a_ld, 16 * 4)
                for n in range(2):
                    ins = pe.transpose(ps[:, 7, 16 * n:16 * n + 16], pe_rows[:, n, :], ident[0:16, 0:16])
                ins.then_inc(a_peT, 1)
                for i in range(NT):
                    pe.wait_ge(a_rq, i + 1)
                    if i >= 2:
                        pe.wait_ge(a_q, i - 1)
                    for j in range(CT):
                        ins = pe.transpose(ps[:, i % 2, P * j:P * j + P], q[:, i, P * j:P * j + P], ident)
                    ins.then_inc(a_qT, 1)

                def compress_hidden(n):
                    name = f"w1{'kv'[n]}"
                    pe.wait_ge(a_blk, n + 1)
                    if n:
                        pe.wait_ge(a_q, NT)
                    need(pe, name)
                    for t in range(2):
                        for l in range(16):
                            ins = pe.matmul(ps[:, (5, 0)[n], 2 * NCMP * t:2 * NCMP * (t + 1)],
                                            slot(name, 16, 256)[:, l, P * t:P * t + P],
                                            blk[n][:, l, :, :], start=(l == 0), stop=(l == 15))
                    ins.then_inc(a_hid, 1)
                    pe.wait_ge(a_hid, n + 1)
                    pe.sem_inc(unit_free[index[name] % R], 1)

                def compress_out(n):
                    pe.wait_ge(a_g2, n + 1)
                    for g in range(2):
                        for t in range(2):
                            ins = pe.matmul(ps[0:NCMP, 7, 256 + 128 * n + HD * g:256 + 128 * n + HD * g + HD],
                                            hid[:, 3, NCMP * (2 * t + g):NCMP * (2 * t + g + 1)], w2[:, n, t, :],
                                            start=(t == 0), stop=(t == 1))
                    ins.then_inc(a_cmp, 1)

                compress_hidden(0)
                for i in range(NT):
                    pe.wait_ge(a_rk, i + 1)
                    if i >= 2:
                        pe.wait_ge(a_k, i - 1)
                    for b in range(2):
                        ins = pe.transpose(ps[:, 2 + i % 2, P * b:P * b + P], kv[:, i, 256 * b:256 * b + P], ident)
                    ins.then_inc(a_kT, 1)
                compress_hidden(1)
                pe.wait_ge(a_pe, 1)
                compress_out(0)
                compress_out(1)
                pe.wait_ge(a_crope, 1)
                pe.transpose(ps[:, 7, 0:NCMP], kcr[:, 2, :], ident[0:NCMP, 0:NCMP]).then_inc(a_cT, 1)
                pe.wait_ge(a_cTe, 1)
                pe.wait_ge(a_q, NT)
                pe.wait_ge(a_k, NT)
                pe.wait_ge(a_bf, 3)
                for i in range(NT):
                    if i >= 2:
                        pe.wait_ge(a_sub, i - 1)
                    for hh in range(HEADS):
                        g, j = hh // 4, hh % 4
                        o = ps[:, 2 * (i % 2) + g, NCMP * j:NCMP * (j + 1)]
                        pe.matmul(o, qT[HD * g:HD * g + HD, j, P * i:P * i + P], kcT[HD * g:HD * g + HD, :],
                                  start=True, stop=False)
                        ins = pe.matmul(o, ident_bf[:, :], cmask_bf[:, i, :], start=False, stop=True)
                    ins.then_inc(a_sc, 1)
                pe.wait_ge(a_sub, NT)
                for i in range(NT + 1):
                    if i < NT:
                        pe.wait_ge(a_pm, i + 1)
                        if i >= 2:
                            pe.wait_ge(a_pte, i - 1)
                        b0 = 1 if i % 2 else 3
                        for hh in range(HEADS):
                            ins = pe.transpose(ps[0:NCMP, b0 + hh // 4, P * (hh % 4):P * (hh % 4) + P],
                                               pc[:, i, hh, :], ident)
                        ins.then_inc(a_ptr, 1)
                    if i >= 1:
                        m = i - 1
                        pe.wait_ge(a_pte, m + 1)
                        if m >= 2:
                            pe.wait_ge(a_y, m)
                        for hh in range(HEADS):
                            ins = pe.matmul(ps[:, 5 + m % 2, HD * hh:HD * hh + HD], pcT[m % 2][:, P * hh:P * hh + P],
                                            kcmp[:, 1, HD * (hh // 4):HD * (hh // 4) + HD], start=True, stop=True)
                        ins.then_inc(a_oc, 1)
                pe.wait_ge(a_pte, NT)
                warm(pe)
                for t in range(NI + 4):
                    if t < NI:
                        i, b, hh = items[t]
                        g, j = hh // 4, hh % 4
                        if t >= 3:
                            pe.wait_ge(a_ex, t - 2)
                        lhs = qT[HD * g:HD * g + HD, j, P * i:P * i + P]
                        pe.matmul(ps[:, t % 3, 0:P * (i + 1)], lhs, kT[HD * g:HD * g + HD, b - 1, 0:P * (i + 1)],
                                  start=True, stop=False)
                        pe.matmul(ps[:, t % 3, P * i:P * i + P], ident_bf[:, :], causal_bf[:, :], start=False,
                                  stop=True).then_inc(a_S, 1)
                    m = t - 2
                    if 0 <= m < NI:
                        pe.wait_ge(a_ex, m + 1)
                        if m >= 2:
                            pe.wait_ge((a_evD, a_evA)[m % 2], m // 2)
                        else:
                            pe.wait_ge(a_pte, NT)
                        for j in range(items[m][0] + 1):
                            ins = pe.transpose(ps[:, 3 + m % 2, P * j:P * j + P], prob[m % 3][:, P * j:P * j + P], ident)
                        ins.then_inc(a_TR, 1)
                    m = t - 3
                    if 0 <= m < NI:
                        i, b, hh = items[m]
                        grp = m // 8
                        pe.wait_ge((a_evD, a_evA)[m % 2], m // 2 + 1)
                        if hh == 0:
                            pe.wait_ge(a_y, 1 + NT + grp - 1 if grp >= 2 else 1 + NT)
                        for j in range(i + 1):
                            ins = pe.matmul(ps[:, 5 + grp % 2, HD * hh:HD * hh + HD], probT[m % 3][:, P * j:P * j + P],
                                            kv[:, j, 256 * (b - 1) + 128 + HD * (hh // 4):
                                               256 * (b - 1) + 128 + HD * (hh // 4) + HD],
                                            start=(j == 0), stop=(j == i))
                        ins.then_inc(a_PV, 1)
        stage2.close()
        attn.close()
        end_stage()

        stage3 = top.enter_context(ExitStack())
        NL = consts_np.shape[1] - NC
        late = alloc(stage3, "late", [P, NL])
        vt = alloc(stage3, "vt", [P, NT, RW])
        bt = alloc(stage3, "bt", [P, CT, T])
        bonus = alloc(stage3, "bonus", [P, NT, HEADS])
        carry = alloc(stage3, "carry", [P, CT, NT - 1])
        prep = top.enter_context(ExitStack())
        lora = alloc(prep, "lora", [P, RW])
        logp = alloc(prep, "logp", [P, CT, NT * (P + 1)])
        av = alloc(prep, "av", [P, CT, T])
        kkn = bt
        sg = alloc(prep, "sg", [P, 2, T])
        tmp = alloc(prep, "tmp", [P, 2, T])
        ee = alloc(prep, "ee", [P, NT * (P + 1)])
        ei = alloc(prep, "ei", [P, T])
        omka = alloc(prep, "omka", [P, CT])
        e0 = alloc(prep, "e0", [P, NT])
        wtab = alloc(prep, "wtab", [P, T])
        rT, kT_, vT = zrT[:, 0:4, :], zrT[:, 4:8, :], zrT[:, 8:12, :]

        def L8(name):
            a_, b_ = at[name]
            return late[:, a_ - NC:b_ - NC]

        DK = -float(np.exp(-0.5))
        (w_ld, w_th, w_w, w_a, w_sw, w_sa, w_v, w_ve, w_kk, w_sq, w_ss, w_rt, w_kn, w_lp, w_e, w_rk, w_bo, w_use, w_dve,
         w_bev) = (sem(f"w_{n}") for n in "ld th w a sw sa v ve kk sq ss rt kn lp e rk bo use dve bev".split())

        with nc.Block() as block:
            @block.sync
            def _(sp):
                sp.dma_start(late[:, :], A["consts"][:, NC:NC + NL]).then_inc(w_ld, 16)
                sp.dma_start(lora[0:HD, :], A["rwkv_w2"][0]).then_inc(w_ld, 16)
                sp.dma_start(lora[HD:P, :], A["rwkv_a2"][0]).then_inc(w_ld, 16)
                sp.wait_ge(w_ld, 48)

            @block.scalar
            def _(act):
                act.activation(zrT[0:HD, 12, :], zrT[0:HD, 12, :], ACT.Tanh).then_inc(w_th, 1)
                act.activation(zrT[:, 13, :], zrT[:, 13, :], ACT.Sigmoid).then_inc(w_th, 1)
                for c in range(CT):
                    act.wait_ge(w_w, c + 1)
                    if c >= 2:
                        act.wait_ge(w_lp, c - 1)
                    act.activation(sg[:, c % 2, :], ps[:, 0, :], ACT.Sigmoid, bias=par[:, 14 + c:15 + c])\
                        .then_inc(w_sw, 1)
                    act.wait_ge(w_a, c + 1)
                    act.activation(av[:, c, :], ps[:, 1, :], ACT.Sigmoid, bias=par[:, 18 + c:19 + c]).then_inc(w_sa, 1)
                    act.wait_ge(w_v, c + 1)
                    act.activation(vt[:, :, P * c:P * c + P], ps[:, 2, :].rearrange("p (i d) -> p i d", i=NT),
                                   ACT.Copy).then_inc(w_ve, 1)
                    act.wait_ge(w_kk, c + 1)
                    if c >= 2:
                        act.wait_ge(w_ss, c - 1)
                    act.activation(tmp[:, c % 2, :], kkn[:, c, :], ACT.Square).then_inc(w_sq, 1)
                act.wait_ge(w_ss, CT)
                act.wait_ge(w_lp, CT)
                for c in range(CT):
                    act.wait_ge(w_ss, c + 1)
                    if c >= 2:
                        act.wait_ge(w_kn, c - 1)
                    act.activation(sg[:, c % 2, :], ps[:, 4 + c, :], ACT.Sqrt).then_inc(w_rt, 1)
                for c in range(CT):
                    act.wait_ge(w_lp, c + 1)
                    if c >= 1:
                        act.wait_ge(w_use, c)
                    act.activation(ee[:, :], logp[:, c, :], ACT.Exp, scale=DK).then_inc(w_e, 1)
                    lp = logp[:, c, :].rearrange("p (c t) -> p c t", c=NT)
                    act.activation(ei[:, :].rearrange("p (c t) -> p c t", c=NT), lp[:, :, 1:], ACT.Exp, scale=-DK)\
                        .then_inc(w_e, 1)
                    act.activation(e0[:, :], lp[:, :, 0], ACT.Exp, scale=-DK).then_inc(w_e, 1)

            @block.vector
            def _(dve):
                link = Chain(dve, w_dve)
                dve.tensor_scalar(omka[:, :], par[:, 26:30], -1.0, 1.0, ALU.mult, ALU.add).then_inc(w_dve, 1)
                link.n += 1
                for c in range(CT):
                    dve.tensor_scalar(kkn[:, c, :], kT_[:, c, :], par[:, 22 + c:23 + c], None, ALU.mult)\
                        .then_inc(w_kk, 1)
                dve.wait_ge(w_ld, 48)
                for c in range(CT):
                    dve.wait_ge(w_sw, c + 1)
                    for i in range(NT):
                        link(dve.tensor_tensor_scan(wtab[:, P * i:P * i + P], C("ones"),
                                                    sg[:, c % 2, P * i:P * i + P], 0.0, ALU.mult, ALU.add))
                    cum = wtab[:, :].rearrange("p (c t) -> p c t", c=NT)
                    lp = logp[:, c, :].rearrange("p (c t) -> p c t", c=NT)
                    mid = cum[:, :, P // 2 - 1:P // 2]
                    link(dve.tensor_tensor(lp[:, :, 1:], cum, mid.to_broadcast([P, NT, P]), ALU.subtract))
                    dve.tensor_scalar(lp[:, :, 0:1], mid, -1.0, None, ALU.mult).then_inc(w_lp, 1)
                    dve.wait_ge(w_lp, c + 1)
                for c in range(CT):
                    dve.wait_ge(w_rt, c + 1)
                    s_ = sg[:, c % 2, :]
                    link(dve.tensor_scalar(s_, s_, 1e-12, None, ALU.max))
                    link(dve.reciprocal(s_, s_))
                    dve.tensor_tensor(kkn[:, c, :], kkn[:, c, :], s_, ALU.mult).then_inc(w_kn, 1)
                    dve.wait_ge(w_kn, c + 1)
                dve.wait_ge(w_ve, CT)
                for c in range(CT):
                    dve.wait_ge(w_sa, c + 1)
                    t0, t1 = tmp[:, 0, :], tmp[:, 1, :]
                    link(dve.tensor_scalar(t0, av[:, c, :], par[:, 26 + c:27 + c], omka[:, c:c + 1], ALU.mult, ALU.add))
                    link(dve.tensor_tensor(kT_[:, c, :], kT_[:, c, :], t0, ALU.mult))
                    if c >= 1:
                        dve.wait_ge(w_bo, c)
                    dve.scalar_tensor_tensor(t1, rT[:, c, :], par[:, 30 + c:31 + c], kT_[:, c, :], ALU.mult, ALU.mult)\
                        .then_inc(w_rk, 1)
                    link(dve.tensor_tensor(av[:, c, :], kkn[:, c, :], av[:, c, :], ALU.mult))
                    dve.wait_ge(w_e, 3 * (c + 1))
                    dve.wait_ge(w_rk, c + 1)
                    e3 = ee[:, :].rearrange("p (c t) -> p c t", c=NT)

                    def chunks(ap):
                        return ap.rearrange("p (c t) -> p c t", c=NT)

                    link(dve.tensor_tensor(chunks(rT[:, c, :]), chunks(rT[:, c, :]), e3[:, :, 1:], ALU.mult))
                    link(dve.tensor_tensor(kT_[:, c, :], kT_[:, c, :], ei[:, :], ALU.mult))
                    link(dve.scalar_tensor_tensor(chunks(vT[:, c, :]), chunks(kkn[:, c, :]), -1.0, e3[:, :, 0:P],
                                                  ALU.mult, ALU.mult))
                    link(dve.tensor_tensor(bt[:, c, :], av[:, c, :], ei[:, :], ALU.mult))
                    dve.tensor_tensor(carry[:, c, :], e3[:, 0:NT - 1, P], e0[:, 1:NT], ALU.mult).then_inc(w_use, 1)
                dve.wait_ge(w_bo, CT)
                dve.tensor_copy(bonus[:, :, :], ps[:, 3, 0:8 * NT].rearrange("p (i h) -> p i h", i=NT)).then_inc(w_bev, 1)

            @block.tensor
            def _(pe):
                pe.wait_ge(w_ld, 48)
                pe.wait_ge(w_th, 2)
                for c in range(CT):
                    if c:
                        pe.wait_ge(w_sw, c)
                    pe.matmul(ps[:, 0, :], lora[0:HD, P * c:P * c + P], zrT[0:HD, 12, :], start=True, stop=True)\
                        .then_inc(w_w, 1)
                    if c:
                        pe.wait_ge(w_sa, c)
                    pe.matmul(ps[:, 1, :], lora[HD:P, P * c:P * c + P], zrT[HD:P, 12, :], start=True, stop=True)\
                        .then_inc(w_a, 1)
                    if c:
                        pe.wait_ge(w_ve, c)
                    for i in range(NT):
                        ins = pe.transpose(ps[:, 2, P * i:P * i + P], vT[:, c, P * i:P * i + P], C("ident"))
                    ins.then_inc(w_v, 1)
                    pe.wait_ge(w_sq, c + 1)
                    pe.matmul(ps[:, 4 + c, :], L8("headsum"), tmp[:, c % 2, :], start=True, stop=True).then_inc(w_ss, 1)
                for c in range(CT):
                    pe.wait_ge(w_rk, c + 1)
                    for i in range(NT):
                        ins = pe.matmul(ps[:, 3, HEADS * i + 2 * c:HEADS * i + 2 * c + 2], tmp[:, 1, P * i:P * i + P],
                                        L8("headsel"), start=True, stop=True)
                    ins.then_inc(w_bo, 1)
        prep.close()

        chunk = top.enter_context(ExitStack())
        y = rT.rearrange("p c (i t) -> p i c t", i=NT)
        gb = alloc(chunk, "gb", [P, 2, 4, 2, P])
        gk = alloc(chunk, "gk", [P, 2, 4, 2, P])
        xm = alloc(chunk, "xm", [P, 2, 4, P])
        xt = alloc(chunk, "xt", [P, 2, 4, P])
        t1 = alloc(chunk, "t1", [P, 2, 4, P])
        lm = alloc(chunk, "lm", [P, 2, 4, P])
        kb = lm[:, :, :, :].rearrange("p m j t -> p m (j t)")
        state = alloc(chunk, "state", [P, CT, HD])
        wsb = t1[:, 0, :, :].rearrange("p j (b d) -> p (j b) d", b=2)
        usb = t1[:, 1, :, :].rearrange("p j (b d) -> p (j b) d", b=2)
        g_gr, g_ge, g_x0, g_xt0, g_x0e, g_lm, g_t1, g_t1e, g_x, g_xe, g_xt, g_xte = (
            sem(f"g_{n}") for n in "gr ge x0 xt0 x0e lm t1 t1e x xe xt xte".split())
        g_kb, g_kbe, g_w, g_we, g_u, g_ue, g_y, g_ye, g_s, g_se, g_dve, g_pool = (
            sem(f"g_{n}") for n in "kb kbe w we u ue y ye s se dve pool".split())
        NLV = 6
        bank = {"t1": 0, "x": 2, "xt": 4, "gram": 6}

        def spread4(ap):
            return ap.unsqueeze(1).to_broadcast([P, 4, P])

        with nc.Block() as block:
            @block.gpsimd
            def _(pool):
                for c in range(NT):
                    for n in range(1, NLV + 1):
                        for p_ in range(2):
                            pool.wait_ge(g_ge, 8 * c + 4 * (p_ + 1))
                            s_ = (c * NLV + n - 1) * 2 + p_
                            if s_ >= 2:
                                pool.wait_ge(g_t1, s_ - 1)
                            if n == 1 and c:
                                pool.wait_ge(g_s, c)
                            pool.tensor_tensor(lm[:, p_, :, :], gb[:, p_, :, 0, :], spread4(L8(f"lvl{n}")), ALU.mult)\
                                .then_inc(g_lm, 1)

            @block.vector
            def _(dve):
                link = Chain(dve, g_dve)
                for c in range(NT):
                    if c:
                        dve.wait_ge(g_y, c)
                    for p_ in range(2):
                        for m in range(4):
                            n = 8 * c + 4 * p_ + m
                            dve.wait_ge(g_gr, n + 1)
                            dst = (gb, gk)[m // 2][:, p_, 2 * (m % 2):2 * (m % 2) + 2, :, :]\
                                .rearrange("p j a t -> p j (a t)")
                            a_ = at["strict"][0]
                            mask = cst[:, a_:a_ + 2 * P].unsqueeze(1).to_broadcast([P, 2, 2 * P])
                            dve.tensor_tensor(dst, ps[:, 6 + m % 2, :].rearrange("p (j n) -> p j n", j=2), mask,
                                              ALU.mult).then_inc(g_ge, 1)
                            if m == 1:
                                dve.wait_ge(g_ge, n + 1)
                                link(dve.tensor_tensor(xt[:, p_, :, :], gb[:, p_, :, 0, :], spread4(L8("lvl0")),
                                                       ALU.mult))
                                dve.tensor_tensor(xt[:, p_, :, :], xt[:, p_, :, :], spread4(C("ident")), ALU.add)\
                                    .then_inc(g_xt0, 1)
                    for n in range(NLV):
                        for p_ in range(2):
                            s_ = (c * NLV + n) * 2 + p_
                            dve.wait_ge(g_t1, s_ + 1)
                            if n == 0 and c:
                                dve.wait_ge(g_s, c)
                            dve.tensor_tensor(t1[:, p_, :, :], ps[:, bank["t1"] + p_, :].rearrange("p (j t) -> p j t", j=4),
                                              spread4(C("ident")), ALU.add).then_inc(g_t1e, 1)
                    dve.wait_ge(g_w, c + 1)
                    for p_ in range(2):
                        link(dve.tensor_copy(wsb.rearrange("p (j b) d -> p b j d", b=2)[:, p_, :, :],
                                             ps[:, 0 + p_, 0:256].rearrange("p (j d) -> p j d", j=4)))
                    dve.sem_inc(g_we, 1)
                    dve.wait_ge(g_s, c + 1)
                    if c < NT - 1:
                        dve.wait_ge(g_y, c + 1)
                        for p_ in range(2):
                            r0 = HD * p_
                            new = ps[r0:r0 + HD, 6, :].rearrange("p (c n) -> p c n", c=CT)[:, :, r0:r0 + HD]
                            st = state[r0:r0 + HD, :, :]
                            if c:
                                link(dve.tensor_tensor(st, st, new, ALU.add))
                                new = st
                            link(dve.tensor_tensor(st, new, carry[r0:r0 + HD, :, c:c + 1].to_broadcast([HD, CT, HD]),
                                                   ALU.mult))
                        dve.sem_inc(g_se, 1)

            @block.scalar
            def _(act):
                for c in range(NT):
                    for p_ in range(2):
                        act.wait_ge(g_x0, 2 * c + p_ + 1)
                        act.activation(xm[:, p_, :, :], ps[:, bank["x"] + p_, :].rearrange("p (j t) -> p j t", j=4),
                                       ACT.Copy).then_inc(g_x0e, 1)
                    for n in range(NLV):
                        if n < NLV - 1:
                            for p_ in range(2):
                                s_ = (c * (NLV - 1) + n) * 2 + p_
                                act.wait_ge(g_x, s_ + 1)
                                act.activation(xm[:, p_, :, :],
                                               ps[:, bank["x"] + p_, :].rearrange("p (j t) -> p j t", j=4),
                                               ACT.Copy).then_inc(g_xe, 1)
                        for p_ in range(2):
                            s_ = (c * NLV + n) * 2 + p_
                            act.wait_ge(g_xt, s_ + 1)
                            act.activation(xt[:, p_, :, :], ps[:, bank["xt"] + p_, :].rearrange("p (j t) -> p j t", j=4),
                                           ACT.Copy).then_inc(g_xte, 1)
                    for m in range(2):
                        act.wait_ge(g_kb, 2 * c + m + 1)
                        act.activation(kb[:, m, :], ps[:, 6 + m, :], ACT.Copy).then_inc(g_kbe, 1)
                    act.wait_ge(g_u, c + 1)
                    act.activation(usb, ps[:, 2, :].rearrange("p (h d) -> p h d", h=HEADS), ACT.Copy).then_inc(g_ue, 1)
                    act.wait_ge(g_y, c + 1)
                    for p_ in range(2):
                        act.activation(y[:, c, :, HD * p_:HD * p_ + HD],
                                       ps[:, 4 + p_, 0:256].rearrange("p (j d) -> p j d", j=4), ACT.Copy)\
                            .then_inc(g_ye, 1)

            @block.tensor
            def _(pe):
                ident = C("ident")
                ar = zrT[:, :, :].rearrange("p t (c n) -> p t c n", c=NT)
                for c in range(NT):
                    for p_ in range(2):
                        r0 = HD * p_
                        for m in range(4):
                            n = 8 * c + 4 * p_ + m
                            if n % 8 >= 2:
                                pe.wait_ge(g_ge, n - 1)
                            elif c:
                                pe.wait_ge(g_se, c)
                            for j in range(2):
                                ct = 2 * (m % 2) + j
                                lhs = (bt[r0:r0 + HD, ct, P * c:P * c + P], zrT[r0:r0 + HD, 4 + ct, P * c:P * c + P])[m // 2]
                                rhs = ar[r0:r0 + HD, ct:ct + 9:8, c, :]
                                for a_ in range(2):
                                    ins = pe.matmul(ps[:, 6 + m % 2, 256 * j + P * a_:256 * j + P * a_ + P], lhs,
                                                    rhs[:, 1 - a_, :], start=True, stop=True)
                            ins.then_inc(g_gr, 1)
                    for p_ in range(2):
                        pe.wait_ge(g_xt0, 2 * c + p_ + 1)
                        for j in range(4):
                            ins = pe.transpose(ps[:, bank["x"] + p_, P * j:P * j + P], xt[:, p_, j, :], ident)
                        ins.then_inc(g_x0, 1)
                    for n in range(NLV):
                        for p_ in range(2):
                            s_ = (c * NLV + n) * 2 + p_
                            pe.wait_ge(g_lm, s_ + 1)
                            if n == 0:
                                pe.wait_ge(g_x0e, 2 * c + p_ + 1)
                            else:
                                pe.wait_ge(g_xe, (c * (NLV - 1) + n - 1) * 2 + p_ + 1)
                            for j in range(4):
                                ins = pe.matmul(ps[:, bank["t1"] + p_, P * j:P * j + P], lm[:, p_, j, :], xm[:, p_, j, :],
                                                start=True, stop=True)
                            ins.then_inc(g_t1, 1)
                        if n < NLV - 1:
                            for p_ in range(2):
                                s_ = (c * NLV + n) * 2 + p_
                                pe.wait_ge(g_t1e, s_ + 1)
                                if n:
                                    pe.wait_ge(g_xte, s_ - 1)
                                for j in range(4):
                                    ins = pe.matmul(ps[:, bank["x"] + p_, P * j:P * j + P], xt[:, p_, j, :],
                                                    t1[:, p_, j, :], start=True, stop=True)
                                ins.then_inc(g_x, 1)
                            for p_ in range(2):
                                pe.wait_ge(g_xe, (c * (NLV - 1) + n) * 2 + p_ + 1)
                                for j in range(4):
                                    ins = pe.transpose(ps[:, bank["xt"] + p_, P * j:P * j + P], xm[:, p_, j, :], ident)
                                ins.then_inc(g_xt, 1)
                        else:
                            for p_ in range(2):
                                s_ = (c * NLV + n) * 2 + p_
                                pe.wait_ge(g_t1e, s_ + 1)
                                pe.wait_ge(g_xte, s_ - 1)
                                for j in range(4):
                                    ins = pe.matmul(ps[:, bank["xt"] + p_, P * j:P * j + P], t1[:, p_, j, :],
                                                    xt[:, p_, j, :], start=True, stop=True)
                                ins.then_inc(g_xt, 1)
                    pe.wait_ge(g_ge, 8 * (c + 1))
                    for m in range(2):
                        for ct in range(CT):
                            src = (zrT[:, 4 + ct, P * c:P * c + P], bt[:, ct, P * c:P * c + P])[m]
                            ins = pe.transpose(ps[:, 6 + m, P * ct:P * ct + P], src, ident)
                        ins.then_inc(g_kb, 1)
                    pe.wait_ge(g_t1e, 2 * NLV * (c + 1))
                    if c:
                        pe.wait_ge(g_se, c)
                    for h_ in range(HEADS):
                        ct, p_ = h_ // 2, h_ % 2
                        o = ps[:, p_, HD * ct:HD * ct + HD]
                        v_ = vt[:, c, HD * h_:HD * h_ + HD]
                        ins = pe.matmul(o, gk[:, p_, ct, 0, :], v_, start=True, stop=(c == 0))
                        if c:
                            ins = pe.matmul(o, zrT[HD * p_:HD * p_ + HD, 8 + ct, P * c:P * c + P],
                                            state[HD * p_:HD * p_ + HD, ct, :], start=False, stop=True)
                    ins.then_inc(g_w, 1)
                    pe.wait_ge(g_we, c + 1)
                    pe.wait_ge(g_xte, 2 * NLV * (c + 1))
                    for h_ in range(HEADS):
                        ins = pe.matmul(ps[:, 2, HD * h_:HD * h_ + HD], xt[:, h_ % 2, h_ // 2, :], wsb[:, h_, :],
                                        start=True, stop=True)
                    ins.then_inc(g_u, 1)
                    pe.wait_ge(g_ue, c + 1)
                    for h_ in range(HEADS):
                        ct, p_ = h_ // 2, h_ % 2
                        o = ps[:, 4 + p_, HD * ct:HD * ct + HD]
                        v_ = vt[:, c, HD * h_:HD * h_ + HD]
                        if c:
                            pe.matmul(o, zrT[HD * p_:HD * p_ + HD, ct, P * c:P * c + P],
                                      state[HD * p_:HD * p_ + HD, ct, :], start=True, stop=False)
                        pe.matmul(o, gb[:, p_, ct, 1, :], usb[:, h_, :], start=(c == 0), stop=False)
                        ins = pe.matmul(o, gk[:, p_, ct, 1, :], v_, start=False, stop=True)
                    ins.then_inc(g_y, 1)
                    pe.wait_ge(g_kbe, 2 * (c + 1))
                    for ct in range(CT):
                        o = ps[:, 6, P * ct:P * ct + P]
                        pe.matmul(o, kb[:, 1, P * ct:P * ct + P], usb[:, 2 * ct:2 * ct + 2, :], start=True, stop=False)
                        ins = pe.matmul(o, kb[:, 0, P * ct:P * ct + P], vt[:, c, P * ct:P * ct + P], start=False,
                                        stop=True)
                    ins.then_inc(g_s, 1)
                    pe.wait_ge(g_ye, 2 * (c + 1))
        chunk.close()

        post = top.enter_context(ExitStack())
        yr = zrT[:, 8:12, :]
        lnw = alloc(post, "lnw", [P, RW])
        lnb = alloc(post, "lnb", [P, RW])
        g2 = alloc(post, "g2", [P, RW])
        yc = alloc(post, "yc", [P, 2, RW])
        ysq = alloc(post, "ysq", [P, 2, RW])
        yb = alloc(post, "yb", [P, 2, RW])
        zeros = alloc(post, "zeros", [P, D])
        hm = alloc(post, "hm", [P, NT, HEADS])
        hv = alloc(post, "hv", [P, NT, HEADS])
        hs_ = alloc(post, "hs_", [P, NT, HEADS])
        q_ld, q_yc, q_sq, q_v, q_s, q_yb, q_g, q_done, q_dve, q_pool, q_z = (
            sem(f"q_{n}") for n in "ld yc sq v s yb g done dve pool z".split())

        def by_head(ap):
            return ap.rearrange("p (h d) -> p h d", d=HD)

        with nc.Block() as block:
            @block.sync
            def _(sp):
                sp.dma_start(lnw[:, :], A["rwkv_ln_w"][0].partition_broadcast(P)).then_inc(q_ld, 16)
                sp.dma_start(lnb[:, :], A["rwkv_ln_b"][0].partition_broadcast(P)).then_inc(q_ld, 16)
                sp.dma_start(g2[:, :], A["rwkv_g2"][0]).then_inc(q_ld, 16)
                sp.wait_ge(q_ld, 48)

            @block.gpsimd
            def _(pool):
                link = Chain(pool, q_pool)
                link(pool.memset(zeros[:, :], 0.0))
                pool.dma_start(y_dram[E * P:, :].rearrange("(b p) d -> p b d", p=P),
                               zeros[:, :].unsqueeze(1).to_broadcast([P, OVER, D])).then_inc(q_z, 16)
                pool.wait_ge(q_ld, 48)
                for i in range(NT):
                    if i >= 2:
                        pool.wait_ge(q_done, i - 1)
                    link(pool.tensor_tensor(by_head(yb[:, i % 2, :]), by_head(vt[:, i, :]),
                                            bonus[:, i, :].unsqueeze(2).to_broadcast([P, HEADS, HD]), ALU.mult))
                    pool.tensor_tensor(yb[:, i % 2, :], yb[:, i % 2, :], lnb[:, :], ALU.add).then_inc(q_yb, 1)
                pool.wait_ge(q_z, 16)

            @block.scalar
            def _(act):
                for i in range(NT):
                    act.wait_ge(q_yc, i + 1)
                    act.activation(ysq[:, i % 2, :], yc[:, i % 2, :], ACT.Square).then_inc(q_sq, 1)
                    act.wait_ge(q_v, i + 1)
                    act.activation(hs_[:, i, :], hv[:, i, :], ACT.Sqrt).then_inc(q_s, 1)

            @block.vector
            def _(dve):
                link = Chain(dve, q_dve)
                dve.wait_ge(q_ld, 48)
                for i in range(NT):
                    c_ = yc[:, i % 2, :]
                    y4 = y[:, i, :, :].rearrange("p c (b d) -> p c b d", b=2)
                    c4 = c_.rearrange("p (c b d) -> p c b d", b=2, d=HD)
                    m_ = hm[:, i, :].rearrange("p (c b) -> p c b", b=2)
                    link(dve.tensor_reduce(m_, y4, AX, ALU.add))
                    link(dve.tensor_scalar(m_, m_, 1.0 / HD, None, ALU.mult))
                    dve.tensor_tensor(c4, y4, m_.unsqueeze(3).to_broadcast([P, CT, 2, HD]), ALU.subtract)\
                        .then_inc(q_yc, 1)
                    dve.wait_ge(q_sq, i + 1)
                    link(dve.tensor_reduce(hv[:, i, :], by_head(ysq[:, i % 2, :]), AX, ALU.add))
                    dve.tensor_scalar(hv[:, i, :], hv[:, i, :], 1.0 / HD, 64e-5, ALU.mult, ALU.add).then_inc(q_v, 1)
                    dve.wait_ge(q_s, i + 1)
                    link(dve.reciprocal(hs_[:, i, :], hs_[:, i, :]))
                    link(dve.tensor_tensor(by_head(c_), by_head(c_),
                                           hs_[:, i, :].unsqueeze(2).to_broadcast([P, HEADS, HD]), ALU.mult))
                    link(dve.tensor_tensor(c_, c_, lnw[:, :], ALU.mult))
                    dve.wait_ge(q_yb, i + 1)
                    link(dve.tensor_tensor(c_, c_, yb[:, i % 2, :], ALU.add))
                    dve.wait_ge(q_g, i + 1)
                    dve.tensor_tensor(yr[:, i, :], c_, ps[:, i, :], ALU.mult).then_inc(q_done, 1)

            @block.tensor
            def _(pe):
                pe.wait_ge(q_ld, 48)
                for i in range(NT):
                    pe.matmul(ps[:, i, :], zrT[:, 13, P * i:P * i + P], g2[:, :], start=True, stop=True).then_inc(q_g, 1)
        post.close()
        stage3.close()
        end_stage()

        h = alloc(top, "h", [P, NT, D])
        row_y = alloc(top, "row_y", [P, NT, 2], I32)
        wts = alloc(top, "wts", [P, NT, 2])
        slots = alloc(top, "slots", [P, NBLK], I32)
        over = alloc(top, "over", [1, 8], I32)
        stage4 = top.enter_context(ExitStack())
        uT = alloc(stage4, "uT2", [P, KD, T])
        mg = alloc(stage4, "mg", [P, NT, D])
        tmps = alloc(stage4, "tmps", [P, 2, RW])
        yn = mg[:, 0:2, :].rearrange("p b (a n) -> p (b a) n", a=2)
        yrT, ynT = zrT[:, 0:4, :], zrT[:, 4:8, :]
        mgT = zrT[:, 0:8, :]
        grow2 = zrT[:, 8:10, :].rearrange("p a n -> p (a n)")
        u2 = mg[:, 0:2, :]
        m_ld, m_yT, m_yTe, m_zg, m_sig, m_mg, m_mT, m_mTe, m_o, m_h, m_dve, m_h0, m_g = (
            sem(f"m_{n}") for n in "ld yT yTe zg sig mg mT mTe o h dve h0 g".split())
        combos = [(j, i) for j in range(2) for i in range(NT)]
        moe_first = NU

        n_act, n_evac, n_mean, n_dve, n_pe, n_store, n2_ev = norm_mod(stage4, "n2", h, u2, uT, grow2, 3, 4, True)

        with nc.Block() as block:
            @block.sync
            def _(sp):
                sp.dma_start(yn, yn_dram).then_inc(m_ld, 16)
                sp.dma_start(uT[:, :, :], uT_dram).then_inc(m_ld, 16)
                sp.dma_start(h[:, :, :], A["x"][0].rearrange("(i p) d -> p i d", p=P)).then_inc(m_h0, 16)
                load_units(sp, index["p_rwkv"] + R, NU)
                sp.wait_ge(m_ld, 32)
                sp.wait_ge(m_h0, 16)

            @block.scalar
            def _(act):
                for n in range(8):
                    act.wait_ge(m_yT, n + 1)
                    act.activation((yrT, ynT)[n % 2][:, :, P * (n // 2):P * (n // 2) + P],
                                   ps[:, n % 4, :].rearrange("p (j t) -> p j t", j=4), ACT.Copy).then_inc(m_yTe, 1)
                for n in range(8):
                    if n:
                        act.wait_ge(m_mg, n)
                    for b in range(2):
                        act.wait_ge(m_zg, 2 * n + b + 1)
                        act.activation(tmps[:, b, :], ps[:, 4 * (n % 2) + 2 * b, :], ACT.Sigmoid).then_inc(m_sig, 1)
                for n in range(8):
                    act.wait_ge(m_mT, n + 1)
                    act.activation(mgT[:, 4 * (n % 2):4 * (n % 2) + 4, P * (n // 2):P * (n // 2) + P],
                                   ps[:, n % 4, :].rearrange("p (k t) -> p k t", k=4), ACT.Copy).then_inc(m_mTe, 1)
                n_act_wait = NT * 2
                act.wait_ge(m_h, n_act_wait)
                n_act(act)
                n_evac(act)

            @block.vector
            def _(dve):
                link = Chain(dve, m_dve)
                for n, (j, i) in enumerate(combos):
                    cols = slice(512 * j, 512 * j + 512)
                    for b in range(2):
                        dve.wait_ge(m_sig, 2 * n + b + 1)
                        link(dve.tensor_tensor(tmps[:, b, :], tmps[:, b, :], ps[:, 4 * (n % 2) + 2 * b + 1, :],
                                               ALU.mult))
                    dve.tensor_tensor(mg[:, i, cols], tmps[:, 0, :], tmps[:, 1, :], ALU.add).then_inc(m_mg, 1)
                dve.wait_ge(m_h0, 16)
                n = 0
                for i in range(NT):
                    for j in range(2):
                        cols = slice(512 * j, 512 * j + 512)
                        dve.wait_ge(m_o, n + 1)
                        link(dve.tensor_tensor(tmps[:, 0, :], ps[:, 4 + n % 4, :], mod[:, 2, cols], ALU.mult))
                        dve.tensor_tensor(h[:, i, cols], h[:, i, cols], tmps[:, 0, :], ALU.add).then_inc(m_h, 1)
                        dve.wait_ge(m_h, n + 1)
                        n += 1
                n_mean(dve)
                dve.wait_ge(m_g, 16)
                n_dve(dve, link)

            @block.gpsimd
            def _(pool):
                pool.wait_ge(m_yTe, 8)
                pool.dma_start(grow2, A["norm_ffn_g"][0].partition_broadcast(P)).then_inc(m_g, 16)
                n_store(pool)
                pool.wait_ge(m_g, 16)

            @block.tensor
            def _(pe):
                ident = C("ident")
                pe.wait_ge(m_ld, 32)
                for n in range(8):
                    i = n // 2
                    src = (yr, yn)[n % 2][:, i, :].rearrange("t (p j) -> t j p", j=4)
                    if n >= 4:
                        pe.wait_ge(m_yTe, n - 3)
                    for j in range(4):
                        ins = pe.transpose(ps[:, n % 4, P * j:P * j + P], src[:, j, :], ident)
                    ins.then_inc(m_yT, 1)
                pe.wait_ge(m_yTe, 8)
                for name in ("p_rwkv", "p_nsa"):
                    need(pe, name)
                for n, (j, i) in enumerate(combos):
                    cols = slice(512 * j, 512 * j + 512)
                    if n >= 2:
                        pe.wait_ge(m_mg, n - 1)
                    for b in range(2):
                        need(pe, f"zg{b}{j}")
                        w, yT = slot(("p_rwkv", "p_nsa")[b], 4, D), (yrT, ynT)[b]
                        for k in range(4):
                            pe.matmul(ps[:, 4 * (n % 2) + 2 * b + 1, :], yT[:, k, P * i:P * i + P], w[:, k, cols],
                                      start=(k == 0), stop=(k == 3))
                        for k in range(KD):
                            ins = pe.matmul(ps[:, 4 * (n % 2) + 2 * b, :], uT[:, k, P * i:P * i + P],
                                            slot(f"zg{b}{j}", KD, 512)[:, k, :], start=(k == 0), stop=(k == KD - 1))
                        ins.then_inc(m_zg, 1)
                    if i == NT - 1:
                        pe.wait_ge(m_zg, 2 * n + 2)
                        for b in range(2):
                            pe.sem_inc(unit_free[index[f"zg{b}{j}"] % R], 1)
                for name in ("p_rwkv", "p_nsa"):
                    pe.sem_inc(unit_free[index[name] % R], 1)
                for n in range(8):
                    i, b = n // 2, n % 2
                    pe.wait_ge(m_mg, max(7, 5 + i))
                    if n >= 4:
                        pe.wait_ge(m_mTe, n - 3)
                    src = mg[:, i, :].rearrange("t (p k) -> t k p", k=KD)
                    for k in range(4):
                        ins = pe.transpose(ps[:, n % 4, P * k:P * k + P], src[:, 4 * b + k, :], ident)
                    ins.then_inc(m_mT, 1)
                n = 0
                pe.wait_ge(m_mTe, 8)
                pe.wait_ge(m_mg, 8)
                for name in ("wo0", "wo1"):
                    need(pe, name)
                for i in range(NT):
                    for j in range(2):
                        if n >= 4:
                            pe.wait_ge(m_h, n - 3)
                        for k in range(KD):
                            ins = pe.matmul(ps[:, 4 + n % 4, :], mgT[:, k, P * i:P * i + P],
                                            slot(f"wo{k // 4}", 4, D)[:, k % 4, 512 * j:512 * j + 512],
                                            start=(k == 0), stop=(k == KD - 1))
                        ins.then_inc(m_o, 1)
                        n += 1
                pe.wait_ge(m_o, 8)
                for name in ("wo0", "wo1"):
                    pe.sem_inc(unit_free[index[name] % R], 1)
                n_pe(pe)

        scratch = mg[:, :, :].rearrange("p i n -> p (i n)")
        used = [0]

        def rb(name, shape, dt=F32):
            n = int(np.prod(shape[1:]))
            words = n // 2 if dt == BF16 else n
            v = scratch[0:shape[0], used[0]:used[0] + words]
            used[0] += words
            v = v if dt == F32 else v.bitcast(dt)
            axes = "abc"[:len(shape) - 1]
            return v.rearrange(f"p ({' '.join(axes)}) -> p {' '.join(axes)}", **dict(zip(axes, shape[1:])))

        wr = rb("w", [P, KD, NG + E])
        rbias = rb("bias", [P, NG + E])
        lg = rb("lg", [P, NT, NG + E])
        gmax, gsum, gpick, m12, pick, e2, den = (rb(n, [P, NT] if n != "m12" else [P, 2, NT]) for n in
                                                 ("gmax", "gsum", "gpick", "m12", "pick", "e2", "den"))
        ge = rb("ge", [P, NT, NG])
        ml = rb("ml", [P, NT, E])
        t32 = rb("t32", [P, NT, E])
        oh = rb("oh", [P, 2, NT, E])
        ohb = rb("ohb", [P, NT, E], BF16)
        rank = rb("rank", [P, NT, E])
        cnt, nov, ovi, ovs = (rb(n, [P, E]) for n in ("cnt", "nov", "ovi", "ovs"))
        sel = rb("sel", [P, 3, 2, NT])
        kx, mx_, bx, px, rx = (rb(n, [P, 2, NT]) for n in ("kx", "mx", "bx", "px", "rx"))
        place = rb("place", [P, 2, NT], I32)
        tok = rb("tok", [P, NT], I32)
        zero = rb("zero", [P, NBLK], I32)
        in0 = rb("in0", [1, OVER, E])
        in1 = rb("in1", [1, OVER, E])
        ov8 = rb("ov8", [1, 8])
        r_ld, r_lg, r_a, r_b, r_e, r_oh, r_rk, r_dve, r_z, r_zd, r_sc, r_out, r_ov = (
            sem(f"r_{n}") for n in "ld lg a b e oh rk dve z zd sc out ov".split())

        gu = [A[f"moe_w_{n}"][0].rearrange("e (p k) n -> e p k n", k=KD) for n in ("gate", "up")]
        dn = A["moe_w_down"][0].rearrange("e (p j) n -> e p j n", j=4)
        fills = [sum(1 for n in range(NU) if n % R == s_) for s_ in range(R)]

        def place_of(kind, b, it=None):
            if b == 0 and kind != "d":
                pos = "gu".index(kind)
            elif kind == "d":
                pos = 2 + 3 * b + (2 if b < E - 1 else 0)
            else:
                pos = 2 + 3 * (b - 1) + "gu".index(kind)
            before = pos // R
            return (NU + pos) % R, (before if it is None else before + it)

        def expert_slot(s_, k, n):
            return ring[:, s_, :].rearrange("p (k n) -> p k n", k=k)

        def load_expert(eng, kind, b, it=None):
            s_, before = place_of(kind, b, it)
            eng.wait_ge(unit_free[s_], before + fills[s_])
            e_ = b if it is None else 2 * it + b
            src = dn[e_] if kind == "d" else gu["gu".index(kind)][e_]
            eng.dma_start(expert_slot(s_, 4 if kind == "d" else KD, 0), src).then_inc(unit_in[s_], 16)

        def need_expert(eng, kind, b, it=None):
            s_, before = place_of(kind, b, it)
            eng.wait_ge(unit_in[s_], 16 * before + (total[s_] + 16))
            return expert_slot(s_, 4 if kind == "d" else KD, 0)

        with nc.Block() as block:
            @block.sync
            def _(sp):
                sp.dma_start(wr[:, :, 0:NG], A["w_router_grp"][0].rearrange("(p k) n -> p k n", k=KD)).then_inc(r_ld, 16)
                sp.dma_start(wr[:, :, NG:], A["w_router_exp"][0].rearrange("(p k) n -> p k n", k=KD)).then_inc(r_ld, 16)
                sp.dma_start(rbias[:, 0:NG], A["b_router_grp"][0].partition_broadcast(P)).then_inc(r_ld, 16)
                sp.dma_start(rbias[:, NG:], A["b_router_exp"][0].partition_broadcast(P)).then_inc(r_ld, 16)
                sp.wait_ge(r_z, 1)
                sp.dma_start(slots_dram.rearrange("(p b) o -> p (b o)", p=P), zero[:, :]).then_inc(r_zd, 16)
                for kind, b in (("g", 0), ("u", 0), ("g", 1), ("u", 1), ("d", 0), ("g", 2)):
                    load_expert(sp, kind, b)
                sp.wait_ge(r_ld, 64)
                sp.wait_ge(r_zd, 16)

            @block.scalar
            def _(act):
                act.wait_ge(r_a, 1)
                act.activation(ge[:, :, :], ge[:, :, :], ACT.Exp).then_inc(r_e, 1)
                act.wait_ge(r_b, 1)
                act.activation(e2[:, :], e2[:, :], ACT.Exp).then_inc(r_e, 1)

            @block.tensor
            def _(pe):
                pe.wait_ge(r_ld, 64)
                for i in range(NT):
                    for k in range(KD):
                        ins = pe.matmul(ps[:, 0, (NG + E) * i:(NG + E) * (i + 1)], uT[:, k, P * i:P * i + P], wr[:, k, :],
                                        start=(k == 0), stop=(k == KD - 1))
                ins.then_inc(r_lg, 1)
                pe.wait_ge(r_oh, 1)
                for i in range(NT + 1):
                    o = ps[:, 1, E * i:E * i + E]
                    for j in range(i):
                        ins = pe.matmul(o, ones_bf[:, :], ohb[:, j, :], start=(j == 0), stop=(j == i - 1 and i == NT))
                    if i < NT:
                        ins = pe.matmul(o, strict_bf[:, :], ohb[:, i, :], start=(i == 0), stop=True)
                ins.then_inc(r_rk, 1)

            @block.vector
            def _(dve):
                link = Chain(dve, r_dve)
                TT, TS = dve.tensor_tensor, dve.tensor_scalar

                def wide(ap, n):
                    return ap.unsqueeze(2).to_broadcast([P, NT, n])

                def over_tiles(ap, n):
                    return ap.unsqueeze(1).to_broadcast([P, NT, n])

                dve.memset(zero[:, :], 0).then_inc(r_z, 1)
                link(dve.tensor_copy(tok[:, :], C("token")))
                dve.wait_ge(r_lg, 1)
                link(TT(lg[:, :, :], ps[:, 0, 0:NT * (NG + E)].rearrange("p (i n) -> p i n", i=NT),
                        over_tiles(rbias[:, :], NG + E), ALU.add))
                lgg, lge = lg[:, :, 0:NG], lg[:, :, NG:]
                link(dve.tensor_reduce(gmax[:, :], lgg, AX, ALU.max))
                TT(ge[:, :, :], lgg, wide(gmax[:, :], NG), ALU.subtract).then_inc(r_a, 1)
                t4 = t32[:, :, 0:NG]
                link(TT(t4, lgg, wide(gmax[:, :], NG), ALU.is_equal))
                link(TT(t4, t4, over_tiles(C("group_down"), NG), ALU.mult))
                link(dve.tensor_reduce(gpick[:, :], t4, AX, ALU.max))
                link(TT(ml[:, :, :], over_tiles(C("group_down_of"), E), wide(gpick[:, :], E), ALU.is_equal))
                link(TS(ml[:, :, :], ml[:, :, :], -NEG, NEG, ALU.mult, ALU.add))
                link(TT(ml[:, :, :], ml[:, :, :], lge, ALU.add))
                for j in range(2):
                    link(dve.tensor_reduce(m12[:, j, :], ml[:, :, :], AX, ALU.max))
                    link(TT(t32[:, :, :], ml[:, :, :], wide(m12[:, j, :], E), ALU.is_equal))
                    link(TT(t32[:, :, :], t32[:, :, :], over_tiles(C("expert_down"), E), ALU.mult))
                    link(dve.tensor_reduce(pick[:, :], t32[:, :, :], AX, ALU.max))
                    link(TT(oh[:, j, :, :], over_tiles(C("expert_down"), E), wide(pick[:, :], E), ALU.is_equal))
                    if j == 0:
                        link(dve.scalar_tensor_tensor(ml[:, :, :], oh[:, 0, :, :], 3 * NEG, ml[:, :, :], ALU.mult, ALU.add))
                TT(ohb[:, :, :], oh[:, 0, :, :], oh[:, 1, :, :], ALU.add).then_inc(r_oh, 1)
                TT(e2[:, :], m12[:, 1, :], m12[:, 0, :], ALU.subtract).then_inc(r_b, 1)
                dve.wait_ge(r_e, 2)
                link(dve.tensor_reduce(gsum[:, :], ge[:, :, :], AX, ALU.add))
                link(TS(den[:, :], e2[:, :], 1.0, None, ALU.add))
                link(TT(den[:, :], den[:, :], gsum[:, :], ALU.mult))
                link(dve.reciprocal(wts[:, :, 0], den[:, :]))
                link(TT(wts[:, :, 1], wts[:, :, 0], e2[:, :], ALU.mult))
                dve.wait_ge(r_rk, 1)
                link(dve.tensor_copy(rank[:, :, :], ps[:, 1, 0:NT * E].rearrange("p (i n) -> p i n", i=NT)))
                link(dve.tensor_copy(cnt[:, :], ps[:, 1, NT * E:NT * E + E]))
                link(TS(nov[:, :], cnt[:, :], float(P), None, ALU.is_gt))
                for m in (2, 3):
                    link(dve.scalar_tensor_tensor(nov[:, :], cnt[:, :], float(m * P), nov[:, :], ALU.is_gt, ALU.add))
                link(dve.tensor_tensor_scan(ovi[:, :], C("ones")[:, 0:E], nov[:, :], 0.0, ALU.mult, ALU.add))
                link(TT(ovs[:, :], ovi[:, :], nov[:, :], ALU.subtract))
                for m, src in enumerate((rank[:, :, :], over_tiles(C("expert"), E), over_tiles(ovs[:, :], E))):
                    for j in range(2):
                        link(TT(t32[:, :, :], oh[:, j, :, :], src, ALU.mult))
                        link(dve.tensor_reduce(sel[:, m, j, :], t32[:, :, :], AX, ALU.add))
                r_, e_, s_ = (sel[:, m, :, :] for m in range(3))
                K_, M_, B_, X_, R_ = (v[:, :, :] for v in (kx, mx_, bx, px, rx))
                link(TS(M_, r_, float(P), None, ALU.is_ge))
                link(dve.scalar_tensor_tensor(K_, r_, 2.0 * P, M_, ALU.is_ge, ALU.add))
                link(dve.scalar_tensor_tensor(K_, r_, 3.0 * P, K_, ALU.is_ge, ALU.add))
                link(dve.scalar_tensor_tensor(X_, K_, -float(P), r_, ALU.mult, ALU.add))
                link(TT(B_, s_, K_, ALU.add))
                link(dve.scalar_tensor_tensor(B_, B_, E - 1.0, e_, ALU.add, ALU.subtract))
                link(TT(B_, B_, M_, ALU.mult))
                link(TT(B_, B_, e_, ALU.add))
                link(dve.scalar_tensor_tensor(R_, B_, float(P), X_, ALU.mult, ALU.add))
                link(dve.tensor_copy(row_y[:, :, :].rearrange("p i j -> p j i"), R_))
                link(dve.scalar_tensor_tensor(R_, X_, float(NBLK), B_, ALU.mult, ALU.add))
                dve.tensor_copy(place[:, :, :], R_).then_inc(r_sc, 1)
                for v in range(OVER):
                    link(TS(in0[:, v, :], ovs[0:1, :], float(v), None, ALU.is_le))
                    link(TS(in1[:, v, :], ovi[0:1, :], float(v), None, ALU.is_gt))
                link(TT(in0[:, :, :], in0[:, :, :], in1[:, :, :], ALU.mult))
                link(TT(in0[:, :, :], in0[:, :, :], C("expert")[0:1, :].unsqueeze(1).to_broadcast([1, OVER, E]), ALU.mult))
                link(dve.tensor_reduce(ov8[:, 0:OVER], in0[:, :, :], AX, ALU.add))
                link(dve.tensor_copy(ov8[:, OVER:8], ovi[0:1, E - 1:E]))
                dve.tensor_copy(over[:, :], ov8[:, :]).then_inc(r_ov, 1)

            @block.gpsimd
            def _(pool):
                pool.wait_ge(r_sc, 1)
                pool.wait_ge(r_zd, 16)
                n = 0
                for j in range(2):
                    for i in range(NT):
                        pool.indirect_dma_start(slots_dram, bass.IndirectOffsetOnAxis(ap=place[:, j, i:i + 1], axis=0),
                                                tok[:, i:i + 1], None).then_inc(r_out, 16)
                        n += 16
                        pool.wait_ge(r_out, n)
                pool.dma_start(slots[:, :], slots_dram.rearrange("(p b) o -> p (b o)", p=P)).then_inc(r_out, 16)
                pool.wait_ge(r_out, 16 + n)
        stage4.close()

        moe = top.enter_context(ExitStack())
        xg = alloc(moe, "xg", [P, 2, D])
        xgT = alloc(moe, "xgT", [P, 2, KD, P])
        act_g = alloc(moe, "act_g", [P, EH])
        hd = alloc(moe, "hd", [P, EH])
        hdT = alloc(moe, "hdT", [P, 4, P])
        yo = alloc(moe, "yo", [P, 2, D])
        idx = alloc(moe, "idx", [P, 2], I32)
        x_in = [sem(f"x_in{q_}") for q_ in range(2)]
        y_st = [sem(f"y_st{q_}") for q_ in range(2)]
        e_idx, e_xT, e_xe, e_g, e_sl, e_u, e_hd, e_hT, e_he, e_d, e_ya, e_yd, e_seen = (
            sem(f"e_{n}") for n in "idx xT xe g sl u hd hT he d ya yd seen".split())
        LOOPS = (E - 2) // 2

        def wait(eng, s_, v):
            if not isinstance(v, int) or v > 0:
                eng.wait_ge(s_, v)

        def turn(it, b):
            return b if it is None else 2 * it + b

        def pairs(eng, pair):
            pair(None, 0)
            with eng.Fori(1, LOOPS) as it:
                pair(it, it)

        with nc.Block() as block:
            @block.sync
            def _(sp):
                load_expert(sp, "u", 2)
                load_expert(sp, "d", 1)
                with sp.Fori(0, LOOPS - 1) as it:
                    for b in (3, 4):
                        for kind in "gud":
                            load_expert(sp, kind, b - (kind == "d"), it)
                for kind, b in (("g", E - 1), ("u", E - 1), ("d", E - 2), ("d", E - 1)):
                    load_expert(sp, kind, b)

            @block.gpsimd
            def _(pool):
                def gather(b, it=None):
                    q_, n = b % 2, turn(it, b)
                    wait(pool, e_xT, n - 1)
                    pool.tensor_copy(idx[:, q_:q_ + 1], slots[:, bass.ds(n, 1)]).then_inc(e_idx, 1)
                    pool.wait_ge(e_idx, n + 1)
                    pool.sem_inc(e_seen, 1)
                    pool.indirect_dma_start(xg[:, q_, :], None, u2_dram,
                                            bass.IndirectOffsetOnAxis(ap=idx[:, q_:q_ + 1], axis=0))\
                        .then_inc(x_in[q_], 16)

                def store(b, it=None):
                    n = turn(it, b)
                    pool.wait_ge(e_ya, n + 1)
                    pool.wait_ge(e_yd, n + 1)
                    pool.dma_start(y_dram.rearrange("(b p) d -> b p d", p=P)[n], yo[:, b % 2, :]).then_inc(y_st[b % 2], 16)

                gather(0)
                gather(1)

                def pair(it, half):
                    for b in range(2):
                        gather(b + 2, it)
                        store(b, it)

                pairs(pool, pair)
                for b in (E - 2, E - 1):
                    store(b)
                for q_ in range(2):
                    pool.wait_ge(y_st[q_], 16 * (E // 2))

            @block.scalar
            def _(act):
                def silu(b, it=None):
                    n = turn(it, b)
                    act.wait_ge(e_g, n + 1)
                    wait(act, e_hd, n)
                    act.sem_inc(unit_free[place_of("g", b)[0]], 1)
                    act.activation(act_g[:, :], ps[:, 0, :], ACT.Silu).then_inc(e_sl, 1)

                def finish(b, half, it=None):
                    n = turn(it, b)
                    act.wait_ge(e_hT, n + 1)
                    wait(act, e_d, n)
                    act.activation(hdT[:, :, :], ps[:, 6, :].rearrange("p (j t) -> p j t", j=4), ACT.Copy).then_inc(e_he, 1)
                    act.wait_ge(e_d, n + 1)
                    wait(act, y_st[b % 2], 16 * half)
                    act.activation(yo[:, b % 2, 0:512], ps[:, 2, :], ACT.Copy).then_inc(e_ya, 1)

                silu(0)

                def pair(it, half):
                    silu(1, it)
                    finish(0, half, it)
                    silu(2, it)
                    finish(1, half, it)

                pairs(act, pair)
                silu(E - 1)
                finish(E - 2, LOOPS)
                finish(E - 1, LOOPS)

            @block.vector
            def _(dve):
                def tokens(b, it=None):
                    dve.wait_ge(e_xT, turn(it, b) + 1)
                    dve.tensor_copy(xgT[:, b % 2, :, :], ps[:, 4:6, :].rearrange("p b (k t) -> p (b k) t", k=4))\
                        .then_inc(e_xe, 1)

                def gated(b, it=None):
                    n = turn(it, b)
                    dve.wait_ge(e_u, n + 1)
                    dve.sem_inc(unit_free[place_of("u", b)[0]], 1)
                    dve.wait_ge(e_sl, n + 1)
                    wait(dve, e_hT, n)
                    dve.tensor_tensor(hd[:, :], act_g[:, :], ps[:, 1, :], ALU.mult).then_inc(e_hd, 1)

                def finish(b, half, it=None):
                    n = turn(it, b)
                    dve.wait_ge(e_d, n + 1)
                    dve.sem_inc(unit_free[place_of("d", b)[0]], 1)
                    wait(dve, y_st[b % 2], 16 * half)
                    dve.tensor_copy(yo[:, b % 2, 512:D], ps[:, 3, :]).then_inc(e_yd, 1)

                tokens(0)
                gated(0)
                tokens(1)

                def pair(it, half):
                    gated(1, it)
                    finish(0, half, it)
                    tokens(2, it)
                    gated(2, it)
                    finish(1, half, it)
                    tokens(3, it)

                pairs(dve, pair)
                gated(E - 1)
                finish(E - 2, LOOPS)
                finish(E - 1, LOOPS)

            @block.tensor
            def _(pe):
                ident = C("ident")

                def tokens(b, half, it=None):
                    n = turn(it, b)
                    pe.wait_ge(x_in[b % 2], 16 * half + 16)
                    wait(pe, e_xe, n)
                    src = xg[:, b % 2, :].rearrange("t (p k) -> t k p", k=KD)
                    for k in range(KD):
                        ins = pe.transpose(ps[:, 4 + k // 4, P * (k % 4):P * (k % 4) + P], src[:, k, :], ident)
                    ins.then_inc(e_xT, 1)

                def product(kind, b, it=None):
                    n = turn(it, b)
                    w = need_expert(pe, kind, b, it)
                    if kind == "g":
                        pe.wait_ge(e_xe, n + 1)
                        wait(pe, e_sl, n)
                    else:
                        wait(pe, e_hd, n)
                    for k in range(KD):
                        ins = pe.matmul(ps[:, "gu".index(kind), :], xgT[:, b % 2, k, :], w[:, k, :], start=(k == 0),
                                        stop=(k == KD - 1))
                    ins.then_inc(e_g if kind == "g" else e_u, 1)

                def hidden(b, it=None):
                    n = turn(it, b)
                    pe.wait_ge(e_hd, n + 1)
                    wait(pe, e_he, n)
                    src = hd[:, :].rearrange("t (p j) -> t j p", j=4)
                    for j in range(4):
                        ins = pe.transpose(ps[:, 6, P * j:P * j + P], src[:, j, :], ident)
                    ins.then_inc(e_hT, 1)

                def down(b, it=None):
                    n = turn(it, b)
                    w = need_expert(pe, "d", b, it)
                    pe.wait_ge(e_he, n + 1)
                    wait(pe, e_ya, n)
                    wait(pe, e_yd, n)
                    for c in range(2):
                        for j in range(4):
                            ins = pe.matmul(ps[:, 2 + c, :], hdT[:, j, :], w[:, j, 512 * c:512 * c + 512],
                                            start=(j == 0), stop=(j == 3))
                    ins.then_inc(e_d, 1)

                tokens(0, 0)
                product("g", 0)
                product("u", 0)
                tokens(1, 0)

                def pair(it, half):
                    for b in (1, 2):
                        product("g", b, it)
                        hidden(b - 1, it)
                        product("u", b, it)
                        down(b - 1, it)
                        tokens(b + 1, half + 1, it)

                pairs(pe, pair)
                product("g", E - 1)
                hidden(E - 2)
                product("u", E - 1)
                down(E - 2)
                hidden(E - 1)
                down(E - 1)

        v_ld, v_idx, v_x, v_xT, v_xe, v_g, v_sl, v_hd, v_hT, v_he, v_d, v_y, v_st, v_seen = (
            sem(f"v_{n}") for n in "ld idx x xT xe g sl hd hT he d y st seen".split())

        def further(eng, body):
            n_over = eng.value_load(over[0:1, OVER:8], min_val=0, max_val=OVER)
            with eng.Fori(0, OVER) as v:
                with eng.If(n_over > v):
                    body(v)

        with nc.Block() as block:
            @block.sync
            def _(sp):
                def body(v):
                    e_ = sp.value_load(over[0:1, bass.ds(v, 1)], min_val=0, max_val=E - 1)
                    for m in range(2):
                        sp.dma_start(expert_slot(m, KD, 0), gu[m][e_]).then_inc(v_ld, 16)
                    sp.dma_start(expert_slot(2, 4, 0), dn[e_]).then_inc(v_ld, 16)
                    sp.wait_ge(v_y, 2 * v + 2)
                    sp.dma_start(y_dram.rearrange("(b p) d -> b p d", p=P)[v + E], yo[:, 0, :]).then_inc(v_st, 16)
                    sp.wait_ge(v_st, 16 * v + 16)
                    sp.sem_inc(v_seen, 1)
                further(sp, body)

            @block.gpsimd
            def _(pool):
                def body(v):
                    pool.tensor_copy(idx[:, 0:1], slots[:, bass.ds(v + E, 1)]).then_inc(v_idx, 1)
                    pool.wait_ge(v_idx, v + 1)
                    pool.sem_inc(v_seen, 1)
                    pool.indirect_dma_start(xg[:, 0, :], None, u2_dram,
                                            bass.IndirectOffsetOnAxis(ap=idx[:, 0:1], axis=0)).then_inc(v_x, 16)
                    pool.wait_ge(v_xT, v + 1)
                    pool.sem_inc(v_seen, 1)
                further(pool, body)

            @block.scalar
            def _(act):
                def body(v):
                    act.wait_ge(v_g, v + 1)
                    act.activation(act_g[:, :], ps[:, 0, :], ACT.Silu).then_inc(v_sl, 1)
                    act.wait_ge(v_d, v + 1)
                    act.activation(yo[:, 0, 0:512], ps[:, 2, :], ACT.Copy).then_inc(v_y, 1)
                further(act, body)

            @block.vector
            def _(dve):
                def body(v):
                    dve.wait_ge(v_xT, v + 1)
                    dve.tensor_copy(xgT[:, 0, :, :], ps[:, 4:6, :].rearrange("p b (k t) -> p (b k) t", k=4)).then_inc(v_xe, 1)
                    dve.wait_ge(v_sl, v + 1)
                    dve.tensor_tensor(hd[:, :], act_g[:, :], ps[:, 1, :], ALU.mult).then_inc(v_hd, 1)
                    dve.wait_ge(v_hT, v + 1)
                    dve.tensor_copy(hdT[:, :, :], ps[:, 6, :].rearrange("p (j t) -> p j t", j=4)).then_inc(v_he, 1)
                    dve.wait_ge(v_d, v + 1)
                    dve.tensor_copy(yo[:, 0, 512:D], ps[:, 3, :]).then_inc(v_y, 1)
                further(dve, body)

            @block.tensor
            def _(pe):
                ident = C("ident")

                def body(v):
                    pe.wait_ge(v_x, 16 * v + 16)
                    src = xg[:, 0, :].rearrange("t (p k) -> t k p", k=KD)
                    for k in range(KD):
                        ins = pe.transpose(ps[:, 4 + k // 4, P * (k % 4):P * (k % 4) + P], src[:, k, :], ident)
                    ins.then_inc(v_xT, 1)
                    pe.wait_ge(v_xe, v + 1)
                    pe.wait_ge(v_ld, 48 * v + 48)
                    for m in range(2):
                        for k in range(KD):
                            ins = pe.matmul(ps[:, m, :], xgT[:, 0, k, :], expert_slot(m, KD, 0)[:, k, :], start=(k == 0),
                                            stop=(k == KD - 1))
                    ins.then_inc(v_g, 1)
                    pe.wait_ge(v_hd, v + 1)
                    src = hd[:, :].rearrange("t (p j) -> t j p", j=4)
                    for j in range(4):
                        ins = pe.transpose(ps[:, 6, P * j:P * j + P], src[:, j, :], ident)
                    ins.then_inc(v_hT, 1)
                    pe.wait_ge(v_he, v + 1)
                    for c in range(2):
                        for j in range(4):
                            ins = pe.matmul(ps[:, 2 + c, :], hdT[:, j, :], expert_slot(2, 4, 0)[:, j, 512 * c:512 * c + 512],
                                            start=(j == 0), stop=(j == 3))
                    ins.then_inc(v_d, 1)
                further(pe, body)
        moe.close()

        last = top.enter_context(ExitStack())
        ya = alloc(last, "ya", [P, NT, 2, D])
        gf = alloc(last, "gf", [P, D])
        fss, fms, frt = (alloc(last, f"f{n}", [P, NT]) for n in ("ss", "ms", "rt"))
        fidx = alloc(last, "fidx", [P, 2 * NT], I32)
        f_in = [sem(f"f_in{n}") for n in range(2 * NT)]
        f_ld, f_idx, f_h, f_sq, f_ms, f_rt, f_o, f_out, f_dve = (sem(f"f_{n}") for n in "ld idx h sq ms rt o out dve".split())
        out_t = out[0].rearrange("(i p) d -> i p d", p=P)

        with nc.Block() as block:
            @block.gpsimd
            def _(pool):
                pool.tensor_copy(fidx[:, :], row_y[:, :, :].rearrange("p i j -> p (i j)")).then_inc(f_idx, 1)
                pool.wait_ge(f_idx, 1)
                for i in range(NT):
                    for j in range(2):
                        n = 2 * i + j
                        pool.indirect_dma_start(ya[:, i, j, :], None, y_dram,
                                                bass.IndirectOffsetOnAxis(ap=fidx[:, n:n + 1], axis=0))\
                            .then_inc(f_in[n], 16)
                for n in range(2 * NT):
                    pool.wait_ge(f_in[n], 16)

            @block.sync
            def _(sp):
                sp.dma_start(gf[:, :], A["norm_final_g"].partition_broadcast(P)).then_inc(f_ld, 16)
                for i in range(NT):
                    sp.wait_ge(f_o, i + 1)
                    sp.dma_start(out_t[i], ya[:, i, 0, :]).then_inc(f_out, 16)
                sp.wait_ge(f_ld, 16)
                sp.wait_ge(f_out, 16 * NT)

            @block.scalar
            def _(act):
                junk = ps[:, 0:2, :].rearrange("p b n -> p (b n)")
                for i in range(NT):
                    act.wait_ge(f_h, i + 1)
                    if i:
                        act.wait_ge(f_sq, i)
                    act.activation(junk, h[:, i, :], ACT.Square, accum_out=fss[:, i:i + 1]).then_inc(f_sq, 1)
                    act.wait_ge(f_ms, i + 1)
                    act.activation(frt[:, i:i + 1], fms[:, i:i + 1], ACT.Sqrt).then_inc(f_rt, 1)

            @block.vector
            def _(dve):
                link = Chain(dve, f_dve)
                dve.wait_ge(f_ld, 16)

                def normed(i):
                    dve.wait_ge(f_rt, i + 1)
                    link(dve.reciprocal(frt[:, i:i + 1], frt[:, i:i + 1]))
                    dve.scalar_tensor_tensor(ya[:, i, 0, :], h[:, i, :], frt[:, i:i + 1], gf[:, :], ALU.mult, ALU.mult)\
                        .then_inc(f_o, 1)

                for i in range(NT):
                    a_, b_ = ya[:, i, 0, :], ya[:, i, 1, :]
                    dve.wait_ge(f_in[2 * i], 16)
                    link(dve.tensor_scalar(a_, a_, wts[:, i, 0:1], None, ALU.mult))
                    dve.wait_ge(f_in[2 * i + 1], 16)
                    link(dve.scalar_tensor_tensor(a_, b_, wts[:, i, 1:2], a_, ALU.mult, ALU.add))
                    link(dve.tensor_tensor(a_, a_, mod[:, 5, :], ALU.mult))
                    dve.tensor_tensor(h[:, i, :], h[:, i, :], a_, ALU.add).then_inc(f_h, 1)
                    dve.wait_ge(f_sq, i + 1)
                    dve.tensor_scalar(fms[:, i:i + 1], fss[:, i:i + 1], 1.0 / D, 1e-6, ALU.mult, ALU.add).then_inc(f_ms, 1)
                    normed(i)


_INS = ['x', 'c', 'w_ada', 'b_ada', 'norm_mix_g', 'w_in', 'rwkv_mu', 'rwkv_w0', 'rwkv_w2', 'rwkv_a0', 'rwkv_a2',
        'rwkv_g2', 'rwkv_kk', 'rwkv_ka', 'rwkv_rk', 'rwkv_ln_w', 'rwkv_ln_b', 'cmp_pe_k', 'cmp_w1_k', 'cmp_w2_k',
        'cmp_pe_v', 'cmp_w1_v', 'cmp_w2_v', 'p_rwkv', 'p_nsa', 'w_out', 'norm_ffn_g', 'w_router_grp',
        'b_router_grp', 'w_router_exp', 'b_router_exp', 'moe_w_gate', 'moe_w_up', 'moe_w_down', 'norm_final_g']


def kernel(**inputs):
    import numpy as _np
    import concourse.bacc as _bacc
    from concourse import mybir as _mybir
    from concourse.bass_utils import run_bass_kernel_spmd as _run

    nc = _bacc.Bacc("TRN2", target_bir_lowering=False, num_devices=1)
    arrays, aps = {}, {}
    for name in _INS:
        a = _np.ascontiguousarray(inputs[name])
        arrays[f"in_{name}_dram"] = a
        aps[name] = nc.dram_tensor(f"in_{name}_dram", a.shape, _mybir.dt.from_np(a.dtype), kind="ExternalInput").ap()
    table = constants()[0]
    arrays["consts_dram"] = table
    aps["consts"] = nc.dram_tensor("consts_dram", table.shape, _mybir.dt.float32, kind="ExternalInput").ap()
    out = nc.dram_tensor("out_0_dram", (1, T, D), _mybir.dt.float32, kind="ExternalOutput").ap()
    build(nc, aps, out)
    r = _run(nc, [arrays], core_ids=[0])
    return r.results[0]["out_0_dram"]
```

```python
from contextlib import ExitStack

import numpy as np

import concourse.bass as bass
from concourse import mybir

P = 128
D = 1024
T = 512
NT = T // P
KD = D // P
RW = 512
HEADS = 8
HD = 64
CT = RW // P
RW_COLS = 3 * RW + 64 + 64 + 128
ZT_TILES = RW_COLS // P
NSA0 = RW_COLS
GATE0 = NSA0 + 512 + 6 * 128 + 24
IN_COLS = GATE0 + 2 * D
NCMP = 31
E = 32
EG = 8
NG = 4
EH = 512
OVER = 7
NBLK = E + OVER
R = 6
SLOT = 4096
NEG = -1e30

F32 = mybir.dt.float32
BF16 = mybir.dt.bfloat16
I32 = mybir.dt.int32
U32 = mybir.dt.uint32
ALU = mybir.AluOpType
ACT = mybir.ActivationFunctionType
AX = mybir.AxisListType.X


def constants():
    f = np.float32
    i = np.arange(P)
    parts = {}
    parts["ident"] = np.eye(P)
    strict = (i[:, None] < i[None, :])
    parts["strict"] = strict
    parts["incl"] = (i[:, None] <= i[None, :])
    for n in range(7):
        m = 1 << n
        same = (i[:, None] // (2 * m)) == (i[None, :] // (2 * m))
        parts[f"lvl{n}"] = same & (i[:, None] % (2 * m) < m) & (i[None, :] % (2 * m) >= m)
    head_of = np.arange(RW) // HD
    parts["headsums"] = (head_of.reshape(CT, P).T[:, :, None] == np.arange(HEADS)).reshape(P, CT * HEADS)
    parts["headspread"] = (i[:, None] == head_of[None, :])
    parts["headsel"] = (i[:, None] // HD == np.arange(2)[None, :])
    parts["causal"] = np.where(i[None, :] <= i[:, None], 0.0, NEG)
    parts["ones"] = np.ones((P, P))
    half = HD // 2
    inv = np.exp(f(-np.log(10000.0)) * np.arange(half, dtype=f) / f(half)).astype(f)
    ang = (np.arange(T, dtype=f)[:, None] * inv[None, :]).astype(f)
    cos, sin = np.cos(ang).astype(f), np.sin(ang).astype(f)
    tile = lambda a: a.reshape(NT, P, -1).transpose(1, 0, 2).reshape(P, -1)
    parts["cos"], parts["sin"] = tile(cos), tile(sin)
    end = np.arange(NCMP) * 16 + 31
    cc, cs = np.zeros((P, half), f), np.zeros((P, half), f)
    cc[:NCMP], cs[:NCMP] = cos[end], sin[end]
    parts["ccos"], parts["csin"] = cc, cs
    seen = end[None, :] <= np.arange(T)[:, None]
    parts["cmask"] = tile(np.where(seen, 0.0, NEG))
    parts["cseen"] = tile(seen.astype(f))
    parts["expert"] = np.broadcast_to(np.arange(E), (P, E))
    parts["expert_down"] = np.broadcast_to(E - np.arange(E), (P, E))
    parts["group_down"] = np.broadcast_to(NG - np.arange(NG), (P, NG))
    parts["group_down_of"] = np.broadcast_to(NG - np.arange(E) // EG, (P, E))
    parts["iota"] = np.broadcast_to(i, (P, P))
    parts["token"] = i[:, None] + P * np.arange(NT)[None, :]
    late = lambda k: 3 if k == "iota" else 2 if k == "headspread" else 1 if k.startswith("lvl") or k in ("headsums", "headsel") else 0
    at, cols, n, common = {}, [], 0, 0
    for k in sorted(parts, key=late):
        at[k] = (n, n + parts[k].shape[1])
        n += parts[k].shape[1]
        common = common if late(k) else n
        cols.append(parts[k].astype(f))
    return np.concatenate(cols, 1), at, common


def stream_units(A):
    ada = A["w_ada"][0].rearrange("(p k) n -> p k n", k=KD)
    win = A["w_in"][0].rearrange("(p k) n -> p k n", k=KD)
    units = []

    def ada_unit(u):
        units.append((f"ada{u}", [(0, P, (KD, 512), ada[:, :, 512 * u:512 * u + 512])]))

    def win_unit(name, c0, n):
        units.append((name, [(0, P, (KD, n), win[:, :, c0:c0 + n])]))

    for u in range(4):
        ada_unit(u)
    win_unit("zr0", 0, 512)
    win_unit("zr1", 512, 512)
    ada_unit(4)
    win_unit("zr2", 1024, 512)
    ada_unit(5)
    win_unit("zr3", 1536, 256)
    ada_unit(6)
    win_unit("q", NSA0, 512)
    ada_unit(7)
    win_unit("kcvc", NSA0 + 512, 256)
    ada_unit(8)
    win_unit("kv", NSA0 + 768, 512)
    for u in (9, 10, 11):
        ada_unit(u)
    for name in ("k", "v"):
        units.append((f"w1{name}", [(0, P, (16, 256), A[f"cmp_w1_{name}"][0].rearrange("(l q) f -> q l f", q=P))]))
    for j in range(2):
        for b in range(2):
            win_unit(f"zg{b}{j}", GATE0 + D * b + 512 * j, 512)
        if j == 0:
            for name in ("p_rwkv", "p_nsa"):
                units.append((name, [(0, P, (4, D), A[name][0].rearrange("(p j) n -> p j n", j=4))]))
    wo = A["w_out"][0].rearrange("(p k) n -> p k n", k=KD)
    for h in range(2):
        units.append((f"wo{h}", [(0, P, (4, D), wo[:, 4 * h:4 * h + 4, :])]))
    return units


def build(nc, A, out):
    consts_np, at, NC = constants()
    units = stream_units(A)
    index = {name: n for n, (name, _) in enumerate(units)}
    NU = len(units)
    total, arrived = [0] * R, []
    for n, (_, parts) in enumerate(units):
        total[n % R] += 16 * len(parts)
        arrived.append(total[n % R])

    with ExitStack() as top:
        stage_sems = []

        def sem(name):
            stage_sems.append(nc.alloc_semaphore(name))
            return stage_sems[-1]

        def end_stage():
            nc.clear_and_free_semaphores(stage_sems)
            nc.all_engine_barrier()
            stage_sems.clear()

        def alloc(ctx, name, shape, dt=F32):
            return ctx.enter_context(nc.sbuf_tensor(name, shape, dt))

        def sb(name, shape, dt=F32):
            return alloc(top, name, shape, dt)

        ring = sb("ring", [P, R, SLOT])
        cst = sb("cst", [P, NC])
        ones_bf = sb("ones_bf", [P, P], BF16)
        strict_bf = sb("strict_bf", [P, P], BF16)
        mod = sb("mod", [P, 6, D])
        ps = top.enter_context(nc.psum_tensor("ps", [P, 8, 512], F32))
        uT_dram = nc.dram_tensor("uT_dram", [P, KD, T], F32).ap()
        yn_dram = nc.dram_tensor("yn_dram", [P, NT, RW], F32).ap()
        u2_dram = nc.dram_tensor("u2_dram", [T, D], F32).ap()
        y_dram = nc.dram_tensor("y_dram", [NBLK * P, D], F32).ap()

        def C(name):
            a, b = at[name]
            return cst[:, a:b]

        unit_in = [nc.alloc_semaphore(f"unit_in{s}") for s in range(R)]
        unit_free = [nc.alloc_semaphore(f"unit_free{s}") for s in range(R)]
        s_const = sem("s_const")
        s_spill = sem("s_spill")

        def slot(name, k, n):
            return ring[:, index[name] % R, 0:k * n].rearrange("p (k n) -> p k n", k=k)

        def need(eng, name):
            n = index[name]
            eng.wait_ge(unit_in[n % R], arrived[n])

        def give_back(ins, name):
            ins.then_inc(unit_free[index[name] % R], 1)

        def load_units(eng, first, last):
            for n in range(first, last):
                if n >= R:
                    eng.wait_ge(unit_free[n % R], n // R)
                for p0, np_, (k, w), src in units[n][1]:
                    eng.dma_start(ring[p0:p0 + np_, n % R, 0:k * w].rearrange("p (k n) -> p k n", k=k), src)\
                       .then_inc(unit_in[n % R], 16)

        def warm(pe, n=8):
            for _ in range(n):
                pe.matmul(ps[:, 7, :], C("ident"), cst[:, 0:T], start=True, stop=True)

        class Chain:

            def __init__(self, eng, s):
                self.eng, self.s, self.n = eng, s, 0

            def __call__(self, ins):
                self.n += 1
                ins.then_inc(self.s, 1)
                self.eng.wait_ge(self.s, self.n)

        def norm_mod(ctx, tag, src, u, uT, g_row, junk, shift, scale, keep_rows):
            s_sq, s_sc, s_rt, s_u, s_uT, s_ev, s_row = (sem(f"{tag}_{x}") for x in
                                                      ("sq", "sc", "rt", "u", "uT", "ev", "row"))
            gs = g_row
            ss = alloc(ctx, f"{tag}_ss", [P, NT])
            ms = alloc(ctx, f"{tag}_ms", [P, NT])
            rt = alloc(ctx, f"{tag}_rt", [P, NT])
            rs = alloc(ctx, f"{tag}_rs", [P, NT])

            def square(eng, i):
                if i:
                    eng.wait_ge(s_sq, i)
                eng.activation(junk, src[:, i, :], ACT.Square, accum_out=ss[:, i:i + 1]).then_inc(s_sq, 1)

            def mean(eng, a, b):
                eng.wait_ge(s_sq, b)
                eng.tensor_scalar(ms[:, a:b], ss[:, a:b], 1.0 / D, 1e-6, ALU.mult, ALU.add).then_inc(s_sc, b - a)

            def root(eng, a, b):
                eng.wait_ge(s_sc, b)
                eng.activation(rt[:, a:b], ms[:, a:b], ACT.Sqrt).then_inc(s_rt, b - a)

            def gain(eng, link):
                link(eng.scalar_tensor_tensor(gs[:, :], mod[:, scale, :], 1.0, gs[:, :], ALU.add, ALU.mult))

            def rows(eng, link, i):
                eng.wait_ge(s_rt, i + 1)
                link(eng.reciprocal(rs[:, i:i + 1], rt[:, i:i + 1]))
                if i >= 2:
                    eng.wait_ge(s_uT, 2 * (i - 1))
                    if keep_rows:
                        eng.wait_ge(s_row, 16 * (i - 1))
                link(eng.scalar_tensor_tensor(u[:, i % 2, :], src[:, i, :], rs[:, i:i + 1], gs[:, :],
                                              ALU.mult, ALU.mult))
                eng.tensor_tensor(u[:, i % 2, :], u[:, i % 2, :], mod[:, shift, :], ALU.add).then_inc(s_u, 1)

            def turned(eng, i):
                eng.wait_ge(s_u, i + 1)
                uv = u[:, i % 2, :].rearrange("t (p k) -> t k p", k=KD)
                for b in range(2):
                    n = 2 * i + b
                    if n >= 4:
                        eng.wait_ge(s_ev, n - 3)
                    for k in range(4):
                        ins = eng.transpose(ps[:, n % 4, P * k:P * k + P], uv[:, 4 * b + k, :], C("ident"))
                    ins.then_inc(s_uT, 1)

            def evacuate(eng, i):
                for b in range(2):
                    eng.wait_ge(s_uT, 2 * i + b + 1)
                    eng.activation(uT[:, 4 * b:4 * b + 4, P * i:P * i + P],
                                   ps[:, (2 * i + b) % 4, :].rearrange("p (k t) -> p k t", k=4),
                                   ACT.Copy).then_inc(s_ev, 1)

            def store(eng):
                for i in range(NT):
                    eng.wait_ge(s_u, i + 1)
                    eng.dma_start(u2_dram[P * i:P * i + P, :], u[:, i % 2, :]).then_inc(s_row, 16)
                    eng.wait_ge(s_row, 16 * (i + 1))

            return square, mean, root, gain, rows, turned, evacuate, store, s_ev

        mixers = top.enter_context(ExitStack())
        attn = top.enter_context(ExitStack())
        zrT = alloc(mixers, "zrT", [P, ZT_TILES, T])
        par = alloc(mixers, "par", [P, 34])
        x = zrT[:, 0:8, :].rearrange("p (i a) n -> p i (a n)", a=2)
        kcvc = alloc(attn, "kcvc", [P, 2, T])
        q = alloc(attn, "q", [P, NT, 512])
        kv = alloc(attn, "kv", [P, NT, 512])
        glog = alloc(attn, "glog", [P, NT, 24])
        stage1 = top.enter_context(ExitStack())
        crow = alloc(stage1, "crow", [P, KD])
        csil = alloc(stage1, "csil", [P, KD])
        csig = alloc(stage1, "csig", [P, KD])
        bada = alloc(stage1, "bada", [12, 512])
        uT = alloc(stage1, "uT", [P, KD, T])
        acc = alloc(stage1, "acc", [P, 2, 512])
        parr = alloc(stage1, "parr", [34, P])
        wgl = alloc(stage1, "wgl", [P, KD, 24])
        misc = alloc(stage1, "misc", [P, 3 * T + 2])
        grow = misc[:, 0:D]
        u1 = zrT[:, 8:12, :].rearrange("p (b a) n -> p b (a n)", b=2)
        zb = misc[:, 0:2 * T + 2].rearrange("p (b t) -> p b t", b=2)
        zd = misc[:, 2 * T + 2:3 * T + 2]
        s_c, s_h, s_small = sem("s_c"), sem("s_h"), sem("s_small")
        s_csig, s_dve, s_bf, s_par, s_parT = sem("s_csig"), sem("s_dve"), sem("s_bf"), sem("s_par"), sem("s_parT")
        s_acc, s_modp, s_mod, s_zp, s_ze, s_zbz, s_shift = (sem(x) for x in
            ("s_acc", "s_modp", "s_mod", "s_zp", "s_ze", "s_zbz", "s_shift"))
        junk1 = ps[:, 6:8, :].rearrange("p b n -> p (b n)")
        n1_square, n1_mean, n1_root, n1_gain, n1_rows, n1_turned, n1_evacuate, _, n1_ev = norm_mod(
            stage1, "n1", x, u1, uT, grow, junk1, 0, 1, False)

        ztiles = [("T", f"zr{t // 4}", t, P * (t % 4)) for t in range(ZT_TILES)]
        ztiles += [("q", "q", i, 0) for i in range(NT)]
        ztiles += [("T", "kcvc", ZT_TILES + t, P * t) for t in range(2)]
        ztiles += [("kv", "kv", i, 0) for i in range(NT)]
        ztiles += [("gl", None, i, 0) for i in range(NT)]
        last_of = {u: n for n, (_, u, _, _) in enumerate(ztiles) if u}
        stage1_units = index["ada11"] + 1
        ada_at, u = [], 4
        for _, name, _, _ in ztiles:
            ada_at.append([])
            while u < 12 and index[f"ada{u}"] < (index[name] if name else NU) + R - 2:
                ada_at[-1].append(u)
                u += 1
        ada_later = [[], []] + ada_at[:-2]
        ada_later[-1] = ada_later[-1] + ada_at[-2] + ada_at[-1]

        with nc.Block() as block:
            @block.sync
            def _(sp):
                sp.dma_start(crow[:, :], A["c"][0].rearrange("(p k) -> p k", k=KD)).then_inc(s_c, 16)
                sp.dma_start(bada[:, :], A["b_ada"].rearrange("a (u n) -> (a u) n", n=512)).then_inc(s_c, 16)
                sp.dma_start(cst[:, :], A["consts"][:, 0:NC]).then_inc(s_const, 16)
                load_units(sp, 0, 2)
                sp.dma_start(x, A["x"][0].rearrange("(i p) d -> p i d", p=P)).then_inc(s_h, 16)
                load_units(sp, 2, 10)
                sp.wait_ge(n1_ev, 2 * NT)
                sp.dma_start(uT_dram, uT[:, :, :]).then_inc(s_spill, 16)
                load_units(sp, 10, stage1_units)
                sp.wait_ge(s_spill, 16)

            @block.gpsimd
            def _(pool):
                pool.dma_start(grow[:, :], A["norm_mix_g"][0].partition_broadcast(P)).then_inc(s_small, 16)
                pool.dma_start(wgl[:, :, :], A["w_in"][0].rearrange("(p k) n -> p k n", k=KD)
                               [:, :, NSA0 + 1280:NSA0 + 1304]).then_inc(s_small, 16)
                row = 0
                for name in ("rwkv_mu", "rwkv_w0", "rwkv_a0", "rwkv_kk", "rwkv_ka"):
                    v = A[name].rearrange("a (t p) -> (a t) p", p=P)
                    pool.dma_start(parr[row:row + v.shape[0], :], v).then_inc(s_par, 16)
                    row += v.shape[0]
                pool.dma_start(parr[row:row + CT, :], A["rwkv_rk"][0].rearrange("(t h) d -> t (h d)", h=2))\
                    .then_inc(s_par, 16)
                pool.wait_ge(n1_ev, 2 * NT)
                pool.memset(zb[:, :, 0:1], 0.0).then_inc(s_zbz, 1)
                pool.wait_ge(s_small, 32)
                pool.wait_ge(s_par, 96)

            @block.scalar
            def _(act):
                act.wait_ge(s_c, 32)
                act.activation(csig[:, :], crow[:, :], ACT.Sigmoid).then_inc(s_csig, 1)
                act.wait_ge(s_h, 16)
                for i in range(NT):
                    n1_square(act, i)
                n1_root(act, 0, NT)
                act.wait_ge(s_const, 16)
                for u in range(4):
                    act.wait_ge(s_modp, u + 1)
                    act.activation(mod[:, u // 2, 512 * (u % 2):512 * (u % 2) + 512], ps[:, 4 + u % 2, :],
                                   ACT.Copy).then_inc(s_mod, 1)
                act.wait_ge(s_parT, 1)
                act.activation(par[:, :], ps[:, 6, 0:34], ACT.Copy).then_inc(s_mod, 1)
                for i in range(NT):
                    n1_evacuate(act, i)
                nshift = 0
                for n, (kind, _, i, _) in enumerate(ztiles):
                    act.wait_ge(s_zp, n + 1)
                    src = ps[:, n % 4, :]
                    if kind == "T" and i < ZT_TILES:
                        if nshift >= 2:
                            act.wait_ge(s_shift, nshift - 1)
                        if nshift == 0:
                            act.wait_ge(s_zbz, 1)
                        dst = zb[:, nshift % 2, 1:T + 1]
                        nshift += 1
                    elif kind == "T":
                        dst = kcvc[:, i - ZT_TILES, :]
                    elif kind == "gl":
                        dst, src = glog[:, i, :], ps[:, n % 4, 0:24]
                    else:
                        dst = (q if kind == "q" else kv)[:, i, :]
                    act.activation(dst, src, ACT.Copy).then_inc(s_ze, 1)
                    for u in ada_later[n]:
                        act.wait_ge(s_modp, u + 1)
                        act.activation(mod[:, u // 2, 512 * (u % 2):512 * (u % 2) + 512], ps[:, 4 + u % 2, :],
                                       ACT.Copy).then_inc(s_mod, 1)

            @block.vector
            def _(dve):
                link = Chain(dve, s_dve)
                dve.wait_ge(s_csig, 1)
                link(dve.tensor_tensor(csil[:, :], crow[:, :], csig[:, :], ALU.mult))

                def ada(u):
                    need(dve, f"ada{u}")
                    w = slot(f"ada{u}", KD, 512)
                    a = acc[:, u % 2, :]
                    if u >= 2:
                        dve.wait_ge(s_modp, u - 1)
                    link(dve.tensor_scalar(a, w[:, 0, :], csil[:, 0:1], None, ALU.mult))
                    for k in range(1, KD):
                        link(dve.scalar_tensor_tensor(a, w[:, k, :], csil[:, k:k + 1], a, ALU.mult, ALU.add))
                    dve.sem_inc(unit_free[index[f"ada{u}"] % R], 1)
                    dve.sem_inc(s_acc, 1)

                for u in range(4):
                    ada(u)
                    if u == 1:
                        n1_mean(dve, 0, NT)
                dve.wait_ge(s_const, 16)
                dve.tensor_copy(ones_bf[:, :], C("ones")).then_inc(s_bf, 1)
                dve.tensor_copy(strict_bf[:, :], C("strict")).then_inc(s_bf, 1)
                dve.wait_ge(s_small, 32)
                dve.wait_ge(s_mod, 4)
                n1_gain(dve, link)
                for i in range(NT):
                    n1_rows(dve, link, i)
                dve.wait_ge(s_mod, 5)
                nshift = 0
                for n, (kind, name, i, _) in enumerate(ztiles):
                    if kind == "T" and i < ZT_TILES:
                        dve.wait_ge(s_ze, n + 1)
                        z = zb[:, nshift % 2, :]
                        link(dve.tensor_tensor(zd, z[:, 0:T], z[:, 1:T + 1], ALU.subtract))
                        dve.scalar_tensor_tensor(zrT[:, i, :], zd, par[:, i:i + 1], z[:, 1:T + 1],
                                                 ALU.mult, ALU.add).then_inc(s_shift, 1)
                        nshift += 1
                        dve.wait_ge(s_shift, nshift)
                    for u in ada_at[n]:
                        ada(u)

            @block.tensor
            def _(pe):
                pe.wait_ge(s_const, 16)
                pe.wait_ge(s_c, 32)

                def spread(u):
                    pe.wait_ge(s_acc, u + 1)
                    if 2 <= u < 4:
                        pe.wait_ge(s_mod, u - 1)
                    elif u == 4:
                        pe.wait_ge(s_mod, 5)
                    elif u > 4:
                        pe.wait_ge(s_mod, u)
                    pe.matmul(ps[:, 4 + u % 2, :], C("ones"), acc[:, u % 2, :], start=True, stop=False)
                    pe.matmul(ps[:, 4 + u % 2, :], C("ident")[0:12, u:u + 1].to_broadcast([12, P]), bada[:, :],
                              start=False, stop=True).then_inc(s_modp, 1)

                for u in range(4):
                    spread(u)
                pe.wait_ge(s_par, 96)
                pe.transpose(ps[:, 6, 0:34], parr[:, :], C("ident")[0:34, 0:34]).then_inc(s_parT, 1)
                for i in range(NT):
                    n1_turned(pe, i)
                pe.wait_ge(n1_ev, 2 * NT)
                pe.wait_ge(s_small, 32)
                for n, (kind, name, i, c0) in enumerate(ztiles):
                    if name:
                        need(pe, name)
                    if n >= 4:
                        pe.wait_ge(s_ze, n - 3)
                    for k in range(KD):
                        if kind == "T":
                            w = 256 if name in ("zr3", "kcvc") else 512
                            ins = pe.matmul(ps[:, n % 4, :], slot(name, KD, w)[:, k, c0:c0 + P], uT[:, k, :],
                                            start=(k == 0), stop=(k == KD - 1))
                        elif kind == "gl":
                            ins = pe.matmul(ps[:, n % 4, 0:24], uT[:, k, P * i:P * i + P], wgl[:, k, :],
                                            start=(k == 0), stop=(k == KD - 1))
                        else:
                            w = slot(name, KD, 512)[:, k, :]
                            if kind == "q":
                                w = w.rearrange("p (g j d) -> p j g d", g=2, j=4)
                            ins = pe.matmul(ps[:, n % 4, :], uT[:, k, P * i:P * i + P], w, start=(k == 0), stop=(k == KD - 1))
                    ins.then_inc(s_zp, 1)
                    if name and last_of[name] == n:
                        pe.wait_ge(s_zp, n + 1)
                        pe.sem_inc(unit_free[index[name] % R], 1)
                    for u in ada_later[n]:
                        spread(u)
        stage1.close()

        stage2 = top.enter_context(ExitStack())
        yn = q
        qT = alloc(stage2, "qT", [P, CT, T])
        kT = alloc(stage2, "kT", [P, 2, T])
        buf = alloc(stage2, "buf", [P, 6 * 512])
        rope_k = alloc(stage2, "rope_k", [P, 2, 128])
        kc2 = qT.rearrange("p (n g) t -> p n g t", n=2)
        pe_rows = alloc(stage2, "pe_rows", [16, 2, P])
        peT = alloc(stage2, "peT", [P, 2, 16])
        w2 = alloc(stage2, "w2", [P, 2, 2, HD])
        hid = kcvc[0:2 * NCMP, :, :].rearrange("p a (m f) -> p (a m) f", m=2)
        kcmp = alloc(stage2, "kcmp", [NCMP, 2, 128])
        kcr = alloc(stage2, "kcr", [NCMP, 3, 128])
        kcT = alloc(stage2, "kcT", [P, NCMP])
        gate = alloc(stage2, "gate", [P, NT, 24])
        top8 = alloc(stage2, "top8", [P, 3, NT, HEADS])
        rsum = alloc(stage2, "rsum", [P, 3, NT, HEADS])
        coef = alloc(stage2, "coef", [P, 3, NT, HEADS])
        causal_bf = alloc(stage2, "causal_bf", [P, P], BF16)
        ident_bf = alloc(stage2, "ident_bf", [P, P], BF16)
        cmask_bf = alloc(stage2, "cmask_bf", [P, NT, NCMP], BF16)
        ot = kcvc[:, 0, :]
        prob = [buf[:, 512 * n:512 * n + 512] for n in range(3)]
        probT = [buf[:, 512 * n:512 * n + 512] for n in range(3, 6)]
        blk = [buf[:, 1024 * n:1024 * n + 32 * NCMP].rearrange("p (l g n) -> p l g n", l=16, g=2) for n in (1, 2)]
        hidT = [buf[:, 2 * P * n:2 * P * n + 4 * NCMP] for n in range(2)]
        pc = buf[:, 1024:1024 + 8 * NT * NCMP].rearrange("p (i h n) -> p i h n", i=NT, h=8)
        pcT = [buf[0:NCMP, 0:1024], buf[0:NCMP, 2048:3072]]
        (a_hT, a_hTe, a_ld, a_kc, a_bf, a_peT, a_pe, a_blk, a_rq, a_qT, a_q, a_rk, a_kT, a_k, a_hid, a_g1, a_tanh, a_g2, a_cmp, a_cev,
         a_crope, a_cT, a_cTe, a_gate, a_sc, a_sub, a_cexp, a_pm, a_ptr, a_pte, a_oc, a_y, a_dve, a_pool) = (
            sem(f"a_{n}") for n in ("hT hTe ld kc bf peT pe blk rq qT q rk kT k hid g1 tanh g2 cmp cev crope cT cTe gate sc sub "
                                    "cexp pm ptr pte oc y dve pool").split())
        a_S, a_mx, a_ex, a_TR, a_evD, a_evA, a_PV, a_out = (sem(f"a_{n}") for n in
                                                           ("S", "mx", "ex", "TR", "evD", "evA", "PV", "out"))
        items = [(i, b, hh) for i in reversed(range(NT)) for b in (1, 2) for hh in range(HEADS)]
        NI = len(items)

        with nc.Block() as block:
            @block.sync
            def _(sp):
                for parity in range(2):
                    for g in range(2):
                        sp.dma_start(kc2[HD * parity:HD * parity + HD, :, g, 0:T - parity],
                                     kcvc[HD * g:HD * g + HD, :, parity:T]).then_inc(a_kc, 16)
                for n, name in enumerate(("k", "v")):
                    sp.dma_start(pe_rows[:, n, :], A[f"cmp_pe_{name}"][0].rearrange("(l q) d -> l (q d)", q=2))\
                        .then_inc(a_ld, 16)
                    sp.dma_start(w2[:, n, :, :], A[f"cmp_w2_{name}"][0].rearrange("(t f) d -> f t d", t=2))\
                        .then_inc(a_ld, 16)
                load_units(sp, stage1_units, index["zg00"] + R - 2)
                sp.wait_ge(a_y, 1 + NT * 3)
                sp.dma_start(yn_dram, yn[:, :, :]).then_inc(a_out, 16)
                sp.wait_ge(a_out, 16)

            @block.gpsimd
            def _(pool):
                link = Chain(pool, a_pool)
                pool.wait_ge(a_pe, 1)
                pool.wait_ge(a_kc, 64)
                for n in range(2):
                    for half in range(2):
                        for g in range(2):
                            src = kc2[:, n, g, :].rearrange("p (m r x) -> p r m x", r=8, x=2)
                            link(pool.tensor_tensor(blk[n][:, 8 * half:8 * half + 8, g, :],
                                                    src[:, :, half:half + NCMP, 0],
                                                    peT[:, n, 8 * half:8 * half + 8].unsqueeze(2)
                                                    .to_broadcast([P, 8, NCMP]), ALU.add))
                    pool.sem_inc(a_blk, 1)
                for i in range(NT):
                    for b in range(2):
                        k = kv[:, i, 256 * b:256 * b + 128].rearrange("p (h d) -> p h d", d=32)
                        kh = kv[:, i, 256 * b:256 * b + 128].rearrange("p (g c d) -> p g c d", c=2, d=32)
                        t, s_ = (rope_k[:, x, :].rearrange("p (h d) -> p h d", d=32) for x in range(2))
                        th, sh = (rope_k[:, x, :].rearrange("p (g c d) -> p g c d", c=2, d=32) for x in range(2))
                        cos = C("cos")[:, 32 * i:32 * i + 32].unsqueeze(1).to_broadcast([P, 4, 32])
                        sin = C("sin")[:, 32 * i:32 * i + 32].unsqueeze(1).to_broadcast([P, 4, 32])
                        link(pool.tensor_tensor(t, k, cos, ALU.mult))
                        link(pool.tensor_tensor(s_, k, sin, ALU.mult))
                        link(pool.tensor_tensor(kh[:, :, 0, :], th[:, :, 0, :], sh[:, :, 1, :], ALU.subtract))
                        link(pool.tensor_tensor(kh[:, :, 1, :], th[:, :, 1, :], sh[:, :, 0, :], ALU.add))
                    pool.sem_inc(a_rk, 1)

            @block.vector
            def _(dve):
                link = Chain(dve, a_dve)
                dve.tensor_copy(causal_bf[:, :], C("causal")).then_inc(a_bf, 1)
                dve.tensor_copy(ident_bf[:, :], C("ident")).then_inc(a_bf, 1)
                dve.tensor_copy(cmask_bf[:, :, :], C("cmask").rearrange("p (i n) -> p i n", i=NT)).then_inc(a_bf, 1)
                dve.wait_ge(a_peT, 1)
                dve.tensor_copy(peT[:, :, :], ps[:, 7, 0:32].rearrange("p (n l) -> p n l", n=2)).then_inc(a_pe, 1)
                for i in range(NT):
                    x_ = q[:, i, :].rearrange("p (h d) -> p h d", d=32)
                    xh = q[:, i, :].rearrange("p (g c d) -> p g c d", c=2, d=32)
                    t, s_ = (prob[n].rearrange("p (h d) -> p h d", d=32) for n in range(2))
                    th, sh = (prob[n].rearrange("p (g c d) -> p g c d", c=2, d=32) for n in range(2))
                    cos = C("cos")[:, 32 * i:32 * i + 32].unsqueeze(1).to_broadcast([P, 16, 32])
                    sin = C("sin")[:, 32 * i:32 * i + 32].unsqueeze(1).to_broadcast([P, 16, 32])
                    link(dve.tensor_tensor(t, x_, cos, ALU.mult))
                    link(dve.tensor_tensor(s_, x_, sin, ALU.mult))
                    link(dve.tensor_tensor(xh[:, :, 0, :], th[:, :, 0, :], sh[:, :, 1, :], ALU.subtract))
                    dve.tensor_tensor(xh[:, :, 1, :], th[:, :, 1, :], sh[:, :, 0, :], ALU.add).then_inc(a_rq, 1)
                    dve.wait_ge(a_rq, i + 1)
                dve.wait_ge(a_blk, 2)
                for n in range(2):
                    xg, g1, g2, g3 = (hid[:, m, :] for m in range(4))
                    if n:
                        dve.wait_ge(a_hT, 1)
                    dve.wait_ge(a_hid, n + 1)
                    link(dve.tensor_copy(xg, ps[0:2 * NCMP, (5, 0)[n], 0:2 * P]))
                    link(dve.tensor_tensor(g1, xg, xg, ALU.mult))
                    link(dve.tensor_scalar(g1, g1, 0.044715, 1.0, ALU.mult, ALU.add))
                    dve.tensor_tensor(g1, g1, xg, ALU.mult).then_inc(a_g1, 1)
                    dve.wait_ge(a_tanh, n + 1)
                    link(dve.scalar_tensor_tensor(g3, g2, 1.0, xg, ALU.add, ALU.mult))
                    dve.tensor_scalar(g3, g3, 0.5, None, ALU.mult).then_inc(a_g2, 1)
                    dve.wait_ge(a_hT, n + 1)
                    dve.tensor_copy(hidT[n], ps[:, (6, 1)[n], 0:4 * NCMP]).then_inc(a_hTe, 1)
                dve.wait_ge(a_cmp, 2)
                link(dve.tensor_copy(kcmp[:, :, :], ps[0:NCMP, 7, 256:512].rearrange("p (n d) -> p n d", n=2)))
                kk_, kh = (kcmp[:, 0, :].rearrange("p (h d) -> p h d", d=32),
                           kcr[:, 2, :].rearrange("p (g c d) -> p g c d", c=2, d=32))
                t, s_ = (kcr[:, n, :].rearrange("p (h d) -> p h d", d=32) for n in range(2))
                th, sh = (kcr[:, n, :].rearrange("p (g c d) -> p g c d", c=2, d=32) for n in range(2))
                link(dve.tensor_tensor(t, kk_, C("ccos")[0:NCMP, :].unsqueeze(1).to_broadcast([NCMP, 4, 32]), ALU.mult))
                link(dve.tensor_tensor(s_, kk_, C("csin")[0:NCMP, :].unsqueeze(1).to_broadcast([NCMP, 4, 32]), ALU.mult))
                link(dve.tensor_tensor(kh[:, :, 0, :], th[:, :, 0, :], sh[:, :, 1, :], ALU.subtract))
                dve.tensor_tensor(kh[:, :, 1, :], th[:, :, 1, :], sh[:, :, 0, :], ALU.add).then_inc(a_crope, 1)
                dve.wait_ge(a_cT, 1)
                dve.tensor_copy(kcT[:, :], ps[:, 7, 0:NCMP]).then_inc(a_cTe, 1)

                for i in range(NT):
                    dve.wait_ge(a_sc, i + 1)
                    S = ps[:, 2 * (i % 2):2 * (i % 2) + 2, 0:4 * NCMP].rearrange("p g (j n) -> p g j n", j=4)
                    mx = top8[:, 0, i, :].rearrange("p (g j) -> p g j", g=2)
                    link(dve.tensor_reduce(mx, S, AX, ALU.max))
                    dve.tensor_tensor(pc[:, i, :, :].rearrange("p (g j) n -> p g j n", g=2), S,
                                      mx.unsqueeze(3).to_broadcast([P, 2, 4, NCMP]), ALU.subtract).then_inc(a_sub, 1)
                    dve.wait_ge(a_cexp, i + 1)
                    link(dve.tensor_reduce(rsum[:, 0, i, :], pc[:, i, :, :], AX, ALU.add))
                    seen = C("cseen")[:, NCMP * i:NCMP * i + NCMP].unsqueeze(1).to_broadcast([P, HEADS, NCMP])
                    dve.tensor_tensor(pc[:, i, :, :], pc[:, i, :, :], seen, ALU.mult).then_inc(a_pm, 1)
                dve.wait_ge(a_gate, 1)

                def coefs(b, i):
                    link(dve.reciprocal(coef[:, b, i, :], rsum[:, b, i, :]))
                    g = gate[:, i, :].rearrange("p (h b) -> p b h", b=3)[:, b, :]
                    link(dve.tensor_tensor(coef[:, b, i, :], coef[:, b, i, :], g, ALU.mult))
                    return coef[:, b, i, :].unsqueeze(2).to_broadcast([P, HEADS, HD])

                def heads(ap):
                    return ap.rearrange("p (h d) -> p h d", h=HEADS)

                dve.sem_inc(a_y, 1)
                for i in range(NT):
                    c = coefs(0, i)
                    dve.wait_ge(a_oc, i + 1)
                    dve.tensor_tensor(heads(yn[:, i, :]), heads(ps[:, 5 + i % 2, :]), c, ALU.mult).then_inc(a_y, 1)
                    dve.wait_ge(a_y, i + 2)

                def combine(grp):
                    i, b = NT - 1 - grp // 2, 1 + grp % 2
                    dve.wait_ge(a_ex, 8 * (grp + 1))
                    c = coefs(b, i)
                    dve.wait_ge(a_PV, 8 * (grp + 1))
                    link(dve.tensor_tensor(heads(ot), heads(ps[:, 5 + grp % 2, :]), c, ALU.mult))
                    dve.tensor_tensor(yn[:, i, :], yn[:, i, :], ot, ALU.add).then_inc(a_y, 1)
                    dve.wait_ge(a_y, 1 + NT + grp + 1)

                for t in range(NI + 4):
                    if t < NI:
                        i, b, hh = items[t]
                        dve.wait_ge(a_S, t + 1)
                        dve.tensor_reduce(top8[:, b, i, hh:hh + 1], ps[:, t % 3, 0:P * (i + 1)], AX, ALU.max,
                                          negate=True).then_inc(a_mx, 1)
                    e = t - 2
                    if 0 <= e < NI and e % 2 == 0:
                        n = P * (items[e][0] + 1)
                        dve.wait_ge(a_TR, e + 1)
                        dve.tensor_copy(probT[e % 3][:, 0:n], ps[:, 3 + e % 2, 0:n]).then_inc(a_evD, 1)
                    if t >= 11 and (t - 11) % 8 == 0 and (t - 11) // 8 < NI // 8:
                        combine((t - 11) // 8)

            @block.scalar
            def _(act):
                act.activation(gate[:, :, :], glog[:, :, :], ACT.Sigmoid).then_inc(a_gate, 1)
                act.wait_ge(a_blk, 2)
                for i in range(NT):
                    act.wait_ge(a_qT, i + 1)
                    act.activation(qT[:, :, P * i:P * i + P], ps[:, i % 2, :].rearrange("p (j t) -> p j t", j=CT),
                                   ACT.Copy, scale=HD ** -0.5).then_inc(a_q, 1)
                for i in range(NT):
                    act.wait_ge(a_kT, i + 1)
                    act.activation(kT[:, :, P * i:P * i + P],
                                   ps[:, 2 + i % 2, 0:256].rearrange("p (b t) -> p b t", b=2), ACT.Copy)\
                        .then_inc(a_k, 1)
                for n in range(2):
                    act.wait_ge(a_g1, n + 1)
                    act.activation(hid[:, 2, :], hid[:, 1, :], ACT.Tanh, scale=float(np.sqrt(2 / np.pi)))\
                        .then_inc(a_tanh, 1)
                for i in range(NT):
                    act.wait_ge(a_sub, i + 1)
                    act.activation(pc[:, i, :, :], pc[:, i, :, :], ACT.Exp).then_inc(a_cexp, 1)
                for i in range(NT):
                    act.wait_ge(a_ptr, i + 1)
                    if i >= 2:
                        act.wait_ge(a_oc, i - 1)
                    act.activation(pcT[i % 2], ps[0:NCMP, 1:3, :].rearrange("p b n -> p (b n)")
                                   if i % 2 else ps[0:NCMP, 3:5, :].rearrange("p b n -> p (b n)"), ACT.Copy)\
                        .then_inc(a_pte, 1)
                act.wait_ge(a_oc, NT)
                for t in range(NI + 4):
                    if t < NI:
                        i, b, hh = items[t]
                        act.wait_ge(a_mx, t + 1)
                        if t >= 3:
                            act.wait_ge(a_TR, t - 2)
                        n = P * (i + 1)
                        act.activation(prob[t % 3][:, 0:n], ps[:, t % 3, 0:n], ACT.Exp,
                                       bias=top8[:, b, i, hh:hh + 1], accum_out=rsum[:, b, i, hh:hh + 1])\
                            .then_inc(a_ex, 1)
                    e = t - 2
                    if 0 <= e < NI and e % 2 == 1:
                        n = P * (items[e][0] + 1)
                        act.wait_ge(a_TR, e + 1)
                        act.activation(probT[e % 3][:, 0:n], ps[:, 3 + e % 2, 0:n], ACT.Copy).then_inc(a_evA, 1)

            @block.tensor
            def _(pe):
                ident = C("ident")
                pe.wait_ge(a_ld, 16 * 4)
                for n in range(2):
                    ins = pe.transpose(ps[:, 7, 16 * n:16 * n + 16], pe_rows[:, n, :], ident[0:16, 0:16])
                ins.then_inc(a_peT, 1)
                for i in range(NT):
                    pe.wait_ge(a_rq, i + 1)
                    if i >= 2:
                        pe.wait_ge(a_q, i - 1)
                    for j in range(CT):
                        ins = pe.transpose(ps[:, i % 2, P * j:P * j + P], q[:, i, P * j:P * j + P], ident)
                    ins.then_inc(a_qT, 1)

                def compress_hidden(n):
                    name = f"w1{'kv'[n]}"
                    pe.wait_ge(a_blk, n + 1)
                    if n:
                        pe.wait_ge(a_q, NT)
                    need(pe, name)
                    for l in range(16):
                        ins = pe.matmul(ps[0:2 * NCMP, (5, 0)[n], 0:2 * P],
                                        blk[n][:, l, :, :].rearrange("p g n -> p (g n)"),
                                        slot(name, 16, 256)[:, l, :], start=(l == 0), stop=(l == 15))
                    ins.then_inc(a_hid, 1)
                    pe.wait_ge(a_hid, n + 1)
                    pe.sem_inc(unit_free[index[name] % R], 1)

                def hidden_transposed(n):
                    pe.wait_ge(a_g2, n + 1)
                    for t in range(2):
                        ins = pe.transpose(ps[:, (6, 1)[n], 2 * NCMP * t:2 * NCMP * (t + 1)],
                                           hid[:, 3, P * t:P * t + P], ident[0:2 * NCMP, 0:2 * NCMP])
                    ins.then_inc(a_hT, 1)

                def compress_out(n):
                    pe.wait_ge(a_hTe, n + 1)
                    for g in range(2):
                        for t in range(2):
                            ins = pe.matmul(ps[0:NCMP, 7, 256 + 128 * n + HD * g:256 + 128 * n + HD * g + HD],
                                            hidT[n][:, NCMP * (2 * t + g):NCMP * (2 * t + g + 1)], w2[:, n, t, :],
                                            start=(t == 0), stop=(t == 1))
                    ins.then_inc(a_cmp, 1)

                compress_hidden(0)
                for i in range(NT):
                    pe.wait_ge(a_rk, i + 1)
                    if i >= 2:
                        pe.wait_ge(a_k, i - 1)
                    for b in range(2):
                        ins = pe.transpose(ps[:, 2 + i % 2, P * b:P * b + P], kv[:, i, 256 * b:256 * b + P], ident)
                    ins.then_inc(a_kT, 1)
                hidden_transposed(0)
                compress_hidden(1)
                pe.wait_ge(a_pe, 1)
                compress_out(0)
                hidden_transposed(1)
                compress_out(1)
                pe.wait_ge(a_crope, 1)
                pe.transpose(ps[:, 7, 0:NCMP], kcr[:, 2, :], ident[0:NCMP, 0:NCMP]).then_inc(a_cT, 1)
                pe.wait_ge(a_cTe, 1)
                pe.wait_ge(a_q, NT)
                pe.wait_ge(a_k, NT)
                pe.wait_ge(a_bf, 3)
                for i in range(NT):
                    if i >= 2:
                        pe.wait_ge(a_sub, i - 1)
                    for hh in range(HEADS):
                        g, j = hh // 4, hh % 4
                        o = ps[:, 2 * (i % 2) + g, NCMP * j:NCMP * (j + 1)]
                        pe.matmul(o, qT[HD * g:HD * g + HD, j, P * i:P * i + P], kcT[HD * g:HD * g + HD, :],
                                  start=True, stop=False)
                        ins = pe.matmul(o, ident_bf[:, :], cmask_bf[:, i, :], start=False, stop=True)
                    ins.then_inc(a_sc, 1)
                pe.wait_ge(a_sub, NT)
                for i in range(NT + 1):
                    if i < NT:
                        pe.wait_ge(a_pm, i + 1)
                        if i >= 2:
                            pe.wait_ge(a_pte, i - 1)
                        b0 = 1 if i % 2 else 3
                        for hh in range(HEADS):
                            ins = pe.transpose(ps[0:NCMP, b0 + hh // 4, P * (hh % 4):P * (hh % 4) + P],
                                               pc[:, i, hh, :], ident)
                        ins.then_inc(a_ptr, 1)
                    if i >= 1:
                        m = i - 1
                        pe.wait_ge(a_pte, m + 1)
                        if m >= 2:
                            pe.wait_ge(a_y, m)
                        for hh in range(HEADS):
                            ins = pe.matmul(ps[:, 5 + m % 2, HD * hh:HD * hh + HD], pcT[m % 2][:, P * hh:P * hh + P],
                                            kcmp[:, 1, HD * (hh // 4):HD * (hh // 4) + HD], start=True, stop=True)
                        ins.then_inc(a_oc, 1)
                pe.wait_ge(a_pte, NT)
                warm(pe)
                for t in range(NI + 4):
                    if t < NI:
                        i, b, hh = items[t]
                        g, j = hh // 4, hh % 4
                        if t >= 3:
                            pe.wait_ge(a_ex, t - 2)
                        lhs = qT[HD * g:HD * g + HD, j, P * i:P * i + P]
                        pe.matmul(ps[:, t % 3, 0:P * (i + 1)], lhs, kT[HD * g:HD * g + HD, b - 1, 0:P * (i + 1)],
                                  start=True, stop=False)
                        pe.matmul(ps[:, t % 3, P * i:P * i + P], ident_bf[:, :], causal_bf[:, :], start=False,
                                  stop=True).then_inc(a_S, 1)
                    m = t - 2
                    if 0 <= m < NI:
                        pe.wait_ge(a_ex, m + 1)
                        if m >= 2:
                            pe.wait_ge((a_evD, a_evA)[m % 2], m // 2)
                        else:
                            pe.wait_ge(a_pte, NT)
                        for j in range(items[m][0] + 1):
                            ins = pe.transpose(ps[:, 3 + m % 2, P * j:P * j + P], prob[m % 3][:, P * j:P * j + P], ident)
                        ins.then_inc(a_TR, 1)
                    m = t - 3
                    if 0 <= m < NI:
                        i, b, hh = items[m]
                        grp = m // 8
                        pe.wait_ge((a_evD, a_evA)[m % 2], m // 2 + 1)
                        if hh == 0:
                            pe.wait_ge(a_y, 1 + NT + grp - 1 if grp >= 2 else 1 + NT)
                        for j in range(i + 1):
                            ins = pe.matmul(ps[:, 5 + grp % 2, HD * hh:HD * hh + HD], probT[m % 3][:, P * j:P * j + P],
                                            kv[:, j, 256 * (b - 1) + 128 + HD * (hh // 4):
                                               256 * (b - 1) + 128 + HD * (hh // 4) + HD],
                                            start=(j == 0), stop=(j == i))
                        ins.then_inc(a_PV, 1)
        stage2.close()
        attn.close()
        end_stage()

        stage3 = top.enter_context(ExitStack())
        NL = at["headspread"][0] - NC
        late = alloc(stage3, "late", [P, NL])
        vt = alloc(stage3, "vt", [P, NT, RW])
        bt = alloc(stage3, "bt", [P, CT, T])
        bonus = alloc(stage3, "bonus", [P, NT, HEADS])
        carry = alloc(stage3, "carry", [P, CT, NT - 1])
        prep = top.enter_context(ExitStack())
        lora = alloc(prep, "lora", [P, RW])
        logp = alloc(prep, "logp", [P, CT, NT * (P + 1)])
        av = alloc(prep, "av", [P, CT, T])
        kkn = bt
        sg = alloc(prep, "sg", [P, 2, T])
        tmp = alloc(prep, "tmp", [P, 2, T])
        lent = [ring[:, (index["zg00"] + R - 2 + n) % R, :] for n in range(2)]
        ees = [lent[0][:, 1024 * n:1024 * n + NT * (P + 1)] for n in range(2)]
        eis = [lent[0][:, 1024 * n:1024 * n + T] for n in range(2, 4)]
        spread = alloc(prep, "spread", [HEADS, RW])
        norms = alloc(prep, "norms", [HEADS, T])
        omka = alloc(prep, "omka", [P, CT])
        e0s = alloc(prep, "e0s", [P, 2, NT])
        spread_bank = (5, 6, 7, 0)
        wtab = alloc(prep, "wtab", [P, T])
        rT, kT_, vT = zrT[:, 0:4, :], zrT[:, 4:8, :], zrT[:, 8:12, :]

        def L8(name):
            a_, b_ = at[name]
            return late[:, a_ - NC:b_ - NC]

        DK = -float(np.exp(-0.5))
        (w_ld, w_th, w_w, w_a, w_sw, w_sa, w_v, w_ve, w_kk, w_sq, w_ss, w_rt, w_kn, w_lp, w_e, w_rk, w_bo, w_use, w_dve,
         w_bev, w_b, w_A, w_rn, w_sp, w_pool) = (
            sem(f"w_{n}") for n in "ld th w a sw sa v ve kk sq ss rt kn lp e rk bo use dve bev b A rn sp pool".split())

        with nc.Block() as block:
            @block.sync
            def _(sp):
                sp.dma_start(late[:, :], A["consts"][:, NC:NC + NL]).then_inc(w_ld, 16)
                sp.dma_start(spread[:, :], A["consts"][0:HEADS, NC + NL:NC + NL + RW]).then_inc(w_ld, 16)
                sp.dma_start(lora[0:HD, :], A["rwkv_w2"][0]).then_inc(w_ld, 16)
                sp.dma_start(lora[HD:P, :], A["rwkv_a2"][0]).then_inc(w_ld, 16)
                sp.wait_ge(w_ld, 64)

            @block.scalar
            def _(act):
                act.activation(zrT[0:HD, 12, :], zrT[0:HD, 12, :], ACT.Tanh).then_inc(w_th, 1)
                act.activation(zrT[:, 13, :], zrT[:, 13, :], ACT.Sigmoid).then_inc(w_th, 1)
                for c in range(CT):
                    act.wait_ge(w_w, c + 1)
                    if c >= 2:
                        act.wait_ge(w_lp, c - 1)
                    act.activation(sg[:, c % 2, :], ps[:, 0, :], ACT.Sigmoid, bias=par[:, 14 + c:15 + c])\
                        .then_inc(w_sw, 1)
                    act.wait_ge(w_a, c + 1)
                    act.activation(av[:, c, :], ps[:, 1, :], ACT.Sigmoid, bias=par[:, 18 + c:19 + c]).then_inc(w_sa, 1)
                    act.wait_ge(w_v, c + 1)
                    act.activation(vt[:, :, P * c:P * c + P], ps[:, 2, :].rearrange("p (i d) -> p i d", i=NT),
                                   ACT.Copy).then_inc(w_ve, 1)
                    act.wait_ge(w_kk, c + 1)
                    if c >= 2:
                        act.wait_ge(w_ss, c - 1)
                    act.activation(tmp[:, c % 2, :], kkn[:, c, :], ACT.Square).then_inc(w_sq, 1)
                act.wait_ge(w_ss, CT)
                act.activation(norms[:, :], ps[0:HEADS, 4, :], ACT.Sqrt).then_inc(w_rt, 1)
                for c in range(CT):
                    ee, ei, e0 = ees[c % 2], eis[c % 2], e0s[:, c % 2, :]
                    act.wait_ge(w_lp, c + 1)
                    if c >= 2:
                        act.wait_ge(w_use, c - 1)
                        act.wait_ge(w_b, c - 1)
                    act.activation(ee, logp[:, c, :], ACT.Exp, scale=DK).then_inc(w_e, 1)
                    lp = logp[:, c, :].rearrange("p (c t) -> p c t", c=NT)
                    act.activation(ei.rearrange("p (c t) -> p c t", c=NT), lp[:, :, 1:], ACT.Exp, scale=-DK)\
                        .then_inc(w_e, 1)
                    act.activation(e0, lp[:, :, 0], ACT.Exp, scale=-DK).then_inc(w_e, 1)

            @block.gpsimd
            def _(pool):
                link = Chain(pool, w_pool)
                for c in range(CT):
                    pool.wait_ge(w_kn, c + 1)
                    pool.wait_ge(w_sa, c + 1)
                    pool.wait_ge(w_rk, c + 1)
                    link(pool.tensor_tensor(av[:, c, :], kkn[:, c, :], av[:, c, :], ALU.mult))
                    pool.wait_ge(w_e, 3 * (c + 1))
                    pool.wait_ge(w_A, c + 1)
                    pool.tensor_tensor(bt[:, c, :], av[:, c, :], eis[c % 2], ALU.mult).then_inc(w_b, 1)
                pool.wait_ge(w_b, CT)

            @block.vector
            def _(dve):
                link = Chain(dve, w_dve)
                dve.tensor_scalar(omka[:, :], par[:, 26:30], -1.0, 1.0, ALU.mult, ALU.add).then_inc(w_dve, 1)
                link.n += 1
                for c in range(CT):
                    dve.tensor_scalar(kkn[:, c, :], kT_[:, c, :], par[:, 22 + c:23 + c], None, ALU.mult)\
                        .then_inc(w_kk, 1)
                dve.wait_ge(w_ld, 64)
                for c in range(CT):
                    dve.wait_ge(w_sw, c + 1)
                    for i in range(NT):
                        link(dve.tensor_tensor_scan(wtab[:, P * i:P * i + P], C("ones"),
                                                    sg[:, c % 2, P * i:P * i + P], 0.0, ALU.mult, ALU.add))
                    cum = wtab[:, :].rearrange("p (c t) -> p c t", c=NT)
                    lp = logp[:, c, :].rearrange("p (c t) -> p c t", c=NT)
                    mid = cum[:, :, P // 2 - 1:P // 2]
                    link(dve.tensor_tensor(lp[:, :, 1:], cum, mid.to_broadcast([P, NT, P]), ALU.subtract))
                    dve.tensor_scalar(lp[:, :, 0:1], mid, -1.0, None, ALU.mult).then_inc(w_lp, 1)
                    dve.wait_ge(w_lp, c + 1)
                dve.wait_ge(w_rt, 1)
                link(dve.tensor_scalar(norms[:, :], norms[:, :], 1e-12, None, ALU.max))
                dve.reciprocal(norms[:, :], norms[:, :]).then_inc(w_rn, 1)
                for c in range(CT):
                    dve.wait_ge(w_sp, c + 1)
                    dve.tensor_tensor(kkn[:, c, :], kkn[:, c, :], ps[:, spread_bank[c], :], ALU.mult).then_inc(w_kn, 1)
                dve.wait_ge(w_kn, CT)
                dve.wait_ge(w_ve, CT)
                for c in range(CT):
                    dve.wait_ge(w_sa, c + 1)
                    t0, t1 = tmp[:, 0, :], tmp[:, 1, :]
                    link(dve.tensor_scalar(t0, av[:, c, :], par[:, 26 + c:27 + c], omka[:, c:c + 1], ALU.mult, ALU.add))
                    link(dve.tensor_tensor(kT_[:, c, :], kT_[:, c, :], t0, ALU.mult))
                    if c >= 1:
                        dve.wait_ge(w_bo, c)
                    dve.scalar_tensor_tensor(t1, rT[:, c, :], par[:, 30 + c:31 + c], kT_[:, c, :], ALU.mult, ALU.mult)\
                        .then_inc(w_rk, 1)
                    dve.wait_ge(w_e, 3 * (c + 1))
                    dve.wait_ge(w_rk, c + 1)
                    e3 = ees[c % 2].rearrange("p (c t) -> p c t", c=NT)

                    def chunks(ap):
                        return ap.rearrange("p (c t) -> p c t", c=NT)

                    dve.scalar_tensor_tensor(chunks(vT[:, c, :]), chunks(kkn[:, c, :]), -1.0, e3[:, :, 0:P],
                                             ALU.mult, ALU.mult).then_inc(w_A, 1)
                    link(dve.tensor_tensor(chunks(rT[:, c, :]), chunks(rT[:, c, :]), e3[:, :, 1:], ALU.mult))
                    link(dve.tensor_tensor(kT_[:, c, :], kT_[:, c, :], eis[c % 2], ALU.mult))
                    dve.tensor_tensor(carry[:, c, :], e3[:, 0:NT - 1, P], e0s[:, c % 2, 1:NT], ALU.mult).then_inc(w_use, 1)
                dve.wait_ge(w_bo, CT)
                dve.tensor_copy(bonus[:, :, :], ps[:, 3, 0:8 * NT].rearrange("p (i h) -> p i h", i=NT)).then_inc(w_bev, 1)

            @block.tensor
            def _(pe):
                pe.wait_ge(w_ld, 64)
                pe.wait_ge(w_th, 2)
                for c in range(CT + 1):
                    if c < CT:
                        if c:
                            pe.wait_ge(w_sw, c)
                        pe.matmul(ps[:, 0, :], lora[0:HD, P * c:P * c + P], zrT[0:HD, 12, :], start=True, stop=True)\
                            .then_inc(w_w, 1)
                        if c:
                            pe.wait_ge(w_sa, c)
                        pe.matmul(ps[:, 1, :], lora[HD:P, P * c:P * c + P], zrT[HD:P, 12, :], start=True, stop=True)\
                            .then_inc(w_a, 1)
                        if c:
                            pe.wait_ge(w_ve, c)
                        for i in range(NT):
                            ins = pe.transpose(ps[:, 2, P * i:P * i + P], vT[:, c, P * i:P * i + P], C("ident"))
                        ins.then_inc(w_v, 1)
                    if c:
                        pe.wait_ge(w_sq, c)
                        pe.matmul(ps[0:HEADS, 4, :], L8("headsums")[:, HEADS * (c - 1):HEADS * c], tmp[:, (c - 1) % 2, :],
                                  start=(c == 1), stop=(c == CT)).then_inc(w_ss, 1)
                pe.wait_ge(w_rn, 1)
                pe.wait_ge(w_sw, CT)
                for c in range(CT):
                    pe.matmul(ps[:, spread_bank[c], :], spread[:, P * c:P * c + P], norms[:, :],
                              start=True, stop=True).then_inc(w_sp, 1)
                for c in range(CT):
                    pe.wait_ge(w_rk, c + 1)
                    for i in range(NT):
                        ins = pe.matmul(ps[:, 3, HEADS * i + 2 * c:HEADS * i + 2 * c + 2], tmp[:, 1, P * i:P * i + P],
                                        L8("headsel"), start=True, stop=True)
                    ins.then_inc(w_bo, 1)
        prep.close()

        chunk = top.enter_context(ExitStack())
        y = rT.rearrange("p c (i t) -> p i c t", i=NT)
        lent4 = [lent[1][:, 1024 * n:1024 * n + 1024] for n in range(4)]

        def quads(ap):
            return ap.rearrange("p (m j t) -> p m j t", m=2, j=4)

        gb = [alloc(chunk, "gb", [P, 2, 4, 2, P]),
              lent[0][:, 0:2048].rearrange("p (m j a t) -> p m j a t", m=2, j=4, a=2)]
        gk = [alloc(chunk, "gk", [P, 2, 4, 2, P]),
              lent[0][:, 2048:4096].rearrange("p (m j a t) -> p m j a t", m=2, j=4, a=2)]
        xm = alloc(chunk, "xm", [P, 2, 4, P])
        xts = [alloc(chunk, "xt", [P, 2, 4, P]), quads(lent4[0])]
        t1 = alloc(chunk, "t1", [P, 2, 4, P])
        lm = [alloc(chunk, "lm", [P, 2, 4, P]), quads(lent4[1])]
        kb = lent4[2].rearrange("p (m n) -> p m n", m=2)
        state = alloc(chunk, "state", [P, CT, HD])
        wsb, usb = (lent4[3][:, 512 * n:512 * n + 512].rearrange("p (h d) -> p h d", h=HEADS) for n in range(2))
        g_gr, g_ge, g_x0, g_xt0, g_x0e, g_lm, g_t1, g_t1e, g_x, g_xe, g_xt, g_xte = (
            sem(f"g_{n}") for n in "gr ge x0 xt0 x0e lm t1 t1e x xe xt xte".split())
        g_kb, g_kbe, g_w, g_we, g_u, g_ue, g_y, g_ye, g_s, g_se, g_dve, g_pool = (
            sem(f"g_{n}") for n in "kb kbe w we u ue y ye s se dve pool".split())
        NLV = 6
        bank = {"t1": 0, "x": 2, "xt": 4}
        gram_bank = (7, 3)

        def spread4(ap):
            return ap.unsqueeze(1).to_broadcast([P, 4, P])

        with nc.Block() as block:
            @block.gpsimd
            def _(pool):
                for c in range(NT):
                    for n in range(1, NLV + 1):
                        for p_ in range(2):
                            pool.wait_ge(g_ge, 8 * c + 4 * p_ + 2)
                            s_ = (c * NLV + n - 1) * 2 + p_
                            if s_ >= 4:
                                pool.wait_ge(g_t1, s_ - 3)
                            pool.tensor_tensor(lm[n % 2][:, p_, :, :], gb[c % 2][:, p_, :, 0, :],
                                               spread4(L8(f"lvl{n}")), ALU.mult).then_inc(g_lm, 1)

            @block.vector
            def _(dve):
                link = Chain(dve, g_dve)

                def masked(c):
                    xt = xts[c % 2]
                    if c >= 2:
                        dve.wait_ge(g_y, c - 1)
                    for p_ in range(2):
                        for m in range(4):
                            n = 8 * c + 4 * p_ + m
                            dve.wait_ge(g_gr, n + 1)
                            dst = (gb, gk)[m // 2][c % 2][:, p_, 2 * (m % 2):2 * (m % 2) + 2, :, :]\
                                .rearrange("p j a t -> p j (a t)")
                            a_ = at["strict"][0]
                            mask = cst[:, a_:a_ + 2 * P].unsqueeze(1).to_broadcast([P, 2, 2 * P])
                            dve.tensor_tensor(dst, ps[:, gram_bank[m % 2], :].rearrange("p (j n) -> p j n", j=2), mask,
                                              ALU.mult).then_inc(g_ge, 1)
                            if m == 3:
                                dve.wait_ge(g_ge, n - 1)
                                link(dve.tensor_tensor(xt[:, p_, :, :], gb[c % 2][:, p_, :, 0, :], spread4(L8("lvl0")),
                                                       ALU.mult))
                                dve.tensor_tensor(xt[:, p_, :, :], xt[:, p_, :, :], spread4(C("ident")), ALU.add)\
                                    .then_inc(g_xt0, 1)

                masked(0)
                for c in range(NT):
                    for n in range(NLV):
                        for p_ in range(2):
                            s_ = (c * NLV + n) * 2 + p_
                            dve.wait_ge(g_t1, s_ + 1)
                            dve.tensor_tensor(t1[:, p_, :, :], ps[:, bank["t1"] + p_, :].rearrange("p (j t) -> p j t", j=4),
                                              spread4(C("ident")), ALU.add).then_inc(g_t1e, 1)
                    dve.wait_ge(g_w, c + 1)
                    for p_ in range(2):
                        link(dve.tensor_copy(wsb.rearrange("p (j b) d -> p b j d", b=2)[:, p_, :, :],
                                             ps[:, 0 + p_, 0:256].rearrange("p (j d) -> p j d", j=4)))
                    dve.sem_inc(g_we, 1)
                    if c < NT - 1:
                        masked(c + 1)
                        dve.wait_ge(g_s, c + 1)
                        dve.wait_ge(g_y, c + 1)
                        for p_ in range(2):
                            r0 = HD * p_
                            new = ps[r0:r0 + HD, 6, :].rearrange("p (c n) -> p c n", c=CT)[:, :, r0:r0 + HD]
                            st = state[r0:r0 + HD, :, :]
                            if c:
                                link(dve.tensor_tensor(st, st, new, ALU.add))
                                new = st
                            link(dve.tensor_tensor(st, new, carry[r0:r0 + HD, :, c:c + 1].to_broadcast([HD, CT, HD]),
                                                   ALU.mult))
                        dve.sem_inc(g_se, 1)

            @block.scalar
            def _(act):
                for c in range(NT):
                    xt = xts[c % 2]
                    for p_ in range(2):
                        act.wait_ge(g_x0, 2 * c + p_ + 1)
                        act.activation(xm[:, p_, :, :], ps[:, bank["x"] + p_, :].rearrange("p (j t) -> p j t", j=4),
                                       ACT.Copy).then_inc(g_x0e, 1)
                    for n in range(NLV):
                        if n < NLV - 1:
                            for p_ in range(2):
                                s_ = (c * (NLV - 1) + n) * 2 + p_
                                act.wait_ge(g_x, s_ + 1)
                                act.activation(xm[:, p_, :, :],
                                               ps[:, bank["x"] + p_, :].rearrange("p (j t) -> p j t", j=4),
                                               ACT.Copy).then_inc(g_xe, 1)
                        for p_ in range(2):
                            s_ = (c * NLV + n) * 2 + p_
                            act.wait_ge(g_xt, s_ + 1)
                            act.activation(xt[:, p_, :, :], ps[:, bank["xt"] + p_, :].rearrange("p (j t) -> p j t", j=4),
                                           ACT.Copy).then_inc(g_xte, 1)
                    for m in range(2):
                        act.wait_ge(g_kb, 2 * c + m + 1)
                        act.activation(kb[:, m, :], ps[:, 6 + m, :], ACT.Copy).then_inc(g_kbe, 1)
                    act.wait_ge(g_u, c + 1)
                    act.activation(usb, ps[:, 2, :].rearrange("p (h d) -> p h d", h=HEADS), ACT.Copy).then_inc(g_ue, 1)
                    act.wait_ge(g_y, c + 1)
                    for p_ in range(2):
                        act.activation(y[:, c, :, HD * p_:HD * p_ + HD],
                                       ps[:, 4 + p_, 0:256].rearrange("p (j d) -> p j d", j=4), ACT.Copy)\
                            .then_inc(g_ye, 1)

            @block.tensor
            def _(pe):
                ident = C("ident")
                ar = zrT[:, :, :].rearrange("p t (c n) -> p t c n", c=NT)

                def gram(c, p_):
                    r0 = HD * p_
                    for m in range(4):
                        n = 8 * c + 4 * p_ + m
                        if n >= 2:
                            pe.wait_ge(g_ge, n - 1)
                        if c and n % 8 == 0:
                            pe.wait_ge(g_kbe, 2 * c)
                        for j in range(2):
                            ct = 2 * (m % 2) + j
                            lhs = (bt[r0:r0 + HD, ct, P * c:P * c + P], zrT[r0:r0 + HD, 4 + ct, P * c:P * c + P])[m // 2]
                            rhs = ar[r0:r0 + HD, ct:ct + 9:8, c, :]
                            for a_ in range(2):
                                o = ps[:, gram_bank[m % 2], 256 * j + P * a_:256 * j + P * a_ + P]
                                ins = pe.matmul(o, lhs, rhs[:, 1 - a_, :], start=True, stop=True)
                        ins.then_inc(g_gr, 1)

                gram(0, 0)
                gram(0, 1)
                for c in range(NT):
                    gbc, gkc, xt = gb[c % 2], gk[c % 2], xts[c % 2]
                    for p_ in range(2):
                        pe.wait_ge(g_xt0, 2 * c + p_ + 1)
                        pe.wait_ge(g_ge, 8 * (c + 1))
                        for j in range(4):
                            ins = pe.transpose(ps[:, bank["x"] + p_, P * j:P * j + P], xt[:, p_, j, :], ident)
                        ins.then_inc(g_x0, 1)
                    for n in range(NLV):
                        for p_ in range(2):
                            s_ = (c * NLV + n) * 2 + p_
                            pe.wait_ge(g_lm, s_ + 1)
                            if n == 0:
                                pe.wait_ge(g_x0e, 2 * c + p_ + 1)
                            else:
                                pe.wait_ge(g_xe, (c * (NLV - 1) + n - 1) * 2 + p_ + 1)
                            for j in range(4):
                                ins = pe.matmul(ps[:, bank["t1"] + p_, P * j:P * j + P], lm[(n + 1) % 2][:, p_, j, :],
                                                xm[:, p_, j, :],
                                                start=True, stop=True)
                            ins.then_inc(g_t1, 1)
                        if n < NLV - 1:
                            for p_ in range(2):
                                s_ = (c * NLV + n) * 2 + p_
                                pe.wait_ge(g_t1e, s_ + 1)
                                if n:
                                    pe.wait_ge(g_xte, s_ - 1)
                                for j in range(4):
                                    ins = pe.matmul(ps[:, bank["x"] + p_, P * j:P * j + P], xt[:, p_, j, :],
                                                    t1[:, p_, j, :], start=True, stop=True)
                                ins.then_inc(g_x, 1)
                            for p_ in range(2):
                                pe.wait_ge(g_xe, (c * (NLV - 1) + n) * 2 + p_ + 1)
                                if c and n == 0:
                                    pe.wait_ge(g_ye, 2 * c)
                                for j in range(4):
                                    ins = pe.transpose(ps[:, bank["xt"] + p_, P * j:P * j + P], xm[:, p_, j, :], ident)
                                ins.then_inc(g_xt, 1)
                        else:
                            for p_ in range(2):
                                s_ = (c * NLV + n) * 2 + p_
                                pe.wait_ge(g_t1e, s_ + 1)
                                pe.wait_ge(g_xte, s_ - 1)
                                for j in range(4):
                                    ins = pe.matmul(ps[:, bank["xt"] + p_, P * j:P * j + P], t1[:, p_, j, :],
                                                    xt[:, p_, j, :], start=True, stop=True)
                                ins.then_inc(g_xt, 1)
                    if c:
                        pe.wait_ge(g_se, c)
                    for m in range(2):
                        for ct in range(CT):
                            src = (zrT[:, 4 + ct, P * c:P * c + P], bt[:, ct, P * c:P * c + P])[m]
                            ins = pe.transpose(ps[:, 6 + m, P * ct:P * ct + P], src, ident)
                        ins.then_inc(g_kb, 1)
                    pe.wait_ge(g_t1e, 2 * NLV * (c + 1))
                    for h_ in range(HEADS):
                        ct, p_ = h_ // 2, h_ % 2
                        o = ps[:, p_, HD * ct:HD * ct + HD]
                        v_ = vt[:, c, HD * h_:HD * h_ + HD]
                        ins = pe.matmul(o, gkc[:, p_, ct, 0, :], v_, start=True, stop=(c == 0))
                        if c:
                            ins = pe.matmul(o, zrT[HD * p_:HD * p_ + HD, 8 + ct, P * c:P * c + P],
                                            state[HD * p_:HD * p_ + HD, ct, :], start=False, stop=True)
                    ins.then_inc(g_w, 1)
                    if c < NT - 1:
                        gram(c + 1, 0)
                    pe.wait_ge(g_we, c + 1)
                    pe.wait_ge(g_xte, 2 * NLV * (c + 1))
                    for h_ in range(HEADS):
                        ins = pe.matmul(ps[:, 2, HD * h_:HD * h_ + HD], xt[:, h_ % 2, h_ // 2, :], wsb[:, h_, :],
                                        start=True, stop=True)
                    ins.then_inc(g_u, 1)
                    if c < NT - 1:
                        gram(c + 1, 1)
                    pe.wait_ge(g_ue, c + 1)
                    for h_ in range(HEADS):
                        ct, p_ = h_ // 2, h_ % 2
                        o = ps[:, 4 + p_, HD * ct:HD * ct + HD]
                        v_ = vt[:, c, HD * h_:HD * h_ + HD]
                        if c:
                            pe.matmul(o, zrT[HD * p_:HD * p_ + HD, ct, P * c:P * c + P],
                                      state[HD * p_:HD * p_ + HD, ct, :], start=True, stop=False)
                        pe.matmul(o, gbc[:, p_, ct, 1, :], usb[:, h_, :], start=(c == 0), stop=False)
                        ins = pe.matmul(o, gkc[:, p_, ct, 1, :], v_, start=False, stop=True)
                    ins.then_inc(g_y, 1)
                    pe.wait_ge(g_kbe, 2 * (c + 1))
                    for ct in range(CT):
                        o = ps[:, 6, P * ct:P * ct + P]
                        pe.matmul(o, kb[:, 1, P * ct:P * ct + P], usb[:, 2 * ct:2 * ct + 2, :], start=True, stop=False)
                        ins = pe.matmul(o, kb[:, 0, P * ct:P * ct + P], vt[:, c, P * ct:P * ct + P], start=False,
                                        stop=True)
                    ins.then_inc(g_s, 1)
                pe.wait_ge(g_ye, 2 * NT)
        chunk.close()

        post = top.enter_context(ExitStack())
        yr = zrT[:, 8:12, :]
        lnw = alloc(post, "lnw", [P, RW])
        lnb = alloc(post, "lnb", [P, RW])
        g2 = alloc(post, "g2", [P, RW])
        yc = alloc(post, "yc", [P, 2, RW])
        ysq = alloc(post, "ysq", [P, 2, RW])
        yb = alloc(post, "yb", [P, 2, RW])
        zeros = alloc(post, "zeros", [P, D])
        hm = alloc(post, "hm", [P, NT, HEADS])
        hv = alloc(post, "hv", [P, NT, HEADS])
        hs_ = alloc(post, "hs_", [P, NT, HEADS])
        q_ld, q_yc, q_sq, q_v, q_s, q_yb, q_g, q_done, q_dve, q_pool, q_z = (
            sem(f"q_{n}") for n in "ld yc sq v s yb g done dve pool z".split())

        def by_head(ap):
            return ap.rearrange("p (h d) -> p h d", d=HD)

        with nc.Block() as block:
            @block.sync
            def _(sp):
                sp.dma_start(lnw[:, :], A["rwkv_ln_w"][0].partition_broadcast(P)).then_inc(q_ld, 16)
                sp.dma_start(lnb[:, :], A["rwkv_ln_b"][0].partition_broadcast(P)).then_inc(q_ld, 16)
                sp.dma_start(g2[:, :], A["rwkv_g2"][0]).then_inc(q_ld, 16)
                sp.wait_ge(q_ld, 48)

            @block.gpsimd
            def _(pool):
                link = Chain(pool, q_pool)
                link(pool.memset(zeros[:, :], 0.0))
                pool.dma_start(y_dram[E * P:, :].rearrange("(b p) d -> p b d", p=P),
                               zeros[:, :].unsqueeze(1).to_broadcast([P, OVER, D])).then_inc(q_z, 16)
                pool.wait_ge(q_ld, 48)
                for i in range(NT):
                    if i >= 2:
                        pool.wait_ge(q_done, i - 1)
                    link(pool.tensor_tensor(by_head(yb[:, i % 2, :]), by_head(vt[:, i, :]),
                                            bonus[:, i, :].unsqueeze(2).to_broadcast([P, HEADS, HD]), ALU.mult))
                    pool.tensor_tensor(yb[:, i % 2, :], yb[:, i % 2, :], lnb[:, :], ALU.add).then_inc(q_yb, 1)
                pool.wait_ge(q_z, 16)

            @block.scalar
            def _(act):
                for i in range(NT):
                    act.wait_ge(q_yc, i + 1)
                    act.activation(ysq[:, i % 2, :], yc[:, i % 2, :], ACT.Square).then_inc(q_sq, 1)
                    act.wait_ge(q_v, i + 1)
                    act.activation(hs_[:, i, :], hv[:, i, :], ACT.Sqrt).then_inc(q_s, 1)

            @block.vector
            def _(dve):
                link = Chain(dve, q_dve)
                dve.wait_ge(q_ld, 48)
                for i in range(NT):
                    c_ = yc[:, i % 2, :]
                    y4 = y[:, i, :, :].rearrange("p c (b d) -> p c b d", b=2)
                    c4 = c_.rearrange("p (c b d) -> p c b d", b=2, d=HD)
                    m_ = hm[:, i, :].rearrange("p (c b) -> p c b", b=2)
                    link(dve.tensor_reduce(m_, y4, AX, ALU.add))
                    link(dve.tensor_scalar(m_, m_, 1.0 / HD, None, ALU.mult))
                    dve.tensor_tensor(c4, y4, m_.unsqueeze(3).to_broadcast([P, CT, 2, HD]), ALU.subtract)\
                        .then_inc(q_yc, 1)
                    dve.wait_ge(q_sq, i + 1)
                    link(dve.tensor_reduce(hv[:, i, :], by_head(ysq[:, i % 2, :]), AX, ALU.add))
                    dve.tensor_scalar(hv[:, i, :], hv[:, i, :], 1.0 / HD, 64e-5, ALU.mult, ALU.add).then_inc(q_v, 1)
                    dve.wait_ge(q_s, i + 1)
                    link(dve.reciprocal(hs_[:, i, :], hs_[:, i, :]))
                    link(dve.tensor_tensor(by_head(c_), by_head(c_),
                                           hs_[:, i, :].unsqueeze(2).to_broadcast([P, HEADS, HD]), ALU.mult))
                    link(dve.tensor_tensor(c_, c_, lnw[:, :], ALU.mult))
                    dve.wait_ge(q_yb, i + 1)
                    link(dve.tensor_tensor(c_, c_, yb[:, i % 2, :], ALU.add))
                    dve.wait_ge(q_g, i + 1)
                    dve.tensor_tensor(yr[:, i, :], c_, ps[:, i, :], ALU.mult).then_inc(q_done, 1)

            @block.tensor
            def _(pe):
                pe.wait_ge(q_ld, 48)
                for i in range(NT):
                    pe.matmul(ps[:, i, :], zrT[:, 13, P * i:P * i + P], g2[:, :], start=True, stop=True).then_inc(q_g, 1)
        post.close()
        stage3.close()
        end_stage()

        h = alloc(top, "h", [P, NT, D])
        row_y = alloc(top, "row_y", [P, NT, 2], I32)
        wts = alloc(top, "wts", [P, NT, 2])
        slots = alloc(top, "slots", [P, NBLK], I32)
        over = alloc(top, "over", [1, 8], I32)
        stage4 = top.enter_context(ExitStack())
        uT = alloc(stage4, "uT2", [P, KD, T])
        mg = alloc(stage4, "mg", [P, NT, D])
        tmps = alloc(stage4, "tmps", [P, 2, RW])
        yn = mg[:, 0:2, :].rearrange("p b (a n) -> p (b a) n", a=2)
        yrT, ynT = zrT[:, 0:4, :], zrT[:, 4:8, :]
        mgT = zrT[:, 0:8, :]
        grow2 = zrT[:, 8:10, :].rearrange("p a n -> p (a n)")
        u2 = mg[:, 0:2, :]
        m_ld, m_yT, m_yTe, m_zg, m_sig, m_mg, m_mT, m_mTe, m_o, m_h, m_dve, m_h0, m_g = (
            sem(f"m_{n}") for n in "ld yT yTe zg sig mg mT mTe o h dve h0 g".split())
        combos = [(j, i) for j in range(2) for i in range(NT)]
        gu = [A[f"moe_w_{n}"][0].rearrange("e (p k) n -> e p k n", k=KD) for n in ("gate", "up")]
        dn = A["moe_w_down"][0].rearrange("e (p j) n -> e p j n", j=4)
        fills = [sum(1 for n in range(NU) if n % R == s_) for s_ in range(R)]

        def place_of(kind, b, it=None):
            if b == 0 and kind != "d":
                pos = "gu".index(kind)
            elif kind == "d":
                pos = 2 + 3 * b + (2 if b < E - 1 else 0)
            else:
                pos = 2 + 3 * (b - 1) + "gu".index(kind)
            before = pos // R
            return (NU + pos) % R, (before if it is None else before + it)

        def expert_slot(s_, k, n):
            return ring[:, s_, :].rearrange("p (k n) -> p k n", k=k)

        def load_expert(eng, kind, b, it=None):
            s_, before = place_of(kind, b, it)
            eng.wait_ge(unit_free[s_], before + fills[s_])
            e_ = b if it is None else 2 * it + b
            src = dn[e_] if kind == "d" else gu["gu".index(kind)][e_]
            eng.dma_start(expert_slot(s_, 4 if kind == "d" else KD, 0), src).then_inc(unit_in[s_], 16)

        def need_expert(eng, kind, b, it=None):
            s_, before = place_of(kind, b, it)
            eng.wait_ge(unit_in[s_], 16 * before + (total[s_] + 16))
            return expert_slot(s_, 4 if kind == "d" else KD, 0)

        wr = alloc(stage4, "wr", [P, KD, NG + E])
        rbias = alloc(stage4, "rbias", [P, NG + E])
        m_wr, m_lg = sem("m_wr"), sem("m_lg")

        n2_square, n2_mean, n2_root, n2_gain, n2_rows, n2_turned, n2_evacuate, n2_store, n2_ev = norm_mod(
            stage4, "n2", h, u2, uT, grow2, zrT[:, 10:12, :].rearrange("p a n -> p (a n)"), 3, 4, True)

        with nc.Block() as block:
            @block.sync
            def _(sp):
                sp.dma_start(yn, yn_dram).then_inc(m_ld, 16)
                sp.dma_start(uT[:, :, :], uT_dram).then_inc(m_ld, 16)
                sp.dma_start(h[:, :, :], A["x"][0].rearrange("(i p) d -> p i d", p=P)).then_inc(m_h0, 16)
                load_units(sp, index["zg00"] + R - 2, NU)
                sp.dma_start(wr[:, :, 0:NG], A["w_router_grp"][0].rearrange("(p k) n -> p k n", k=KD)).then_inc(m_wr, 16)
                sp.dma_start(wr[:, :, NG:], A["w_router_exp"][0].rearrange("(p k) n -> p k n", k=KD)).then_inc(m_wr, 16)
                sp.dma_start(rbias[:, 0:NG], A["b_router_grp"][0].partition_broadcast(P)).then_inc(m_wr, 16)
                sp.dma_start(rbias[:, NG:], A["b_router_exp"][0].partition_broadcast(P)).then_inc(m_wr, 16)
                for kind, b in (("g", 0), ("u", 0), ("g", 1), ("u", 1), ("d", 0), ("g", 2)):
                    load_expert(sp, kind, b)
                sp.wait_ge(m_wr, 64)
                sp.wait_ge(m_ld, 32)
                sp.wait_ge(m_h0, 16)

            @block.scalar
            def _(act):
                for n in range(8):
                    act.wait_ge(m_yT, n + 1)
                    act.activation((yrT, ynT)[n % 2][:, :, P * (n // 2):P * (n // 2) + P],
                                   ps[:, n % 4, :].rearrange("p (j t) -> p j t", j=4), ACT.Copy).then_inc(m_yTe, 1)
                for n in range(8):
                    if n:
                        act.wait_ge(m_mg, n)
                    for b in range(2):
                        act.wait_ge(m_zg, 2 * n + b + 1)
                        act.activation(tmps[:, b, :], ps[:, 4 * (n % 2) + 2 * b, :], ACT.Sigmoid).then_inc(m_sig, 1)
                for n in range(8):
                    act.wait_ge(m_mT, n + 1)
                    act.activation(mgT[:, 4 * (n % 2):4 * (n % 2) + 4, P * (n // 2):P * (n // 2) + P],
                                   ps[:, n % 4, :].rearrange("p (k t) -> p k t", k=4), ACT.Copy).then_inc(m_mTe, 1)
                for i in range(NT):
                    act.wait_ge(m_h, 2 * (i + 1))
                    n2_square(act, i)
                    n2_root(act, i, i + 1)
                    if i:
                        n2_evacuate(act, i - 1)
                n2_evacuate(act, NT - 1)

            @block.vector
            def _(dve):
                link = Chain(dve, m_dve)
                for n, (j, i) in enumerate(combos):
                    cols = slice(512 * j, 512 * j + 512)
                    for b in range(2):
                        dve.wait_ge(m_sig, 2 * n + b + 1)
                        link(dve.tensor_tensor(tmps[:, b, :], tmps[:, b, :], ps[:, 4 * (n % 2) + 2 * b + 1, :],
                                               ALU.mult))
                    dve.tensor_tensor(mg[:, i, cols], tmps[:, 0, :], tmps[:, 1, :], ALU.add).then_inc(m_mg, 1)
                dve.wait_ge(m_h0, 16)
                dve.wait_ge(m_g, 16)
                n2_gain(dve, link)
                n = 0
                for i in range(NT):
                    for j in range(2):
                        cols = slice(512 * j, 512 * j + 512)
                        dve.wait_ge(m_o, n + 1)
                        link(dve.tensor_tensor(tmps[:, 0, :], ps[:, 4 + n % 3, :], mod[:, 2, cols], ALU.mult))
                        dve.tensor_tensor(h[:, i, cols], h[:, i, cols], tmps[:, 0, :], ALU.add).then_inc(m_h, 1)
                        dve.wait_ge(m_h, n + 1)
                        n += 1
                    n2_mean(dve, i, i + 1)
                    if i == 0:
                        dve.wait_ge(m_mT, 8)
                    n2_rows(dve, link, i)

            @block.gpsimd
            def _(pool):
                pool.wait_ge(m_yTe, 8)
                pool.dma_start(grow2, A["norm_ffn_g"][0].partition_broadcast(P)).then_inc(m_g, 16)
                n2_store(pool)
                pool.wait_ge(m_g, 16)

            @block.tensor
            def _(pe):
                ident = C("ident")
                pe.wait_ge(m_ld, 32)
                for n in range(8):
                    i = n // 2
                    src = (yr, yn)[n % 2][:, i, :].rearrange("t (p j) -> t j p", j=4)
                    if n >= 4:
                        pe.wait_ge(m_yTe, n - 3)
                    for j in range(4):
                        ins = pe.transpose(ps[:, n % 4, P * j:P * j + P], src[:, j, :], ident)
                    ins.then_inc(m_yT, 1)
                pe.wait_ge(m_yTe, 8)
                for name in ("p_rwkv", "p_nsa"):
                    need(pe, name)
                for n, (j, i) in enumerate(combos):
                    cols = slice(512 * j, 512 * j + 512)
                    if n >= 2:
                        pe.wait_ge(m_mg, n - 1)
                    for b in range(2):
                        need(pe, f"zg{b}{j}")
                        w, yT = slot(("p_rwkv", "p_nsa")[b], 4, D), (yrT, ynT)[b]
                        for k in range(4):
                            pe.matmul(ps[:, 4 * (n % 2) + 2 * b + 1, :], yT[:, k, P * i:P * i + P], w[:, k, cols],
                                      start=(k == 0), stop=(k == 3))
                        for k in range(KD):
                            ins = pe.matmul(ps[:, 4 * (n % 2) + 2 * b, :], uT[:, k, P * i:P * i + P],
                                            slot(f"zg{b}{j}", KD, 512)[:, k, :], start=(k == 0), stop=(k == KD - 1))
                        ins.then_inc(m_zg, 1)
                    if i == NT - 1:
                        pe.wait_ge(m_zg, 2 * n + 2)
                        for b in range(2):
                            pe.sem_inc(unit_free[index[f"zg{b}{j}"] % R], 1)
                for name in ("p_rwkv", "p_nsa"):
                    pe.sem_inc(unit_free[index[name] % R], 1)
                for n in range(8):
                    i, b = n // 2, n % 2
                    pe.wait_ge(m_mg, max(7, 5 + i))
                    if n >= 4:
                        pe.wait_ge(m_mTe, n - 3)
                    src = mg[:, i, :].rearrange("t (p k) -> t k p", k=KD)
                    for k in range(4):
                        ins = pe.transpose(ps[:, n % 4, P * k:P * k + P], src[:, 4 * b + k, :], ident)
                    ins.then_inc(m_mT, 1)

                def logits(i):
                    pe.wait_ge(n2_ev, 2 * (i + 1))
                    for k in range(KD):
                        ins = pe.matmul(ps[:, 7, (NG + E) * i:(NG + E) * (i + 1)], uT[:, k, P * i:P * i + P], wr[:, k, :],
                                        start=(k == 0), stop=(k == KD - 1))
                    ins.then_inc(m_lg, 1)

                n = 0
                pe.wait_ge(m_mTe, 8)
                pe.wait_ge(m_wr, 64)
                pe.wait_ge(m_mg, 8)
                for name in ("wo0", "wo1"):
                    need(pe, name)
                for i in range(NT):
                    for j in range(2):
                        if n >= 3:
                            pe.wait_ge(m_h, n - 2)
                        for k in range(KD):
                            ins = pe.matmul(ps[:, 4 + n % 3, :], mgT[:, k, P * i:P * i + P],
                                            slot(f"wo{k // 4}", 4, D)[:, k % 4, 512 * j:512 * j + 512],
                                            start=(k == 0), stop=(k == KD - 1))
                        ins.then_inc(m_o, 1)
                        n += 1
                    if i:
                        n2_turned(pe, i - 1)
                    if i >= 2:
                        logits(i - 2)
                pe.wait_ge(m_o, 8)
                for name in ("wo0", "wo1"):
                    pe.sem_inc(unit_free[index[name] % R], 1)
                logits(NT - 2)
                n2_turned(pe, NT - 1)
                logits(NT - 1)
                pe.wait_ge(m_lg, NT)

        scratch = mg[:, :, :].rearrange("p i n -> p (i n)")
        used = [0]

        def rb(name, shape, dt=F32):
            n = int(np.prod(shape[1:]))
            words = n // 2 if dt == BF16 else n
            v = scratch[0:shape[0], used[0]:used[0] + words]
            used[0] += words
            v = v if dt == F32 else v.bitcast(dt)
            axes = "abc"[:len(shape) - 1]
            return v.rearrange(f"p ({' '.join(axes)}) -> p {' '.join(axes)}", **dict(zip(axes, shape[1:])))

        lg = rb("lg", [P, NT, NG + E])
        gmax, gsum, gpick, m12, pick, e2, den = (rb(n, [P, NT] if n != "m12" else [P, 2, NT]) for n in
                                                 ("gmax", "gsum", "gpick", "m12", "pick", "e2", "den"))
        ge = rb("ge", [P, NT, NG])
        ml = rb("ml", [P, NT, E])
        t32 = rb("t32", [P, NT, E])
        oh = rb("oh", [P, 2, NT, E])
        ohb = rb("ohb", [P, NT, E], BF16)
        rank = rb("rank", [P, NT, E])
        cnt, nov, ovi, ovs = (rb(n, [P, E]) for n in ("cnt", "nov", "ovi", "ovs"))
        sel = rb("sel", [P, 3, 2, NT])
        kx, mx_, bx, px, rx = (rb(n, [P, 2, NT]) for n in ("kx", "mx", "bx", "px", "rx"))
        iota = rb("iota", [P, P])
        at_place = rb("at_place", [P, 2, NT, P])
        at_block = rb("at_block", [P, 2, NT, NBLK])
        in0 = rb("in0", [1, OVER, E])
        in1 = rb("in1", [1, OVER, E])
        ov8 = rb("ov8", [1, 8])
        r_ld, r_a, r_b, r_e, r_oh, r_rk, r_dve, r_at, r_tab, r_sl, r_ov = (
            sem(f"r_{n}") for n in "ld a b e oh rk dve at tab sl ov".split())

        with nc.Block() as block:
            @block.sync
            def _(sp):
                sp.dma_start(iota[:, :], A["consts"][:, at["iota"][0]:at["iota"][1]]).then_inc(r_ld, 16)
                sp.wait_ge(r_ld, 16)

            @block.scalar
            def _(act):
                act.wait_ge(r_a, 1)
                act.activation(ge[:, :, :], ge[:, :, :], ACT.Exp).then_inc(r_e, 1)
                act.wait_ge(r_b, 1)
                act.activation(e2[:, :], e2[:, :], ACT.Exp).then_inc(r_e, 1)

            @block.tensor
            def _(pe):
                pe.wait_ge(r_oh, 1)
                for i in range(NT + 1):
                    o = ps[:, 1, E * i:E * i + E]
                    for j in range(i):
                        ins = pe.matmul(o, ones_bf[:, :], ohb[:, j, :], start=(j == 0), stop=(j == i - 1 and i == NT))
                    if i < NT:
                        ins = pe.matmul(o, strict_bf[:, :], ohb[:, i, :], start=(i == 0), stop=True)
                ins.then_inc(r_rk, 1)
                pe.wait_ge(r_at, 1)
                for n in range(2 * NT):
                    ins = pe.matmul(ps[:, 2, 0:NBLK], at_place[:, n // NT, n % NT, :], at_block[:, n // NT, n % NT, :],
                                    start=(n == 0), stop=(n == 2 * NT - 1))
                ins.then_inc(r_tab, 1)

            @block.vector
            def _(dve):
                link = Chain(dve, r_dve)
                TT, TS = dve.tensor_tensor, dve.tensor_scalar

                def wide(ap, n):
                    return ap.unsqueeze(2).to_broadcast([P, NT, n])

                def over_tiles(ap, n):
                    return ap.unsqueeze(1).to_broadcast([P, NT, n])

                link(TT(lg[:, :, :], ps[:, 7, 0:NT * (NG + E)].rearrange("p (i n) -> p i n", i=NT),
                        over_tiles(rbias[:, :], NG + E), ALU.add))
                lgg, lge = lg[:, :, 0:NG], lg[:, :, NG:]
                link(dve.tensor_reduce(gmax[:, :], lgg, AX, ALU.max))
                TT(ge[:, :, :], lgg, wide(gmax[:, :], NG), ALU.subtract).then_inc(r_a, 1)
                t4 = t32[:, :, 0:NG]
                link(TT(t4, lgg, wide(gmax[:, :], NG), ALU.is_equal))
                link(TT(t4, t4, over_tiles(C("group_down"), NG), ALU.mult))
                link(dve.tensor_reduce(gpick[:, :], t4, AX, ALU.max))
                link(TT(ml[:, :, :], over_tiles(C("group_down_of"), E), wide(gpick[:, :], E), ALU.is_equal))
                link(TS(ml[:, :, :], ml[:, :, :], -NEG, NEG, ALU.mult, ALU.add))
                link(TT(ml[:, :, :], ml[:, :, :], lge, ALU.add))
                for j in range(2):
                    link(dve.tensor_reduce(m12[:, j, :], ml[:, :, :], AX, ALU.max))
                    link(TT(t32[:, :, :], ml[:, :, :], wide(m12[:, j, :], E), ALU.is_equal))
                    link(TT(t32[:, :, :], t32[:, :, :], over_tiles(C("expert_down"), E), ALU.mult))
                    link(dve.tensor_reduce(pick[:, :], t32[:, :, :], AX, ALU.max))
                    link(TT(oh[:, j, :, :], over_tiles(C("expert_down"), E), wide(pick[:, :], E), ALU.is_equal))
                    if j == 0:
                        link(dve.scalar_tensor_tensor(ml[:, :, :], oh[:, 0, :, :], 3 * NEG, ml[:, :, :], ALU.mult, ALU.add))
                TT(ohb[:, :, :], oh[:, 0, :, :], oh[:, 1, :, :], ALU.add).then_inc(r_oh, 1)
                TT(e2[:, :], m12[:, 1, :], m12[:, 0, :], ALU.subtract).then_inc(r_b, 1)
                dve.wait_ge(r_e, 2)
                link(dve.tensor_reduce(gsum[:, :], ge[:, :, :], AX, ALU.add))
                link(TS(den[:, :], e2[:, :], 1.0, None, ALU.add))
                link(TT(den[:, :], den[:, :], gsum[:, :], ALU.mult))
                link(dve.reciprocal(wts[:, :, 0], den[:, :]))
                link(TT(wts[:, :, 1], wts[:, :, 0], e2[:, :], ALU.mult))
                dve.wait_ge(r_rk, 1)
                link(dve.tensor_copy(rank[:, :, :], ps[:, 1, 0:NT * E].rearrange("p (i n) -> p i n", i=NT)))
                link(dve.tensor_copy(cnt[:, :], ps[:, 1, NT * E:NT * E + E]))
                link(TS(nov[:, :], cnt[:, :], float(P), None, ALU.is_gt))
                for m in (2, 3):
                    link(dve.scalar_tensor_tensor(nov[:, :], cnt[:, :], float(m * P), nov[:, :], ALU.is_gt, ALU.add))
                link(dve.tensor_tensor_scan(ovi[:, :], C("ones")[:, 0:E], nov[:, :], 0.0, ALU.mult, ALU.add))
                link(TT(ovs[:, :], ovi[:, :], nov[:, :], ALU.subtract))
                for m, src in enumerate((rank[:, :, :], over_tiles(C("expert"), E), over_tiles(ovs[:, :], E))):
                    for j in range(2):
                        link(TT(t32[:, :, :], oh[:, j, :, :], src, ALU.mult))
                        link(dve.tensor_reduce(sel[:, m, j, :], t32[:, :, :], AX, ALU.add))
                r_, e_, s_ = (sel[:, m, :, :] for m in range(3))
                K_, M_, B_, X_, R_ = (v[:, :, :] for v in (kx, mx_, bx, px, rx))
                link(TS(M_, r_, float(P), None, ALU.is_ge))
                link(dve.scalar_tensor_tensor(K_, r_, 2.0 * P, M_, ALU.is_ge, ALU.add))
                link(dve.scalar_tensor_tensor(K_, r_, 3.0 * P, K_, ALU.is_ge, ALU.add))
                link(dve.scalar_tensor_tensor(X_, K_, -float(P), r_, ALU.mult, ALU.add))
                link(TT(B_, s_, K_, ALU.add))
                link(dve.scalar_tensor_tensor(B_, B_, E - 1.0, e_, ALU.add, ALU.subtract))
                link(TT(B_, B_, M_, ALU.mult))
                link(TT(B_, B_, e_, ALU.add))
                dve.wait_ge(r_ld, 16)
                for j in range(2):
                    for i in range(NT):
                        TS(at_place[:, j, i, :], iota[:, :], px[:, j, i:i + 1], None, ALU.is_equal)
                        ins = TS(at_block[:, j, i, :], iota[:, 0:NBLK], bx[:, j, i:i + 1], C("token")[:, i:i + 1],
                                 ALU.is_equal, ALU.mult)
                ins.then_inc(r_at, 1)
                link(dve.scalar_tensor_tensor(R_, B_, float(P), X_, ALU.mult, ALU.add))
                link(dve.tensor_copy(row_y[:, :, :].rearrange("p i j -> p j i"), R_))
                dve.wait_ge(r_tab, 1)
                dve.tensor_copy(slots[:, :], ps[:, 2, 0:NBLK]).then_inc(r_sl, 1)
                for v in range(OVER):
                    link(TS(in0[:, v, :], ovs[0:1, :], float(v), None, ALU.is_le))
                    link(TS(in1[:, v, :], ovi[0:1, :], float(v), None, ALU.is_gt))
                link(TT(in0[:, :, :], in0[:, :, :], in1[:, :, :], ALU.mult))
                link(TT(in0[:, :, :], in0[:, :, :], C("expert")[0:1, :].unsqueeze(1).to_broadcast([1, OVER, E]), ALU.mult))
                link(dve.tensor_reduce(ov8[:, 0:OVER], in0[:, :, :], AX, ALU.add))
                link(dve.tensor_copy(ov8[:, OVER:8], ovi[0:1, E - 1:E]))
                dve.tensor_copy(over[:, :], ov8[:, :]).then_inc(r_ov, 1)
        stage4.close()

        moe = top.enter_context(ExitStack())
        xg = alloc(moe, "xg", [P, 2, D])
        xgT = alloc(moe, "xgT", [P, 2, KD, P])
        act_g = alloc(moe, "act_g", [P, EH])
        hd = alloc(moe, "hd", [P, EH])
        hdT = alloc(moe, "hdT", [P, 4, P])
        yo = alloc(moe, "yo", [P, 2, D])
        idx = alloc(moe, "idx", [P, 2], I32)
        x_in = [sem(f"x_in{q_}") for q_ in range(2)]
        y_st = [sem(f"y_st{q_}") for q_ in range(2)]
        e_idx, e_xT, e_xe, e_g, e_sl, e_u, e_hd, e_hT, e_he, e_d, e_ya, e_yd, e_seen = (
            sem(f"e_{n}") for n in "idx xT xe g sl u hd hT he d ya yd seen".split())
        LOOPS = (E - 2) // 2

        def wait(eng, s_, v):
            if not isinstance(v, int) or v > 0:
                eng.wait_ge(s_, v)

        def turn(it, b):
            return b if it is None else 2 * it + b

        def pairs(eng, pair):
            pair(None, 0)
            with eng.Fori(1, LOOPS) as it:
                pair(it, it)

        with nc.Block() as block:
            @block.sync
            def _(sp):
                load_expert(sp, "u", 2)
                load_expert(sp, "d", 1)
                with sp.Fori(0, LOOPS - 1) as it:
                    for b in (3, 4):
                        for kind in "gud":
                            load_expert(sp, kind, b - (kind == "d"), it)
                for kind, b in (("g", E - 1), ("u", E - 1), ("d", E - 2), ("d", E - 1)):
                    load_expert(sp, kind, b)

            @block.gpsimd
            def _(pool):
                def gather(b, it=None):
                    q_, n = b % 2, turn(it, b)
                    wait(pool, e_xT, n - 1)
                    pool.tensor_copy(idx[:, q_:q_ + 1], slots[:, bass.ds(n, 1)]).then_inc(e_idx, 1)
                    pool.wait_ge(e_idx, n + 1)
                    pool.sem_inc(e_seen, 1)
                    pool.indirect_dma_start(xg[:, q_, :], None, u2_dram,
                                            bass.IndirectOffsetOnAxis(ap=idx[:, q_:q_ + 1], axis=0))\
                        .then_inc(x_in[q_], 16)

                def store(b, it=None):
                    n = turn(it, b)
                    pool.wait_ge(e_ya, n + 1)
                    pool.wait_ge(e_yd, n + 1)
                    pool.dma_start(y_dram.rearrange("(b p) d -> b p d", p=P)[n], yo[:, b % 2, :]).then_inc(y_st[b % 2], 16)

                gather(0)
                gather(1)

                def pair(it, half):
                    for b in range(2):
                        gather(b + 2, it)
                        store(b, it)

                pairs(pool, pair)
                for b in (E - 2, E - 1):
                    store(b)
                for q_ in range(2):
                    pool.wait_ge(y_st[q_], 16 * (E // 2))

            @block.scalar
            def _(act):
                def silu(b, it=None):
                    n = turn(it, b)
                    act.wait_ge(e_g, n + 1)
                    wait(act, e_hd, n)
                    act.sem_inc(unit_free[place_of("g", b)[0]], 1)
                    act.activation(act_g[:, :], ps[:, 0, :], ACT.Silu).then_inc(e_sl, 1)

                def finish(b, half, it=None):
                    n = turn(it, b)
                    act.wait_ge(e_hT, n + 1)
                    wait(act, e_d, n)
                    act.activation(hdT[:, :, :], ps[:, 6, :].rearrange("p (j t) -> p j t", j=4), ACT.Copy).then_inc(e_he, 1)
                    act.wait_ge(e_d, n + 1)
                    wait(act, y_st[b % 2], 16 * half)
                    act.activation(yo[:, b % 2, 0:512], ps[:, 2, :], ACT.Copy).then_inc(e_ya, 1)

                silu(0)

                def pair(it, half):
                    silu(1, it)
                    finish(0, half, it)
                    silu(2, it)
                    finish(1, half, it)

                pairs(act, pair)
                silu(E - 1)
                finish(E - 2, LOOPS)
                finish(E - 1, LOOPS)

            @block.vector
            def _(dve):
                def tokens(b, it=None):
                    dve.wait_ge(e_xT, turn(it, b) + 1)
                    dve.tensor_copy(xgT[:, b % 2, :, :], ps[:, 4:6, :].rearrange("p b (k t) -> p (b k) t", k=4))\
                        .then_inc(e_xe, 1)

                def gated(b, it=None):
                    n = turn(it, b)
                    dve.wait_ge(e_u, n + 1)
                    dve.sem_inc(unit_free[place_of("u", b)[0]], 1)
                    dve.wait_ge(e_sl, n + 1)
                    wait(dve, e_hT, n)
                    dve.tensor_tensor(hd[:, :], act_g[:, :], ps[:, 1, :], ALU.mult).then_inc(e_hd, 1)

                def finish(b, half, it=None):
                    n = turn(it, b)
                    dve.wait_ge(e_d, n + 1)
                    dve.sem_inc(unit_free[place_of("d", b)[0]], 1)
                    wait(dve, y_st[b % 2], 16 * half)
                    dve.tensor_copy(yo[:, b % 2, 512:D], ps[:, 3, :]).then_inc(e_yd, 1)

                tokens(0)
                gated(0)
                tokens(1)

                def pair(it, half):
                    gated(1, it)
                    tokens(2, it)
                    finish(0, half, it)
                    gated(2, it)
                    tokens(3, it)
                    finish(1, half, it)

                pairs(dve, pair)
                gated(E - 1)
                finish(E - 2, LOOPS)
                finish(E - 1, LOOPS)

            @block.tensor
            def _(pe):
                ident = C("ident")

                def tokens(b, half, it=None):
                    n = turn(it, b)
                    pe.wait_ge(x_in[b % 2], 16 * half + 16)
                    wait(pe, e_xe, n)
                    src = xg[:, b % 2, :].rearrange("t (p k) -> t k p", k=KD)
                    for k in range(KD):
                        ins = pe.transpose(ps[:, 4 + k // 4, P * (k % 4):P * (k % 4) + P], src[:, k, :], ident)
                    ins.then_inc(e_xT, 1)

                def product(kind, b, it=None):
                    n = turn(it, b)
                    w = need_expert(pe, kind, b, it)
                    if kind == "g":
                        pe.wait_ge(e_xe, n + 1)
                        wait(pe, e_sl, n)
                    else:
                        wait(pe, e_hd, n)
                    for k in range(KD):
                        ins = pe.matmul(ps[:, "gu".index(kind), :], xgT[:, b % 2, k, :], w[:, k, :], start=(k == 0),
                                        stop=(k == KD - 1))
                    ins.then_inc(e_g if kind == "g" else e_u, 1)

                def hidden(b, it=None):
                    n = turn(it, b)
                    pe.wait_ge(e_hd, n + 1)
                    wait(pe, e_he, n)
                    src = hd[:, :].rearrange("t (p j) -> t j p", j=4)
                    for j in range(4):
                        ins = pe.transpose(ps[:, 6, P * j:P * j + P], src[:, j, :], ident)
                    ins.then_inc(e_hT, 1)

                def down(b, it=None):
                    n = turn(it, b)
                    w = need_expert(pe, "d", b, it)
                    pe.wait_ge(e_he, n + 1)
                    wait(pe, e_ya, n)
                    wait(pe, e_yd, n)
                    for c in range(2):
                        for j in range(4):
                            ins = pe.matmul(ps[:, 2 + c, :], hdT[:, j, :], w[:, j, 512 * c:512 * c + 512],
                                            start=(j == 0), stop=(j == 3))
                    ins.then_inc(e_d, 1)

                tokens(0, 0)
                product("g", 0)
                product("u", 0)
                tokens(1, 0)

                def pair(it, half):
                    for b in (1, 2):
                        product("g", b, it)
                        hidden(b - 1, it)
                        product("u", b, it)
                        tokens(b + 1, half + 1, it)
                        down(b - 1, it)

                pairs(pe, pair)
                product("g", E - 1)
                hidden(E - 2)
                product("u", E - 1)
                down(E - 2)
                hidden(E - 1)
                down(E - 1)

        v_ld, v_idx, v_x, v_xT, v_xe, v_g, v_sl, v_hd, v_hT, v_he, v_d, v_y, v_st, v_seen = (
            sem(f"v_{n}") for n in "ld idx x xT xe g sl hd hT he d y st seen".split())

        def further(eng, body):
            n_over = eng.value_load(over[0:1, OVER:8], min_val=0, max_val=OVER)
            with eng.Fori(0, OVER) as v:
                with eng.If(n_over > v):
                    body(v)

        with nc.Block() as block:
            @block.sync
            def _(sp):
                def body(v):
                    e_ = sp.value_load(over[0:1, bass.ds(v, 1)], min_val=0, max_val=E - 1)
                    for m in range(2):
                        sp.dma_start(expert_slot(m, KD, 0), gu[m][e_]).then_inc(v_ld, 16)
                    sp.dma_start(expert_slot(2, 4, 0), dn[e_]).then_inc(v_ld, 16)
                    sp.wait_ge(v_y, 2 * v + 2)
                    sp.dma_start(y_dram.rearrange("(b p) d -> b p d", p=P)[v + E], yo[:, 0, :]).then_inc(v_st, 16)
                    sp.wait_ge(v_st, 16 * v + 16)
                    sp.sem_inc(v_seen, 1)
                further(sp, body)

            @block.gpsimd
            def _(pool):
                def body(v):
                    pool.tensor_copy(idx[:, 0:1], slots[:, bass.ds(v + E, 1)]).then_inc(v_idx, 1)
                    pool.wait_ge(v_idx, v + 1)
                    pool.sem_inc(v_seen, 1)
                    pool.indirect_dma_start(xg[:, 0, :], None, u2_dram,
                                            bass.IndirectOffsetOnAxis(ap=idx[:, 0:1], axis=0)).then_inc(v_x, 16)
                    pool.wait_ge(v_xT, v + 1)
                    pool.sem_inc(v_seen, 1)
                further(pool, body)

            @block.scalar
            def _(act):
                def body(v):
                    act.wait_ge(v_g, v + 1)
                    act.activation(act_g[:, :], ps[:, 0, :], ACT.Silu).then_inc(v_sl, 1)
                    act.wait_ge(v_d, v + 1)
                    act.activation(yo[:, 0, 0:512], ps[:, 2, :], ACT.Copy).then_inc(v_y, 1)
                further(act, body)

            @block.vector
            def _(dve):
                def body(v):
                    dve.wait_ge(v_xT, v + 1)
                    dve.tensor_copy(xgT[:, 0, :, :], ps[:, 4:6, :].rearrange("p b (k t) -> p (b k) t", k=4)).then_inc(v_xe, 1)
                    dve.wait_ge(v_sl, v + 1)
                    dve.tensor_tensor(hd[:, :], act_g[:, :], ps[:, 1, :], ALU.mult).then_inc(v_hd, 1)
                    dve.wait_ge(v_hT, v + 1)
                    dve.tensor_copy(hdT[:, :, :], ps[:, 6, :].rearrange("p (j t) -> p j t", j=4)).then_inc(v_he, 1)
                    dve.wait_ge(v_d, v + 1)
                    dve.tensor_copy(yo[:, 0, 512:D], ps[:, 3, :]).then_inc(v_y, 1)
                further(dve, body)

            @block.tensor
            def _(pe):
                ident = C("ident")

                def body(v):
                    pe.wait_ge(v_x, 16 * v + 16)
                    src = xg[:, 0, :].rearrange("t (p k) -> t k p", k=KD)
                    for k in range(KD):
                        ins = pe.transpose(ps[:, 4 + k // 4, P * (k % 4):P * (k % 4) + P], src[:, k, :], ident)
                    ins.then_inc(v_xT, 1)
                    pe.wait_ge(v_xe, v + 1)
                    pe.wait_ge(v_ld, 48 * v + 48)
                    for m in range(2):
                        for k in range(KD):
                            ins = pe.matmul(ps[:, m, :], xgT[:, 0, k, :], expert_slot(m, KD, 0)[:, k, :], start=(k == 0),
                                            stop=(k == KD - 1))
                    ins.then_inc(v_g, 1)
                    pe.wait_ge(v_hd, v + 1)
                    src = hd[:, :].rearrange("t (p j) -> t j p", j=4)
                    for j in range(4):
                        ins = pe.transpose(ps[:, 6, P * j:P * j + P], src[:, j, :], ident)
                    ins.then_inc(v_hT, 1)
                    pe.wait_ge(v_he, v + 1)
                    for c in range(2):
                        for j in range(4):
                            ins = pe.matmul(ps[:, 2 + c, :], hdT[:, j, :], expert_slot(2, 4, 0)[:, j, 512 * c:512 * c + 512],
                                            start=(j == 0), stop=(j == 3))
                    ins.then_inc(v_d, 1)
                further(pe, body)
        moe.close()

        last = top.enter_context(ExitStack())
        ya = alloc(last, "ya", [P, NT, 2, D])
        gf = alloc(last, "gf", [P, D])
        fss, fms, frt = (alloc(last, f"f{n}", [P, NT]) for n in ("ss", "ms", "rt"))
        fidx = alloc(last, "fidx", [P, 2 * NT], I32)
        f_in = [sem(f"f_in{n}") for n in range(2 * NT)]
        f_ld, f_idx, f_h, f_sq, f_ms, f_rt, f_o, f_out, f_dve = (sem(f"f_{n}") for n in "ld idx h sq ms rt o out dve".split())
        out_t = out[0].rearrange("(i p) d -> i p d", p=P)

        with nc.Block() as block:
            @block.gpsimd
            def _(pool):
                pool.tensor_copy(fidx[:, :], row_y[:, :, :].rearrange("p i j -> p (i j)")).then_inc(f_idx, 1)
                pool.wait_ge(f_idx, 1)
                for i in range(NT):
                    for j in range(2):
                        n = 2 * i + j
                        pool.indirect_dma_start(ya[:, i, j, :], None, y_dram,
                                                bass.IndirectOffsetOnAxis(ap=fidx[:, n:n + 1], axis=0))\
                            .then_inc(f_in[n], 16)
                for n in range(2 * NT):
                    pool.wait_ge(f_in[n], 16)

            @block.sync
            def _(sp):
                sp.dma_start(gf[:, :], A["norm_final_g"].partition_broadcast(P)).then_inc(f_ld, 16)
                for i in range(NT):
                    sp.wait_ge(f_o, i + 1)
                    sp.dma_start(out_t[i], ya[:, i, 0, :]).then_inc(f_out, 16)
                sp.wait_ge(f_ld, 16)
                sp.wait_ge(f_out, 16 * NT)

            @block.scalar
            def _(act):
                junk = ps[:, 0:2, :].rearrange("p b n -> p (b n)")
                for i in range(NT):
                    act.wait_ge(f_h, i + 1)
                    if i:
                        act.wait_ge(f_sq, i)
                    act.activation(junk, h[:, i, :], ACT.Square, accum_out=fss[:, i:i + 1]).then_inc(f_sq, 1)
                    act.wait_ge(f_ms, i + 1)
                    act.activation(frt[:, i:i + 1], fms[:, i:i + 1], ACT.Sqrt).then_inc(f_rt, 1)

            @block.vector
            def _(dve):
                link = Chain(dve, f_dve)
                dve.wait_ge(f_ld, 16)

                def normed(i):
                    dve.wait_ge(f_rt, i + 1)
                    link(dve.reciprocal(frt[:, i:i + 1], frt[:, i:i + 1]))
                    dve.scalar_tensor_tensor(ya[:, i, 0, :], h[:, i, :], frt[:, i:i + 1], gf[:, :], ALU.mult, ALU.mult)\
                        .then_inc(f_o, 1)

                for i in range(NT):
                    a_, b_ = ya[:, i, 0, :], ya[:, i, 1, :]
                    dve.wait_ge(f_in[2 * i], 16)
                    link(dve.tensor_scalar(a_, a_, wts[:, i, 0:1], None, ALU.mult))
                    dve.wait_ge(f_in[2 * i + 1], 16)
                    link(dve.scalar_tensor_tensor(a_, b_, wts[:, i, 1:2], a_, ALU.mult, ALU.add))
                    link(dve.tensor_tensor(a_, a_, mod[:, 5, :], ALU.mult))
                    dve.tensor_tensor(h[:, i, :], h[:, i, :], a_, ALU.add).then_inc(f_h, 1)
                    dve.wait_ge(f_sq, i + 1)
                    dve.tensor_scalar(fms[:, i:i + 1], fss[:, i:i + 1], 1.0 / D, 1e-6, ALU.mult, ALU.add).then_inc(f_ms, 1)
                    normed(i)


_INS = ['x', 'c', 'w_ada', 'b_ada', 'norm_mix_g', 'w_in', 'rwkv_mu', 'rwkv_w0', 'rwkv_w2', 'rwkv_a0', 'rwkv_a2',
        'rwkv_g2', 'rwkv_kk', 'rwkv_ka', 'rwkv_rk', 'rwkv_ln_w', 'rwkv_ln_b', 'cmp_pe_k', 'cmp_w1_k', 'cmp_w2_k',
        'cmp_pe_v', 'cmp_w1_v', 'cmp_w2_v', 'p_rwkv', 'p_nsa', 'w_out', 'norm_ffn_g', 'w_router_grp',
        'b_router_grp', 'w_router_exp', 'b_router_exp', 'moe_w_gate', 'moe_w_up', 'moe_w_down', 'norm_final_g']


def kernel(**inputs):
    import numpy as _np
    import concourse.bacc as _bacc
    from concourse import mybir as _mybir
    from concourse.bass_utils import run_bass_kernel_spmd as _run

    nc = _bacc.Bacc("TRN2", target_bir_lowering=False, num_devices=1)
    arrays, aps = {}, {}
    for name in _INS:
        a = _np.ascontiguousarray(inputs[name])
        arrays[f"in_{name}_dram"] = a
        aps[name] = nc.dram_tensor(f"in_{name}_dram", a.shape, _mybir.dt.from_np(a.dtype), kind="ExternalInput").ap()
    table = constants()[0]
    arrays["consts_dram"] = table
    aps["consts"] = nc.dram_tensor("consts_dram", table.shape, _mybir.dt.float32, kind="ExternalInput").ap()
    out = nc.dram_tensor("out_0_dram", (1, T, D), _mybir.dt.float32, kind="ExternalOutput").ap()
    build(nc, aps, out)
    r = _run(nc, [arrays], core_ids=[0])
    return r.results[0]["out_0_dram"]
```
